# Optimizing a Trainium2 kernel written in Bass

```python
import jax, jax.numpy as jnp
from jax import lax
import numpy as np
import math

D_MODEL = 1024
BATCH = 1
SEQ = 256
DEPTH = 1

PLE_DIM = 256
GLA_HEADS = 4
GLA_DK = D_MODEL // 8
GLA_DV = D_MODEL // 4
GLA_GATE_RANK = 16
GLA_GATE_TAU = 16.0
GLA_CHUNK = 64
MOBA_HEADS = 8
MOBA_DH = D_MODEL // 8
MOBA_BLOCK = 256
MOBA_TOPK = 3
MOBA_QCHUNK = 32
D_FF = 4 * D_MODEL
EPS = 1e-6

IN_SPLITS = (
    GLA_HEADS * GLA_DK,
    GLA_HEADS * GLA_DK,
    GLA_HEADS * GLA_DV,
    GLA_GATE_RANK,
    GLA_HEADS * GLA_DV,
    MOBA_HEADS * MOBA_DH,
    MOBA_HEADS * MOBA_DH,
    MOBA_HEADS * MOBA_DH,
    D_MODEL,
    D_MODEL,
)
N_IN = sum(IN_SPLITS)


def rms_norm(x, g):
    xf = x.astype(jnp.float32)
    y = xf * lax.rsqrt(jnp.mean(xf * xf, axis=-1, keepdims=True) + EPS)
    return (y * g.astype(jnp.float32)).astype(x.dtype)

def gla_chunked(q, k, v, log_a):
    B, S, H, dk = q.shape
    dv = v.shape[-1]
    n = S // GLA_CHUNK

    def chunk(t):
        return t.astype(jnp.float32).reshape(B, n, GLA_CHUNK, H, t.shape[-1]).transpose(0, 3, 1, 2, 4)

    q, k, v, log_a = chunk(q), chunk(k), chunk(v), chunk(log_a)
    b = jnp.cumsum(log_a, axis=3)
    b_last = b[:, :, :, -1:, :]
    qd = q * jnp.exp(b) * (dk ** -0.5)
    kd = k * jnp.exp(-b)
    kl = k * jnp.exp(b_last - b)
    kv = jnp.einsum('bhncd,bhnce->bhnde', kl, v)
    decay = jnp.exp(b_last[:, :, :, 0, :])

    def step(state, inp):
        dec, kv_n = inp
        return dec[..., None] * state + kv_n, state

    s0 = jnp.zeros((B, H, dk, dv), jnp.float32)
    _, s_prev = lax.scan(step, s0, (jnp.moveaxis(decay, 2, 0), jnp.moveaxis(kv, 2, 0)))
    s_prev = jnp.moveaxis(s_prev, 0, 2)
    o_inter = jnp.einsum('bhncd,bhnde->bhnce', qd, s_prev)
    causal = jnp.tril(jnp.ones((GLA_CHUNK, GLA_CHUNK), bool))
    a = jnp.where(causal, jnp.einsum('bhncd,bhnsd->bhncs', qd, kd), 0.0)
    o = o_inter + jnp.einsum('bhncs,bhnse->bhnce', a, v)
    return o.transpose(0, 2, 3, 1, 4).reshape(B, S, H, dv)

def moba_attention(q, k, v):
    B, S, H, dh = q.shape
    s_pad = -(-S // MOBA_BLOCK) * MOBA_BLOCK
    nb = s_pad // MOBA_BLOCK
    n_sel = min(MOBA_TOPK, max(nb - 1, 1))
    nq = s_pad // MOBA_QCHUNK
    pad = ((0, 0), (0, s_pad - S), (0, 0), (0, 0))
    q, k, v = [jnp.pad(t, pad).transpose(0, 2, 1, 3) for t in (q, k, v)]
    kb = k.reshape(B, H, nb, MOBA_BLOCK, dh)
    vb = v.reshape(B, H, nb, MOBA_BLOCK, dh)
    scale = dh ** -0.5
    slopes = 2.0 ** (-8.0 * jnp.arange(1, H + 1, dtype=jnp.float32) / H)

    k_mean = jnp.mean(kb.astype(jnp.float32), axis=3)
    gate = jnp.einsum('bhsd,bhnd->bhsn', q.astype(jnp.float32), k_mean)
    pos = jnp.arange(s_pad)
    fully_past = jnp.arange(nb)[None, :] < (pos // MOBA_BLOCK)[:, None]
    gate = jnp.where(fully_past, gate, -jnp.inf)
    top_val, top_idx = lax.top_k(gate, n_sel)
    valid = jnp.isfinite(top_val)

    def to_chunks(t):
        return jnp.moveaxis(t.reshape(B, H, nq, MOBA_QCHUNK, *t.shape[3:]), 2, 0)

    b_ix = jnp.arange(B)[:, None, None, None]
    h_ix = jnp.arange(H)[None, :, None, None]

    def attend(args):
        q_c, idx_c, valid_c, c = args
        t = c * MOBA_QCHUNK + jnp.arange(MOBA_QCHUNK)
        blk = (c * MOBA_QCHUNK) // MOBA_BLOCK
        k_own = lax.dynamic_index_in_dim(kb, blk, axis=2, keepdims=False)
        v_own = lax.dynamic_index_in_dim(vb, blk, axis=2, keepdims=False)
        own_pos = blk * MOBA_BLOCK + jnp.arange(MOBA_BLOCK)
        d_own = (t[:, None] - own_pos[None, :]).astype(jnp.float32)
        sc_own = (jnp.einsum('bhqd,bhkd->bhqk', q_c, k_own).astype(jnp.float32) * scale
                  - slopes[:, None, None] * jnp.abs(d_own))
        sc_own = jnp.where(d_own >= 0, sc_own, -jnp.inf)
        k_sel = kb[b_ix, h_ix, idx_c]
        v_sel = vb[b_ix, h_ix, idx_c]
        sel_pos = idx_c[..., None] * MOBA_BLOCK + jnp.arange(MOBA_BLOCK)
        d_sel = (t[:, None, None] - sel_pos).astype(jnp.float32)
        sc_sel = (jnp.einsum('bhqd,bhqnkd->bhqnk', q_c, k_sel).astype(jnp.float32) * scale
                  - slopes[:, None, None, None] * jnp.abs(d_sel))
        sc_sel = jnp.where(valid_c[..., None], sc_sel, -jnp.inf)
        scores = jnp.concatenate(
            [sc_own, sc_sel.reshape(B, H, MOBA_QCHUNK, n_sel * MOBA_BLOCK)], axis=-1)
        prob = jax.nn.softmax(scores, axis=-1).astype(v.dtype)
        p_own = prob[..., :MOBA_BLOCK]
        p_sel = prob[..., MOBA_BLOCK:].reshape(B, H, MOBA_QCHUNK, n_sel, MOBA_BLOCK)
        return (jnp.einsum('bhqk,bhkd->bhqd', p_own, v_own)
                + jnp.einsum('bhqnk,bhqnkd->bhqd', p_sel, v_sel))

    out = lax.map(attend, (to_chunks(q), to_chunks(top_idx), to_chunks(valid), jnp.arange(nq)))
    out = jnp.moveaxis(out, 0, 2).reshape(B, H, s_pad, dh)[:, :, :S]
    return out.transpose(0, 2, 1, 3).reshape(B, S, H * dh)

def first_inputs(seed: int = 0) -> dict:
    key = jax.random.key(seed)
    ks = jax.random.split(key, 20)

    def nrm(k, shape, fan_in, scale=1.0):
        return jax.random.normal(k, shape, jnp.float32) * (scale * fan_in ** -0.5)

    def gain(k, shape):
        return 1.0 + 0.05 * jax.random.normal(k, shape, jnp.float32)

    return {
        'x': jax.random.normal(ks[0], (BATCH, SEQ, D_MODEL), jnp.float32),
        'p': jax.random.normal(ks[1], (DEPTH, BATCH, SEQ, PLE_DIM), jnp.float32),
        'norm_mix': gain(ks[2], (DEPTH, D_MODEL)),
        'w_in': nrm(ks[3], (DEPTH, D_MODEL, N_IN), D_MODEL),
        'gla_gate_w2': nrm(ks[4], (DEPTH, GLA_GATE_RANK, GLA_HEADS * GLA_DK), GLA_GATE_RANK),
        'gla_gate_b': 0.1 * jax.random.normal(ks[5], (DEPTH, GLA_HEADS * GLA_DK), jnp.float32),
        'gla_out_norm': gain(ks[6], (DEPTH, GLA_HEADS, GLA_DV)),
        'moba_q_norm': gain(ks[7], (DEPTH, MOBA_DH)),
        'moba_k_norm': gain(ks[8], (DEPTH, MOBA_DH)),
        'w_branch_a': nrm(ks[9], (DEPTH, GLA_HEADS * GLA_DV, D_MODEL), GLA_HEADS * GLA_DV),
        'w_branch_b': nrm(ks[10], (DEPTH, MOBA_HEADS * MOBA_DH, D_MODEL), MOBA_HEADS * MOBA_DH),
        'w_out': nrm(ks[11], (DEPTH, D_MODEL, D_MODEL), D_MODEL, 0.5),
        'norm_mlp': gain(ks[12], (DEPTH, D_MODEL)),
        'w_up': nrm(ks[13], (DEPTH, D_MODEL, D_FF), D_MODEL),
        'w_down': nrm(ks[14], (DEPTH, D_FF, D_MODEL), D_FF, 0.5),
        'norm_ple': gain(ks[15], (DEPTH, D_MODEL)),
        'w_ple_gate': nrm(ks[16], (DEPTH, D_MODEL, D_MODEL), D_MODEL),
        'w_ple': nrm(ks[17], (DEPTH, PLE_DIM, D_MODEL), PLE_DIM, 0.5),
    }

def first_block(x, p, norm_mix, w_in, gla_gate_w2, gla_gate_b, gla_out_norm, moba_q_norm,
              moba_k_norm, w_branch_a, w_branch_b, w_out, norm_mlp, w_up, w_down,
              norm_ple, w_ple_gate, w_ple):
    B, S, _ = x.shape
    points = []
    acc = 0
    for sz in IN_SPLITS[:-1]:
        acc += sz
        points.append(acc)

    for i in range(DEPTH):
        h = rms_norm(x, norm_mix[i])
        u = h @ w_in[i]
        (gq, gk, gv, g_lr, g_r, mq, mk, mv, gate_a, gate_b) = jnp.split(u, points, axis=-1)

        z = (g_lr @ gla_gate_w2[i] + gla_gate_b[i]).astype(jnp.float32)
        log_a = jax.nn.log_sigmoid(z) / GLA_GATE_TAU
        o_a = gla_chunked(gq.reshape(B, S, GLA_HEADS, GLA_DK),
                          gk.reshape(B, S, GLA_HEADS, GLA_DK),
                          gv.reshape(B, S, GLA_HEADS, GLA_DV),
                          log_a.reshape(B, S, GLA_HEADS, GLA_DK)).astype(x.dtype)
        o_a = rms_norm(o_a, gla_out_norm[i]).reshape(B, S, GLA_HEADS * GLA_DV) * jax.nn.silu(g_r)
        y_a = o_a @ w_branch_a[i]

        qh = rms_norm(mq.reshape(B, S, MOBA_HEADS, MOBA_DH), moba_q_norm[i])
        kh = rms_norm(mk.reshape(B, S, MOBA_HEADS, MOBA_DH), moba_k_norm[i])
        vh = mv.reshape(B, S, MOBA_HEADS, MOBA_DH)
        y_b = moba_attention(qh, kh, vh) @ w_branch_b[i]

        y = jax.nn.sigmoid(gate_a) * y_a + jax.nn.sigmoid(gate_b) * y_b
        x = x + y @ w_out[i]

        h2 = rms_norm(x, norm_mlp[i])
        x = x + jnp.square(jax.nn.relu(h2 @ w_up[i])) @ w_down[i]

        ple_gate = jax.nn.sigmoid(rms_norm(x, norm_ple[i]) @ w_ple_gate[i])
        x = x + ple_gate * (p[i] @ w_ple[i])
    return x


DEPTH_2 = 2

CHUNK = 64
N_MIXERS = 3
ALPHA = (2.0 * DEPTH_2) ** 0.25
BETA = (8.0 * DEPTH_2) ** -0.25
LN_EPS = 1e-5
RMS_EPS = 1e-6
SC_WIDTH = 3
MLA_HEADS = 8
QK_NOPE = 128
QK_ROPE = 64
V_HEAD = 128
Q_LORA = 3 * D_MODEL // 8
KV_LORA = D_MODEL // 4
ROPE_THETA = 10000.0
Q_BLOCK = 128
CONF_WIDTH = 31
D_FF_2 = 4 * D_MODEL
N_A = len(range(0, DEPTH_2, N_MIXERS))
N_B = len(range(1, DEPTH_2, N_MIXERS))
N_C = len(range(2, DEPTH_2, N_MIXERS))


def _layer_norm(x, g, b):
    xf = x.astype(jnp.float32)
    mu = jnp.mean(xf, axis=-1, keepdims=True)
    var = jnp.mean(jnp.square(xf - mu), axis=-1, keepdims=True)
    y = (xf - mu) * lax.rsqrt(var + LN_EPS) * g.astype(jnp.float32) + b.astype(jnp.float32)
    return y.astype(x.dtype)

def _rms_norm(x, g):
    xf = x.astype(jnp.float32)
    y = xf * lax.rsqrt(jnp.mean(jnp.square(xf), axis=-1, keepdims=True) + RMS_EPS) * g.astype(jnp.float32)
    return y.astype(x.dtype)

def _causal_dwconv(x, w):
    k_width, c = w.shape
    return lax.conv_general_dilated(
        x, w[:, None, :].astype(x.dtype), window_strides=(1,), padding=[(k_width - 1, 0)],
        dimension_numbers=("NWC", "WIO", "NWC"), feature_group_count=c)

def _rope(x, cos, sin):
    x1, x2 = jnp.split(x, 2, axis=-1)
    c = cos[None, :, None, :].astype(x.dtype)
    s = sin[None, :, None, :].astype(x.dtype)
    return jnp.concatenate([x1 * c - x2 * s, x1 * s + x2 * c], axis=-1)

def _short_conv_mixer(x, w_in, conv_w, w_out):
    b_gate, c_gate, h = jnp.split(x @ w_in, 3, axis=-1)
    return (b_gate * _causal_dwconv(c_gate * h, conv_w)) @ w_out

def _mla_mixer(x, w_dq, g_q, w_uq, w_dkv, g_kv, w_uk, w_uv, w_o):
    bsz, seq, _ = x.shape
    pos = jnp.arange(seq, dtype=jnp.float32)
    inv_freq = ROPE_THETA ** (-jnp.arange(0, QK_ROPE, 2, dtype=jnp.float32) / QK_ROPE)
    ang = pos[:, None] * inv_freq[None, :]
    cos, sin = jnp.cos(ang), jnp.sin(ang)
    cq = _rms_norm(x @ w_dq, g_q)
    q = (cq @ w_uq).reshape(bsz, seq, MLA_HEADS, QK_NOPE + QK_ROPE)
    q_nope, q_pe = q[..., :QK_NOPE], _rope(q[..., QK_NOPE:], cos, sin)
    ckv_full = x @ w_dkv
    ckv = _rms_norm(ckv_full[..., :KV_LORA], g_kv)
    k_pe = _rope(ckv_full[..., None, KV_LORA:], cos, sin)[:, :, 0, :]
    k_nope = jnp.einsum("bsc,chd->bshd", ckv, w_uk)
    v = jnp.einsum("bsc,chd->bshd", ckv, w_uv)
    scale = (QK_NOPE + QK_ROPE) ** -0.5
    n_blk = seq // Q_BLOCK
    qn_b = q_nope.reshape(bsz, n_blk, Q_BLOCK, MLA_HEADS, QK_NOPE).transpose(1, 0, 2, 3, 4)
    qp_b = q_pe.reshape(bsz, n_blk, Q_BLOCK, MLA_HEADS, QK_ROPE).transpose(1, 0, 2, 3, 4)
    k_chunk = jnp.arange(seq) // CHUNK

    def block(args):
        qn, qp, blk = args
        s = (jnp.einsum("bqhd,bkhd->bhqk", qn, k_nope)
             + jnp.einsum("bqhd,bkd->bhqk", qp, k_pe)).astype(jnp.float32) * scale
        q_chunk = (blk * Q_BLOCK + jnp.arange(Q_BLOCK)) // CHUNK
        allowed = k_chunk[None, :] <= q_chunk[:, None]
        p = jax.nn.softmax(jnp.where(allowed[None, None], s, -jnp.inf), axis=-1).astype(v.dtype)
        return jnp.einsum("bhqk,bkhd->bqhd", p, v)

    o = lax.map(block, (qn_b, qp_b, jnp.arange(n_blk)))
    o = o.transpose(1, 0, 2, 3, 4).reshape(bsz, seq, MLA_HEADS * V_HEAD)
    return o @ w_o

def _conformer_conv_mixer(x, w_pw1, b_pw1, dw_w, dw_b, norm_g, norm_b, w_pw2, b_pw2):
    a, gate = jnp.split(x @ w_pw1 + b_pw1, 2, axis=-1)
    h = a * jax.nn.sigmoid(gate)
    h = _causal_dwconv(h, dw_w) + dw_b
    h = jax.nn.silu(_layer_norm(h, norm_g, norm_b))
    return h @ w_pw2 + b_pw2

def _sq_relu_mlp(x, w1, w2):
    return jnp.square(jax.nn.relu(x @ w1)) @ w2

def _normal(k, shape, fan_in, scale=1.0):
    return jax.random.normal(k, shape, jnp.float32) * (scale * fan_in ** -0.5)

def second_inputs(seed: int = 0) -> dict:
    key = jax.random.key(seed)
    ks = iter(jax.random.split(key, 40))
    D = D_MODEL
    gain = lambda shape: 1.0 + 0.02 * jax.random.normal(next(ks), shape, jnp.float32)
    bias = lambda shape: 0.02 * jax.random.normal(next(ks), shape, jnp.float32)
    return {
        "x": jax.random.normal(next(ks), (BATCH, SEQ, D), jnp.float32),
        "sc_w_in": _normal(next(ks), (N_A, D, 3 * D), D),
        "sc_conv_w": _normal(next(ks), (N_A, SC_WIDTH, D), SC_WIDTH),
        "sc_w_out": _normal(next(ks), (N_A, D, D), D, BETA),
        "mla_w_dq": _normal(next(ks), (N_B, D, Q_LORA), D),
        "mla_g_q": gain((N_B, Q_LORA)),
        "mla_w_uq": _normal(next(ks), (N_B, Q_LORA, MLA_HEADS * (QK_NOPE + QK_ROPE)), Q_LORA),
        "mla_w_dkv": _normal(next(ks), (N_B, D, KV_LORA + QK_ROPE), D),
        "mla_g_kv": gain((N_B, KV_LORA)),
        "mla_w_uk": _normal(next(ks), (N_B, KV_LORA, MLA_HEADS, QK_NOPE), KV_LORA),
        "mla_w_uv": _normal(next(ks), (N_B, KV_LORA, MLA_HEADS, V_HEAD), KV_LORA, BETA),
        "mla_w_o": _normal(next(ks), (N_B, MLA_HEADS * V_HEAD, D), MLA_HEADS * V_HEAD, BETA),
        "cf_w_pw1": _normal(next(ks), (N_C, D, 2 * D), D),
        "cf_b_pw1": bias((N_C, 2 * D)),
        "cf_dw_w": _normal(next(ks), (N_C, CONF_WIDTH, D), CONF_WIDTH),
        "cf_dw_b": bias((N_C, D)),
        "cf_norm_g": gain((N_C, D)),
        "cf_norm_b": bias((N_C, D)),
        "cf_w_pw2": _normal(next(ks), (N_C, D, D), D, BETA),
        "cf_b_pw2": bias((N_C, D)),
        "ff_w1": _normal(next(ks), (DEPTH_2, D, D_FF_2), D, BETA),
        "ff_w2": _normal(next(ks), (DEPTH_2, D_FF_2, D), D_FF_2, BETA),
        "ln_mix_g": gain((DEPTH_2, D)),
        "ln_mix_b": bias((DEPTH_2, D)),
        "ln_ff_g": gain((DEPTH_2, D)),
        "ln_ff_b": bias((DEPTH_2, D)),
    }

def second_block(x, sc_w_in, sc_conv_w, sc_w_out,
              mla_w_dq, mla_g_q, mla_w_uq, mla_w_dkv, mla_g_kv, mla_w_uk, mla_w_uv, mla_w_o,
              cf_w_pw1, cf_b_pw1, cf_dw_w, cf_dw_b, cf_norm_g, cf_norm_b, cf_w_pw2, cf_b_pw2,
              ff_w1, ff_w2, ln_mix_g, ln_mix_b, ln_ff_g, ln_ff_b):
    for i in range(DEPTH_2):
        m, j = i % N_MIXERS, i // N_MIXERS
        if m == 0:
            y = _short_conv_mixer(x, sc_w_in[j], sc_conv_w[j], sc_w_out[j])
        elif m == 1:
            y = _mla_mixer(x, mla_w_dq[j], mla_g_q[j], mla_w_uq[j], mla_w_dkv[j], mla_g_kv[j],
                           mla_w_uk[j], mla_w_uv[j], mla_w_o[j])
        else:
            y = _conformer_conv_mixer(x, cf_w_pw1[j], cf_b_pw1[j], cf_dw_w[j], cf_dw_b[j],
                                      cf_norm_g[j], cf_norm_b[j], cf_w_pw2[j], cf_b_pw2[j])
        x = _layer_norm(ALPHA * x + y, ln_mix_g[i], ln_mix_b[i])
        x = _layer_norm(ALPHA * x + _sq_relu_mlp(x, ff_w1[i], ff_w2[i]), ln_ff_g[i], ln_ff_b[i])
    return x


def setup_inputs(seed=0):
    out = dict(first_inputs(seed))
    for name, value in second_inputs(seed + 1).items():
        if name != "x":
            out[name + "_2"] = value
    return out


def reference(
    x, p, norm_mix, w_in, gla_gate_w2, gla_gate_b, gla_out_norm, moba_q_norm, moba_k_norm,
    w_branch_a, w_branch_b, w_out, norm_mlp, w_up, w_down, norm_ple, w_ple_gate, w_ple,
    sc_w_in_2, sc_conv_w_2, sc_w_out_2, mla_w_dq_2, mla_g_q_2, mla_w_uq_2, mla_w_dkv_2,
    mla_g_kv_2, mla_w_uk_2, mla_w_uv_2, mla_w_o_2, cf_w_pw1_2, cf_b_pw1_2, cf_dw_w_2, cf_dw_b_2,
    cf_norm_g_2, cf_norm_b_2, cf_w_pw2_2, cf_b_pw2_2, ff_w1_2, ff_w2_2, ln_mix_g_2, ln_mix_b_2,
    ln_ff_g_2, ln_ff_b_2,
):
    x = first_block(
        x, p, norm_mix, w_in, gla_gate_w2, gla_gate_b, gla_out_norm, moba_q_norm, moba_k_norm,
        w_branch_a, w_branch_b, w_out, norm_mlp, w_up, w_down, norm_ple, w_ple_gate, w_ple,
    )
    return second_block(
        x, sc_w_in_2, sc_conv_w_2, sc_w_out_2, mla_w_dq_2, mla_g_q_2, mla_w_uq_2, mla_w_dkv_2,
        mla_g_kv_2, mla_w_uk_2, mla_w_uv_2, mla_w_o_2, cf_w_pw1_2, cf_b_pw1_2, cf_dw_w_2,
        cf_dw_b_2, cf_norm_g_2, cf_norm_b_2, cf_w_pw2_2, cf_b_pw2_2, ff_w1_2, ff_w2_2,
        ln_mix_g_2, ln_mix_b_2, ln_ff_g_2, ln_ff_b_2,
    )


_drawn_inputs = setup_inputs


def setup_inputs(seed=0):
    import zlib

    import numpy as np

    out = dict(_drawn_inputs(seed))
    spreads = {}
    factors = {'gla_gate_w2': 2.744,
     'gla_gate_b': 6.634,
     'gla_out_norm': 5.575,
     'moba_q_norm': 8.0,
     'moba_k_norm': 8.0,
     'norm_ple': 8.0,
     'mla_g_q_2': 8.0,
     'mla_w_uq_2': 2.669,
     'mla_g_kv_2': 8.0,
     'mla_w_uk_2': 2.983}
    for name, (base, spread) in spreads.items():
        noise = np.random.default_rng([zlib.crc32(name.encode()), seed]).standard_normal(out[name].shape)
        drawn = base * np.exp(spread * noise) if base else spread * noise
        out[name] = __import__('jax').numpy.asarray(drawn.astype(out[name].dtype))
    for name, factor in factors.items():
        out[name] = (out[name] * factor).astype(out[name].dtype)
    return out
```

```python
import concourse.bass as bass
from concourse import mybir
from contextlib import ExitStack

SEQ, D, D_FF = 256, 1024, 4096
T = SEQ // 128
KD = D // 128
GLA_H, GLA_DK, GLA_DV, GLA_RANK, GLA_CHUNK = 4, 128, 256, 16, 64
HEADS, DH = 8, 128
PLE = 256
QL, KVL, NOPE, ROPE = 384, 256, 128, 64
CONV = 3
EPS, LN_EPS = 1e-6, 1e-5
ALPHA = 4.0 ** 0.25
MASKED = -1e30

O_GQ, O_GK, O_GV, O_LR, O_GR = 0, 512, 1024, 2048, 2064
O_MQ, O_MK, O_MV, O_GA, O_GB = 3088, 4112, 5136, 6160, 7184

UNIT, SLOTS = 2048, 4
N_MIX = 44
N_FF = 32
U_FF0 = N_MIX
U_PLE = U_FF0 + N_FF
U_CONV = U_PLE + 5
U_CONVO = U_CONV + 12
U_FF1 = U_CONVO + 4
U_MLA = U_FF1 + N_FF
U_WO = U_MLA + 10
U_FF2 = U_WO + 4
N_UNITS = U_FF2 + N_FF

C_ID, C_TRI, C_REM, C_DIST, C_CHM = 0, 128, 256, 384, 768
C_COS, C_SIN, C_GM = 1152, 1216, 1280
N_CONST = 1408
V_CONV, V_GLA, V_QN, V_KN, V_GQ, V_GKV, N_VEC = 0, 24, 32, 33, 34, 37, 39


def program(nc, a, out):
    f32, f32r, bf16, i32 = mybir.dt.float32, mybir.dt.float32r, mybir.dt.bfloat16, mybir.dt.int32
    ALU, ACT, AX = mybir.AluOpType, mybir.ActivationFunctionType, mybir.AxisListType
    ctx = ExitStack()

    def rows4(w, k0, c0, width, nk=4):
        return w[k0:k0 + nk * 128, c0:c0 + width].rearrange("(k p) c -> p k c", p=128)

    w_in, w_a, w_b, w_o = a["w_in"][0], a["w_branch_a"][0], a["w_branch_b"][0], a["w_out"][0]
    two = lambda w, c: [rows4(w, 0, c, 512), rows4(w, 512, c, 512)]
    four = lambda w: [rows4(w, 0, 0, 512), rows4(w, 0, 512, 512), rows4(w, 512, 0, 512), rows4(w, 512, 512, 512)]
    mix_cols = [O_GQ, O_GK, O_GV, O_GV + 512, O_GR, O_GR + 512, O_MQ, O_MQ + 512, O_MK, O_MK + 512, O_MV, O_MV + 512]
    units = []
    for c in mix_cols:
        units += two(w_in, c)
    units += two(w_in, O_GA) + two(w_a, 0) + two(w_in, O_GA + 512) + two(w_a, 512)
    units += two(w_in, O_GB) + two(w_in, O_GB + 512) + four(w_b) + four(w_o)
    assert len(units) == N_MIX

    def up_unit(w, chunk, half):
        col = chunk * 512 + half * 256
        return w[:, bass.ds(col, 256)].rearrange("(k p) c -> p k c", p=128)

    def down_unit(w, chunk, half):
        return w[bass.ds(chunk * 512, 512), 512 * half:512 * half + 512].rearrange("(k p) c -> p k c", p=128)

    ffs = [(U_FF0, a["w_up"][0], a["w_down"][0]), (U_FF1, a["ff_w1_2"][0], a["ff_w2_2"][0]),
           (U_FF2, a["ff_w1_2"][1], a["ff_w2_2"][1])]
    units += [None] * N_FF
    units += [rows4(a["w_ple"][0], 0, 0, 1024, nk=2)] + four(a["w_ple_gate"][0])
    for pair in range(KD // 2):
        for part in (1, 2, 0):
            col = part * D + pair * 256
            units.append(a["sc_w_in_2"][0][:, col:col + 256].rearrange("(k p) c -> p k c", p=128))
    units += four(a["sc_w_out_2"][0]) + [None] * N_FF
    units += [rows4(a["mla_w_dq_2"][0], 512 * k, 0, QL) for k in range(2)]
    units += [rows4(a["mla_w_dkv_2"][0], 512 * k, 0, KVL + ROPE) for k in range(2)]
    units += [a[n][0].rearrange("(k p) h d -> p k (h d)", p=128) for n in ("mla_w_uk_2", "mla_w_uv_2")]
    units += [rows4(a["mla_w_uq_2"][0], 0, 384 * q, 384, nk=3) for q in range(4)]
    units += four(a["mla_w_o_2"][0]) + [None] * N_FF
    assert len(units) == N_UNITS
    UNIT_K = [None if u is None else u.shape[1] for u in units]
    UNIT_C = [None if u is None else u.shape[2] for u in units]

    with ctx:
        def sb(name, cols, dt=f32, rows=128):
            return ctx.enter_context(nc.sbuf_tensor(name, [rows] + list(cols), dt))

        def sem(name):
            return ctx.enter_context(nc.semaphore(name))

        RAW = sb("RAW", [SLOTS, UNIT])
        HI = sb("HI", [SLOTS, UNIT], f32r)
        LO = sb("LO", [SLOTS, UNIT], f32r)
        X = sb("X", [T, D])
        XT_h = sb("XT_h", [KD, SEQ], f32r)
        XT_l = sb("XT_l", [KD, SEQ], f32r)
        HT_h = sb("HT_h", [KD, SEQ], f32r)
        HT_l = sb("HT_l", [KD, SEQ], f32r)
        PT_h = sb("PT_h", [PLE // 128, SEQ], f32r)
        PT_l = sb("PT_l", [PLE // 128, SEQ], f32r)
        LR_h = sb("LR_h", [KD, GLA_RANK], f32r)
        LR_l = sb("LR_l", [KD, GLA_RANK], f32r)
        CST = sb("CST", [N_CONST])
        COLS = sb("COLS", [N_VEC + 1])
        ST = sb("ST", [160])
        R = sb("R", [11264])
        overlay = ExitStack()
        with overlay:
            G = overlay.enter_context(nc.sbuf_tensor("G", [128, 4096], f32))
        OT_h = sb("OT_h", [KD, SEQ], f32r)
        OT_l = sb("OT_l", [KD, SEQ], f32r)
        ACC = ctx.enter_context(nc.psum_tensor("ACC", [128, 4, 512], f32))
        C = ctx.enter_context(nc.psum_tensor("C", [128, 4, 512], f32))

        def cut(base, lo_, *dims):
            n = 1
            for d in dims:
                n *= d
            v = base[:, lo_:lo_ + n]
            if len(dims) == 2:
                v = v.rearrange("p (a b) -> p a b", b=dims[1])
            if len(dims) == 3:
                v = v.rearrange("p (a b c) -> p a b c", b=dims[1], c=dims[2])
            return v

        IDENT = CST[:, C_ID:C_ID + 128]
        TRI = CST[:, C_TRI:C_TRI + 128]
        REM = CST[:, C_REM:C_REM + 128]
        DIST = CST[:, C_DIST:C_DIST + 384]
        CHUNK_MASK = CST[:, C_CHM:C_CHM + 384]
        COS = cut(CST, C_COS, T, 32)
        SIN = cut(CST, C_SIN, T, 32)
        GLA_MASK = cut(CST, C_GM, T, 64).bitcast(i32)
        vec = lambda i: COLS[:, i:i + 1]
        GQ, LA, GK, GV = cut(R, 0, T, 512), cut(R, 1024, T, 512), cut(R, 2048, T, 512), cut(R, 3072, T, 2, 512)
        GR, MQ = cut(R, 5120, T, 2, 512), cut(R, 0, T, 2, 512)
        GV, GR, MQ = (v.rearrange("p t b c -> p b t c") for v in (GV, GR, MQ))
        MK = cut(R, 7168, T, 2, 512).rearrange("p t b c -> p b t c")
        MV = cut(R, 3072, T, 2, 512).rearrange("p t b c -> p b t c")
        flat = lambda o: cut(R, o, T, 1024)
        GVt, GRt, MQt, MKt, MVt = flat(3072), flat(5120), flat(0), flat(7168), flat(3072)
        QKT = cut(R, 2048, 2, 512)
        PROBS, PRTS = (cut(R, 5120, 2, 384), cut(R, 8704, 2, 384)), (cut(R, 5888, 2, 384), cut(R, 9472, 2, 384))
        SG0, Y0, Y1, SG1 = cut(R, 9216, T, 512), cut(R, 10240, T, 512), cut(R, 0, T, 512), cut(R, 1024, T, 512)
        W2E, GLRT = R[0:33, 9216:9728], R[0:33, 9728:9984]
        GLR, LR_RAW = cut(R, 9984, T, GLA_RANK), cut(R, 10016, KD, GLA_RANK)
        QD, KDT, AT = cut(G, 0, GLA_H, SEQ), cut(G, 1024, GLA_H, SEQ), cut(G, 2048, T, 128)
        S = cut(G, 2304, 3, GLA_DV)
        OTOK = cut(G, 3072, T, GLA_DV)
        SQJ = cut(G, 3584, T, GLA_DV)
        RELU, SQ, XN = cut(R, 0, 2, 512), cut(R, 1024, 2, 512), cut(R, 2048, T, D)
        GAIN, BIAS, PLEO, SG = R[:, 4096:5120], R[:, 5120:6144], cut(R, 6144, T, D), cut(R, 8192, T, D)
        ZERO = R[:, 10880:11200].bitcast(bf16)
        CS, VB = cut(R, 0, 2, 512), cut(R, 1024, 2, 256)
        Z = cut(R, 1536, 2, 258)
        P_RAW, ROWS, XN0, GAIN0 = cut(R, 7168, T, PLE), R[0:N_VEC, 7680:7808], cut(R, 2048, T, D), R[:, 4096:5120]
        QNT, KNT, VT = cut(R, 0, HEADS, SEQ), cut(R, 2048, HEADS, SEQ), cut(R, 4096, T, D)
        QPT, QPK = cut(R, 6144, 4, SEQ), cut(R, 7168, T, HEADS * ROPE)
        KPT, KPK = R[:, 8192:8448], cut(R, 8448, T, 2 * ROPE)
        CQ, CKV = cut(R, 8704, T, QL), cut(R, 9472, T, KVL)
        RT = cut(R, 9984, 2, 256)

        RSTD, SS, MVAR = ST[:, 0:2], ST[:, 2:4], cut(ST, 4, T, 2)
        BN = cut(ST, 8, T, 12)
        EPSC, LNEPSC, ONEC = ST[:, 32:33], ST[:, 33:34], ST[:, 34:35]
        NMAX, RSUM, RINV = cut(ST, 36, 2, 2), cut(ST, 40, 2, 2), cut(ST, 44, 2, 2)
        SSQ, RQ = ST[:, 48:64], ST[:, 64:80]
        DEC = cut(ST, 80, GLA_H, 4)
        GSS = ST[:, 96:98]

        raw_ready = [sem(f"raw_ready{s}") for s in range(SLOTS)]
        hi_ready, lo_ready = sem("hi_ready"), sem("lo_ready")
        unit_used = sem("unit_used")
        x_loaded, cst_loaded, rows_loaded, p_loaded = sem("x_loaded"), sem("cst_loaded"), sem("rows_loaded"), sem("p_loaded")
        lr_loaded, w2_loaded, gain_loaded = sem("lr_loaded"), sem("w2_loaded"), sem("gain_loaded")
        const_set = sem("const_set")
        act_self, dve_self = sem("act_self"), sem("dve_self")
        rstd_ready, xn_ready = sem("rstd_ready"), sem("xn_ready")
        xt_psum, xt_hi, xt_lo = sem("xt_psum"), sem("xt_hi"), sem("xt_lo")
        x_ready, mv_ready = sem("x_ready"), sem("mv_ready")
        cols_psum, cols_ready = sem("cols_psum"), sem("cols_ready")
        p_psum, p_hi, p_lo = sem("p_psum"), sem("p_hi"), sem("p_lo")
        lr_split, lr_psum, lr_sb, lrt_psum, lrt_sb = (sem("lr_split"), sem("lr_psum"), sem("lr_sb"),
                                                      sem("lrt_psum"), sem("lrt_sb"))
        z_psum, z_l, la_ready = sem("z_psum"), sem("z_l"), sem("la_ready")
        blk_sb = sem("blk_sb")
        cum_psum, cum_exp = sem("cum_psum"), sem("cum_exp")
        qt_psum, qd_ready, kt_psum, kd_ready = sem("qt_psum"), sem("qd_ready"), sem("kt_psum"), sem("kd_ready")
        g1_psum, g1_s1, g1_ready = sem("g1_psum"), sem("g1_s1"), sem("g1_ready")
        g2_psum, g2_rstd, g2_ready = sem("g2_psum"), sem("g2_rstd"), sem("g2_ready")
        g3_psum, g3_hi, g3_lo = sem("g3_psum"), sem("g3_hi"), sem("g3_lo")
        sig_e, gr_ready = sem("sig_e"), sem("gr_ready")
        m_sq, m_ssq, m_rstd, m_norm = sem("m_sq"), sem("m_ssq"), sem("m_rstd"), sem("m_norm")
        m2_psum, m2_q, m2_k = sem("m2_psum"), sem("m2_q"), sem("m2_k")
        sc_psum, sc_max, sc_exp, sc_norm = sem("sc_psum"), sem("sc_max"), sem("sc_exp"), sem("sc_norm")
        pt_psum, pt_sb, o_psum, o_hi, o_lo = sem("pt_psum"), sem("pt_sb"), sem("o_psum"), sem("o_hi"), sem("o_lo")
        y_ready = sem("y_ready")
        ff_relu, ff_sq, ff_hi, ff_lo = sem("ff_relu"), sem("ff_sq"), sem("ff_hi"), sem("ff_lo")
        ple_sb, pg_exp = sem("ple_sb"), sem("pg_exp")
        cv_c, cv_z, cv_v, cv_hi, cv_lo = sem("cv_c"), sem("cv_z"), sem("cv_v"), sem("cv_hi"), sem("cv_lo")
        l_rstd, l_norm, l_psum, l_hi, l_lo = sem("l_rstd"), sem("l_norm"), sem("l_psum"), sem("l_hi"), sem("l_lo")
        kp_psum, kp_sb = sem("kp_psum"), sem("kp_sb")
        kn_sb, v_sb, uq_nope, uq_rope, qp_psum, qp_sb = (sem("kn_sb"), sem("v_sb"), sem("uq_nope"), sem("uq_rope"),
                                                         sem("qp_psum"), sem("qp_sb"))
        stored = sem("stored")

        def block_read(b):
            if b in (4, 5):
                return gr_ready, b - 3
            if b in (13, 15):
                return y_ready, (b - 11) // 2
            if b >= 12:
                return sig_e, {12: 3, 14: 4, 16: 5, 17: 6}[b]
            return blk_sb, b + 1 if b < 4 else b - 1

        def KV_of(n):
            return C[:, n % 2, 128 * n:128 * n + 256] if n != 1 else C[:, 1, 0:256]

        def GV_head(rows, h, t):
            return GVt[rows, t, GLA_DV * h:GLA_DV * h + GLA_DV]

        block = ctx.enter_context(nc.Block())

        @block.sync
        def _(sp):
            def load(n, slot, view):
                nk, width = view.shape[1], view.shape[2]
                dst = RAW[:, slot, 0:nk * width].rearrange("p (k c) -> p k c", c=width)
                sp.dma_start(dst, view).then_inc(raw_ready[slot], 16)

            sp.dma_start(X[:], a["x"][0].rearrange("(t p) c -> p t c", p=128)).then_inc(x_loaded, 16)
            sp.dma_start(LR_RAW, w_in[:, O_LR:O_LR + GLA_RANK].rearrange("(k p) c -> p k c", p=128)).then_inc(lr_loaded, 16)
            for n in range(N_UNITS):
                if units[n] is None:
                    continue
                if n >= SLOTS:
                    sp.wait_ge(lo_ready, n - SLOTS + 1)
                load(n, n % SLOTS, units[n])
                if n + 1 in (U_FF0, U_FF1, U_FF2):
                    base, up, down = ffs[(U_FF0, U_FF1, U_FF2).index(n + 1)]
                    for half in range(2):
                        sp.wait_ge(lo_ready, base + half - SLOTS + 1)
                        load(None, (base + half) % SLOTS, up_unit(up, 0, half))
                    with sp.Fori(0, 7) as i:
                        for q in range(4):
                            sp.wait_ge(lo_ready, i * 4 + (base + 2 + q - SLOTS + 1))
                            v = up_unit(up, i + 1, q) if q < 2 else down_unit(down, i, q - 2)
                            load(None, (base + 2 + q) % SLOTS, v)
                    for half in range(2):
                        sp.wait_ge(lo_ready, base + 30 + half - SLOTS + 1)
                        load(None, (base + 30 + half) % SLOTS, down_unit(down, 7, half))
            for t in range(T):
                sp.wait_ge(x_ready, 12 + t + 1)
                sp.dma_start(out[0, 128 * t:128 * t + 128, :], X[:, t, :]).then_inc(stored, 16)
            sp.wait_ge(stored, 16 * T)

        @block.gpsimd
        def _(pool):
            def gain(dst, row):
                pool.dma_start(dst, row.partition_broadcast(128)).then_inc(gain_loaded, 16)

            pool.memset(EPSC, EPS).then_inc(const_set, 1)
            pool.memset(LNEPSC, LN_EPS).then_inc(const_set, 1)
            pool.memset(ONEC, 1.0).then_inc(const_set, 1)
            pool.dma_start(CST[:], a["consts"]).then_inc(cst_loaded, 16)
            gain(GAIN0, a["norm_mix"][0])
            for row, v in ((V_CONV, a["sc_conv_w_2"][0].rearrange("k (j p) -> (k j) p", p=128)),
                           (V_GLA, a["gla_out_norm"][0].rearrange("h (j p) -> (h j) p", p=128)),
                           (V_QN, a["moba_q_norm"]), (V_KN, a["moba_k_norm"]),
                           (V_GQ, a["mla_g_q_2"][0].rearrange("(j p) -> j p", p=128)),
                           (V_GKV, a["mla_g_kv_2"][0].rearrange("(j p) -> j p", p=128))):
                pool.dma_start(R[row:row + v.shape[0], 7680:7808], v).then_inc(rows_loaded, 16)
            pool.dma_start(P_RAW, a["p"][0, 0].rearrange("(t p) c -> p t c", p=128)).then_inc(p_loaded, 16)
            pool.memset(W2E, 0.0).then_inc(const_set, 1)
            pool.memset(GLRT, 0.0).then_inc(const_set, 1)
            pool.wait_ge(const_set, 5)
            pool.memset(GLRT[32:33, :], 1.0).then_inc(const_set, 1)
            pool.dma_start(W2E[0:GLA_RANK, :], a["gla_gate_w2"][0]).then_inc(w2_loaded, 16)
            pool.dma_start(W2E[32:33, :], a["gla_gate_b"]).then_inc(w2_loaded, 16)
            pool.wait_ge(const_set, 6)
            pool.memset(AT, 0.0).then_inc(const_set, 1)
            pool.wait_ge(o_lo, HEADS)
            gain(GAIN, a["norm_mlp"][0])
            pool.wait_ge(xt_lo, 4)
            pool.memset(ZERO, 0.0).then_inc(const_set, 1)
            pool.wait_ge(xn_ready, 4)
            gain(GAIN, a["norm_ple"][0])
            for j, (g, b) in enumerate((("ln_mix_g_2", "ln_mix_b_2"), ("ln_ff_g_2", "ln_ff_b_2")) * 2):
                if j == 0:
                    pool.wait_ge(xn_ready, 6)
                else:
                    pool.wait_ge(x_ready, 6 + 2 * j)
                if j == 2:
                    pool.wait_ge(o_psum, 2 * HEADS)
                gain(GAIN, a[g][j // 2])
                gain(BIAS, a[b][j // 2])
            pool.wait_ge(gain_loaded, 16 * 11)

        @block.scalar
        def _(act):
            own = [0]

            def chain(ins):
                own[0] += 1
                ins.then_inc(act_self, 1)
                act.wait_ge(act_self, own[0])

            def hi(n, slot, turn, width=UNIT, old=True):
                act.wait_ge(raw_ready[slot], turn)
                if old:
                    act.wait_ge(unit_used, n - SLOTS + 1)
                act.activation(HI[:, slot, 0:width], RAW[:, slot, 0:width], ACT.Copy).then_inc(hi_ready, 1)

            def hi_at(n):
                if n < N_UNITS:
                    w = UNIT if units[n] is None else UNIT_K[n] * UNIT_C[n]
                    hi(n, n % SLOTS, 16 * (n // SLOTS + 1), w, n >= SLOTS)

            def rstd(dst, src, scale, eps):
                chain(act.activation(dst, src, ACT.Ln, bias=eps, scale=scale))
                return act.activation(dst, dst, ACT.Exp, scale=-0.5)

            def xt_split(e, t):
                act.wait_ge(xt_psum, 2 * e + t + 1)
                act.activation(XT_h[:, :, 128 * t:128 * t + 128],
                               C[:, 2 * t:2 * t + 2, :].rearrange("p b (k s) -> p (b k) s", s=128), ACT.Copy).then_inc(xt_hi, 1)

            def rms(r, e, src_ready=None):
                for t in range(T):
                    if r == 0:
                        act.wait_ge(x_loaded, 16)
                        act.wait_ge(const_set, 3)
                    else:
                        act.wait_ge(x_ready, 2 * (r - 1) + t + 1)
                    junk = XN0 if r == 0 else XN
                    chain(act.activation(junk[:, t, :], X[:, t, :], ACT.Square, accum_out=SS[:, t:t + 1]))
                    rstd(RSTD[:, t:t + 1], SS[:, t:t + 1], 1.0 / D, EPSC).then_inc(rstd_ready, 1)
                for t in range(T):
                    xt_split(e, t)

            def ln(j, base):
                for t in range(T):
                    act.wait_ge(mv_ready, 2 * j + t + 1)
                    rstd(RSTD[:, t:t + 1], MVAR[:, t, 1:2], 1.0, LNEPSC).then_inc(rstd_ready, 1)

            def att_exp(j):
                p, PROB = j % 2, PROBS[j // HEADS]
                act.wait_ge(sc_max, j + 1)
                act.activation(PROB[:, p, 0:128], PROB[:, p, 0:128], ACT.Exp, bias=NMAX[:, p, 0:1],
                               accum_out=RSUM[:, p, 0:1])
                act.activation(PROB[:, p, 128:384], PROB[:, p, 128:384], ACT.Exp, bias=NMAX[:, p, 1:2],
                               accum_out=RSUM[:, p, 1:2]).then_inc(sc_exp, 1)

            def att_pt(j):
                act.wait_ge(pt_psum, j + 1)
                if j >= 2:
                    act.wait_ge(o_psum, j - 1)
                act.activation(PRTS[j // HEADS][:, j % 2, :], C[:, 2, 0:384], ACT.Copy).then_inc(pt_sb, 1)

            def att_out(j):
                act.wait_ge(o_psum, j + 1)
                act.activation(OT_h[:, j % HEADS, :], C[:, 3, 0:SEQ], ACT.Copy).then_inc(o_hi, 1)

            def feed_forward(f, base):
                def squares(c, half, slot_unit):
                    if not (isinstance(c, int) and c == 0 and f == 0):
                        act.wait_ge(ff_sq, c * 2 + (16 * f + half - 1))
                    act.wait_ge(unit_used, slot_unit + 1)
                    act.activation(RELU[:, half, :], C[:, half, :], ACT.Relu).then_inc(ff_relu, 1)
                    act.wait_ge(ff_relu, c * 2 + (16 * f + half + 1))

                def square(par, half):
                    k = 4 * par + 2 * half
                    act.activation(HT_h[:, k:k + 2, :].rearrange("p a b -> p (a b)"), RELU[:, half, :],
                                   ACT.Square).then_inc(ff_hi, 1)

                for half in range(2):
                    squares(0, half, base + half)
                    square(0, half)
                    hi_at(base + half + SLOTS)

                def step(i, i_unit, par, peel):
                    for q in range(4):
                        if q < 2:
                            squares(i + 1, q, i_unit + (base + 2 + q))
                            square(par, q)
                        if peel:
                            hi_at(base + 2 + 4 * i + q + SLOTS)
                        else:
                            n0 = base + 2 + q + SLOTS
                            hi(i_unit + n0, n0 % SLOTS, i * 16 + 16 * (n0 // SLOTS + 1))

                with act.Fori(0, 3) as j:
                    for d in range(2):
                        step(j * 2 + d, j * 8 + 4 * d, (d + 1) % 2, False)
                step(6, 24, 1, True)
                for half in range(2):
                    hi_at(base + 30 + half + SLOTS)

            for n in range(SLOTS):
                hi_at(n)
                if n == 0:
                    rms(0, 0)
            act.wait_ge(lr_loaded, 16)
            act.activation(LR_h[:], LR_RAW, ACT.Copy).then_inc(lr_split, 1)
            act.wait_ge(cols_psum, 1)
            act.activation(COLS[:, 0:N_VEC], ACC[:, 2, 0:N_VEC], ACT.Copy).then_inc(cols_ready, 1)
            act.wait_ge(p_psum, 1)
            act.activation(PT_h[:].rearrange("p a b -> p (a b)"), ACC[:, 3, :], ACT.Copy).then_inc(p_hi, 1)
            act.wait_ge(lr_psum, 1)
            act.activation(GLR, C[:, 0, 0:T * GLA_RANK].rearrange("p (t c) -> p t c", t=T), ACT.Copy).then_inc(lr_sb, 1)
            act.wait_ge(lrt_psum, 1)
            act.wait_ge(const_set, 6)
            act.activation(GLRT[0:GLA_RANK, :], C[0:GLA_RANK, 1, 0:SEQ], ACT.Copy).then_inc(lrt_sb, 1)

            blocks = [GQ, GK, GV[:, 0], GV[:, 1], None, None, MQ[:, 0], MQ[:, 1], MK[:, 0], MK[:, 1], MV[:, 0], MV[:, 1]]
            sig_of = {4: GR[:, 0], 5: GR[:, 1], 12: SG0, 14: SG0, 16: SG1, 17: SG0}

            def moba_scales(src, i):
                act.wait_ge(m_ssq, i + 1)
                chain(act.activation(RQ, SSQ, ACT.Ln, bias=EPSC, scale=1.0 / DH))
                act.activation(RQ, RQ, ACT.Exp, scale=-0.5).then_inc(m_rstd, 1)

            for u in range(N_MIX):
                b = u // 2
                if u % 2 and b < 18:
                    src = ACC[:, 2 * (b % 2):2 * (b % 2) + 2, :]
                    if b in sig_of:
                        act.wait_ge(unit_used, u + 1)
                        if b in (14, 17):
                            act.wait_ge(y_ready, 1 if b == 14 else 2)
                        act.activation(sig_of[b], src, ACT.Exp, scale=-1.0).then_inc(sig_e, 1)
                    elif b < 12:
                        act.wait_ge(unit_used, u + 1)
                        if b == 6:
                            act.wait_ge(kd_ready, 2)
                        if b == 10:
                            act.wait_ge(g2_psum, GLA_H)
                        act.activation(blocks[b], src, ACT.Copy).then_inc(blk_sb, 1)
                hi_at(u + SLOTS)
                if u == 1:
                    act.wait_ge(z_psum, 1)
                    zz = C[:, 0:2, :]
                    chain(act.activation(LA, zz, ACT.Abs))
                    chain(act.activation(LA, LA, ACT.Exp, scale=-1.0))
                    act.activation(LA, LA, ACT.Ln, bias=ONEC, scale=1.0).then_inc(z_l, 1)
                if u == 3:
                    act.wait_ge(cum_psum, 1)
                    cb = C[:, 0:2, :].rearrange("p b (h s) -> p (b h) s", s=SEQ)
                    act.activation(QD, cb, ACT.Exp)
                    act.activation(KDT, cb, ACT.Exp, scale=-1.0)
                    act.activation(LA, C[:, 2:4, :], ACT.Exp).then_inc(cum_exp, 1)
                for h in range(GLA_H):
                    if u == 9 + 2 * h:
                        act.wait_ge(g1_psum, h + 1)
                        act.activation(S[:, 0, :], C[:, 0, 0:GLA_DV], ACT.Copy).then_inc(g1_s1, 1)
                    if u == 10 + 2 * h:
                        act.wait_ge(g2_psum, h + 1)
                        for t in range(T):
                            r = act.activation(SQJ[:, t, :], C[:, 2, 256 * t:256 * t + 256], ACT.Square,
                                               accum_out=GSS[:, t:t + 1])
                        chain(r)
                        rstd(GSS, GSS, 1.0 / GLA_DV, EPSC).then_inc(g2_rstd, 1)
                    if u == 11 + 2 * h:
                        act.wait_ge(g3_psum, h + 1)
                        for j in range(2):
                            act.activation(HT_h[:, 2 * h + j, :], C[:, 3, 256 * j:256 * j + 256], ACT.Copy,
                                           scale=vec(V_GLA + 2 * h + j)).then_inc(g3_hi, 1)
                if u == 16:
                    moba_scales(MQt, 0)
                if u == 20:
                    moba_scales(MKt, 1)
                h = u - 21
                if 0 <= h < HEADS:
                    act.wait_ge(m2_psum, h + 1)
                    act.activation(QKT[:, h % 2, 0:256], C[:, 0, 0:256], ACT.Copy, scale=vec(V_QN)).then_inc(m2_q, 1)
                if 1 <= h < HEADS + 1:
                    att_exp(h - 1)
                if 2 <= h < HEADS + 2:
                    att_pt(h - 2)
                if 3 <= h < HEADS + 3:
                    att_out(h - 3)
                if u in (39, 40):
                    k = 4 * (u - 39)
                    act.wait_ge(xt_psum, 2 + u - 38)
                    act.activation(XT_h[:, k:k + 4, :], C[:, k // 2:k // 2 + 2, :].rearrange("p b (k s) -> p (b k) s", s=SEQ),
                                   ACT.Copy).then_inc(xt_hi, 1)

            rms(1, 2)
            feed_forward(0, U_FF0)
            rms(2, 3)
            for q in range(5):
                n = U_PLE + q
                act.wait_ge(unit_used, n + 1)
                if q == 0:
                    act.activation(PLEO, ACC[:].rearrange("p (t b) c -> p t (b c)", t=T), ACT.Copy).then_inc(ple_sb, 1)
                if q == 4:
                    for t in range(T):
                        act.activation(SG[:, t, :], ACC[:, 2 * t:2 * t + 2, :].rearrange("p b c -> p (b c)"), ACT.Exp,
                                       scale=-1.0).then_inc(pg_exp, 1)
                hi_at(n + SLOTS)
            for t in range(T):
                xt_split(4, t)
            for q in range(12):
                n, pair, part = U_CONV + q, q // 3, q % 3
                act.wait_ge(unit_used, n + 1)
                if part == 0:
                    if pair >= 2:
                        act.wait_ge(cv_z, pair - 1)
                    act.activation(CS[:, pair % 2, :], C[:, q % 4, :], ACT.Copy).then_inc(cv_c, 1)
                hi_at(n + SLOTS)
                if part == 2:
                    act.wait_ge(cv_v, pair + 1)
                    act.activation(OT_h[:, 2 * pair:2 * pair + 2, :].rearrange("p a b -> p (a b)"),
                                   VB.rearrange("p a b -> p (a b)"), ACT.Copy).then_inc(cv_hi, 1)
            for q in range(4):
                hi_at(U_CONVO + q + SLOTS)
            ln(0, 0)
            for t in range(T):
                xt_split(5, t)
            feed_forward(1, U_FF1)
            ln(1, 0)
            for t in range(T):
                xt_split(6, t)

            for q in range(4):
                hi_at(U_MLA + q + SLOTS)
            act.wait_ge(unit_used, U_MLA + 4)
            for i, (src, junk, width, col) in enumerate(((0, CQ, QL, 0), (2, CKV, KVL, 2))):
                for t in range(T):
                    r = act.activation(junk[:, t, :], ACC[:, src + t, 0:width], ACT.Square,
                                       accum_out=GSS[:, t:t + 1])
                chain(r)
                rstd(RQ[:, col:col + 2], GSS, 1.0 / width, EPSC).then_inc(l_rstd, 1)
                act.wait_ge(l_rstd, i + 1)
            act.wait_ge(l_psum, 1)
            for k in range(3):
                act.activation(HT_h[:, k, :], C[:, k // 2, 256 * (k % 2):256 * (k % 2) + 256], ACT.Copy,
                               scale=vec(V_GQ + k)).then_inc(l_hi, 1)
            act.wait_ge(l_psum, 2)
            for k in range(2):
                act.activation(HT_h[:, 3 + k, :], C[:, 2, 256 * k:256 * k + 256], ACT.Copy,
                               scale=vec(V_GKV + k)).then_inc(l_hi, 1)
            act.wait_ge(kp_psum, 1)
            act.activation(KPT, C[:, 3, 0:256], ACT.Copy).then_inc(kp_sb, 1)
            act.wait_ge(unit_used, U_MLA + 5)
            act.activation(KNT, ACC[:].rearrange("p b (h s) -> p (b h) s", s=SEQ), ACT.Copy).then_inc(kn_sb, 1)
            hi_at(U_MLA + 4 + SLOTS)
            act.wait_ge(unit_used, U_MLA + 6)
            act.activation(VT, C[:].rearrange("p (t b) c -> p t (b c)", t=T), ACT.Copy).then_inc(v_sb, 1)
            hi_at(U_MLA + 5 + SLOTS)
            scale = float(NOPE + ROPE) ** -0.5
            for q in range(4):
                n = U_MLA + 6 + q
                act.wait_ge(unit_used, n + 1)
                act.activation(QNT[:, 2 * q:2 * q + 2, :].rearrange("p a b -> p (a b)"), ACC[:, 2 * (q % 2), :], ACT.Copy,
                               scale=scale).then_inc(uq_nope, 1)
                hi_at(n + SLOTS)
                act.wait_ge(qp_psum, q + 1)
                act.activation(QPT[:, q, :], C[:, 0, 0:256], ACT.Copy, scale=scale).then_inc(qp_sb, 1)
            for s in range(HEADS + 2):
                if s < HEADS:
                    att_exp(HEADS + s)
                if 1 <= s < HEADS + 1:
                    att_pt(HEADS + s - 1)
                if s >= 2:
                    att_out(HEADS + s - 2)
            for q in range(4):
                hi_at(U_WO + q + SLOTS)
            ln(2, 0)
            for t in range(T):
                xt_split(7, t)
            feed_forward(2, U_FF2)
            ln(3, 0)

        @block.vector
        def _(dve):
            own = [0]

            def chain(ins):
                own[0] += 1
                ins.then_inc(dve_self, 1)
                dve.wait_ge(dve_self, own[0])

            def low(n, slot, width=UNIT):
                dve.wait_ge(hi_ready, n + 1)
                dve.tensor_tensor(LO[:, slot, 0:width], RAW[:, slot, 0:width], HI[:, slot, 0:width].bitcast(f32),
                                  ALU.subtract).then_inc(lo_ready, 1)

            def low_at(n):
                if n < N_UNITS:
                    low(n, n % SLOTS, UNIT if units[n] is None else UNIT_K[n] * UNIT_C[n])

            def xt_low(e, t):
                dve.wait_ge(xt_hi, 2 * e + t + 1)
                s = slice(128 * t, 128 * t + 128)
                dve.tensor_tensor(XT_l[:, :, s], C[:, 2 * t:2 * t + 2, :].rearrange("p b (k s) -> p (b k) s", s=128),
                                  XT_h[:, :, s].bitcast(f32), ALU.subtract).then_inc(xt_lo, 1)

            gains = [0]

            def rms_apply(r, e):
                gains[0] += 1
                dve.wait_ge(gain_loaded, 16 * gains[0])
                dst, g = (XN0, GAIN0) if r == 0 else (XN, GAIN)
                for t in range(T):
                    dve.wait_ge(rstd_ready, 2 * r + t + 1)
                    dve.scalar_tensor_tensor(dst[:, t, :], X[:, t, :], RSTD[:, t:t + 1], g, ALU.mult,
                                             ALU.mult).then_inc(xn_ready, 1)
                for t in range(T):
                    xt_low(e, t)

            def add_to_x(r, last_unit):
                dve.wait_ge(unit_used, last_unit + 1)
                for t in range(T):
                    dve.tensor_tensor(X[:, t, :], X[:, t, :], ACC[:, 2 * t:2 * t + 2, :].rearrange("p b c -> p (b c)"),
                                      ALU.add).then_inc(x_ready, 1)

            def layer_norm(j, last_unit):
                dve.wait_ge(unit_used, last_unit + 1)
                for t in range(T):
                    x = X[:, t, :]
                    chain(dve.scalar_tensor_tensor(x, x, ALPHA, ACC[:, 2 * t:2 * t + 2, :].rearrange("p b c -> p (b c)"),
                                                   ALU.mult, ALU.add))
                    dve.bn_stats(BN[:, t, 0:6], X[:, t, 0:512])
                    chain(dve.bn_stats(BN[:, t, 6:12], X[:, t, 512:1024]))
                    dve.bn_aggr(MVAR[:, t, :], BN[:, t, :]).then_inc(mv_ready, 1)
                gains[0] += 2
                dve.wait_ge(gain_loaded, 16 * gains[0])
                for t in range(T):
                    x = X[:, t, :]
                    dve.wait_ge(rstd_ready, 6 + 2 * j + t + 1)
                    dve.wait_ge(mv_ready, 2 * j + t + 1)
                    chain(dve.tensor_scalar(x, x, MVAR[:, t, 0:1], RSTD[:, t:t + 1], ALU.subtract, ALU.mult))
                    chain(dve.tensor_tensor(x, x, GAIN, ALU.mult))
                    dve.tensor_tensor(x, x, BIAS, ALU.add).then_inc(x_ready, 1)

            def att_scores(j, table, slope):
                p, PROB = j % 2, PROBS[j // HEADS]
                dve.wait_ge(sc_psum, j + 1)
                if j >= 2:
                    dve.wait_ge(pt_psum, j - 1)
                chain(dve.scalar_tensor_tensor(PROB[:, p, :], table, slope, C[:, 1, 0:384], ALU.mult, ALU.add))
                dve.tensor_reduce(NMAX[:, p, 0:1], PROB[:, p, 0:128], AX.X, ALU.max, negate=True)
                dve.tensor_reduce(NMAX[:, p, 1:2], PROB[:, p, 128:384], AX.X, ALU.max, negate=True).then_inc(sc_max, 1)

            def att_norm(j):
                p, PROB = j % 2, PROBS[j // HEADS]
                dve.wait_ge(sc_exp, j + 1)
                chain(dve.reciprocal(RINV[:, p, :], RSUM[:, p, :]))
                dve.tensor_scalar(PROB[:, p, 0:128], PROB[:, p, 0:128], RINV[:, p, 0:1], None, ALU.mult)
                dve.tensor_scalar(PROB[:, p, 128:384], PROB[:, p, 128:384], RINV[:, p, 1:2], None,
                                  ALU.mult).then_inc(sc_norm, 1)

            def att_low(j):
                dve.wait_ge(o_hi, j + 1)
                dve.tensor_tensor(OT_l[:, j % HEADS, :], C[:, 3, 0:SEQ], OT_h[:, j % HEADS, :].bitcast(f32),
                                  ALU.subtract).then_inc(o_lo, 1)

            def feed_forward(f, base):
                def square(c, par, half):
                    k = 4 * par + 2 * half
                    dve.wait_ge(ff_relu, c * 2 + (16 * f + half + 1))
                    dve.tensor_tensor(SQ[:, half, :], RELU[:, half, :], RELU[:, half, :], ALU.mult).then_inc(ff_sq, 1)
                    dve.wait_ge(ff_hi, c * 2 + (16 * f + half + 1))
                    dve.wait_ge(ff_sq, c * 2 + (16 * f + half + 1))
                    dve.tensor_tensor(HT_l[:, k:k + 2, :].rearrange("p a b -> p (a b)"), SQ[:, half, :],
                                      HT_h[:, k:k + 2, :].rearrange("p a b -> p (a b)").bitcast(f32),
                                      ALU.subtract).then_inc(ff_lo, 1)

                for half in range(2):
                    square(0, 0, half)
                    low_at(base + half + SLOTS)
                with dve.Fori(0, 3) as j:
                    for d in range(2):
                        for q in range(4):
                            if q < 2:
                                square(j * 2 + (d + 1), (d + 1) % 2, q)
                            n0 = base + 2 + q + SLOTS + 4 * d
                            low(j * 8 + n0, n0 % SLOTS)
                for q in range(4):
                    if q < 2:
                        square(7, 1, q)
                    low_at(base + 26 + q + SLOTS)
                for half in range(2):
                    low_at(base + 30 + half + SLOTS)

            for n in range(SLOTS):
                if n == 1:
                    rms_apply(0, 0)
                low_at(n)
            dve.wait_ge(lr_split, 1)
            dve.tensor_tensor(LR_l[:], LR_RAW, LR_h[:].bitcast(f32), ALU.subtract).then_inc(lr_split, 1)
            dve.wait_ge(p_hi, 1)
            dve.tensor_tensor(PT_l[:].rearrange("p a b -> p (a b)"), ACC[:, 3, :],
                              PT_h[:].rearrange("p a b -> p (a b)").bitcast(f32), ALU.subtract).then_inc(p_lo, 1)

            sigs = [4, 5, 12, 14, 16, 17]
            sig_of = {4: GR[:, 0], 5: GR[:, 1], 12: SG0, 14: SG0, 16: SG1, 17: SG0}

            def moba_sums(src, i, after):
                dve.wait_ge(blk_sb, after)
                for t in range(T):
                    sq = cut(R, 2048, 1024)
                    chain(dve.tensor_tensor(sq, src[:, t, :], src[:, t, :], ALU.mult))
                    r = dve.tensor_reduce(SSQ[:, 8 * t:8 * t + 8], sq.rearrange("p (h d) -> p h d", d=DH), AX.X, ALU.add)
                    if t:
                        r.then_inc(m_ssq, 1)
                    else:
                        chain(r)

            def moba_norm(src, i):
                dve.wait_ge(m_rstd, i + 1)
                v = src.rearrange("p t (h d) -> p (t h) d", d=DH)
                dve.tensor_tensor(v, v, RQ.unsqueeze(2).broadcast_to([128, 16, DH]), ALU.mult).then_inc(m_norm, 1)

            for u in range(N_MIX):
                b = u // 2
                if u % 2 and b in sig_of:
                    s = sig_of[b]
                    dve.wait_ge(sig_e, sigs.index(b) + 1)
                    chain(dve.tensor_scalar(s, s, 1.0, None, ALU.add))
                    if b in (4, 5):
                        chain(dve.reciprocal(s, s))
                        dve.tensor_tensor(s, s, ACC[:, 2 * (b % 2):2 * (b % 2) + 2, :], ALU.mult).then_inc(gr_ready, 1)
                    else:
                        chain(dve.reciprocal(s, s))
                if u % 2 and b in (13, 15):
                    dve.wait_ge(unit_used, u + 1)
                    dve.tensor_tensor(Y0 if b == 13 else Y1, SG0, ACC[:, 2:4, :], ALU.mult).then_inc(y_ready, 1)
                if u in (38, 39):
                    y, s, p = (Y0, SG1, 0) if u == 38 else (Y1, SG0, 1)
                    dve.wait_ge(unit_used, u + 1)
                    chain(dve.tensor_tensor(s, s, ACC[:, 2 * p:2 * p + 2, :], ALU.mult))
                    dve.tensor_tensor(y, y, s, ALU.add).then_inc(y_ready, 1)
                if u in (39, 40):
                    k = 4 * (u - 39)
                    dve.wait_ge(xt_hi, 2 + u - 38)
                    dve.tensor_tensor(XT_l[:, k:k + 4, :], C[:, k // 2:k // 2 + 2, :].rearrange("p b (k s) -> p (b k) s", s=SEQ),
                                      XT_h[:, k:k + 4, :].bitcast(f32), ALU.subtract).then_inc(xt_lo, 1)
                low_at(u + SLOTS)
                if u == 1:
                    dve.wait_ge(z_l, 1)
                    dve.scalar_tensor_tensor(LA, C[:, 0:2, :], 0.0, LA, ALU.min, ALU.subtract).then_inc(la_ready, 1)
                if u == 4:
                    dve.wait_ge(cum_exp, 1)
                    dec = QD.rearrange("p h (n c) -> p h n c", c=GLA_CHUNK)[:, :, :, GLA_CHUNK - 1]
                    chain(dve.tensor_copy(DEC, dec))
                    dve.wait_ge(qt_psum, 1)
                    dve.scalar_tensor_tensor(QD, C[:, 2:4, :].rearrange("p b (h s) -> p (b h) s", s=SEQ),
                                             float(GLA_DK) ** -0.5, QD, ALU.mult, ALU.mult).then_inc(qd_ready, 1)
                if u == 5:
                    dve.wait_ge(kt_psum, 1)
                    dve.tensor_tensor(KDT, C[:, 0:2, :].rearrange("p b (h s) -> p (b h) s", s=SEQ), KDT,
                                      ALU.mult).then_inc(kd_ready, 1)
                    dve.tensor_tensor(GK, GK, LA, ALU.mult).then_inc(kd_ready, 1)
                for h in range(GLA_H):
                    if u == 9 + 2 * h:
                        dve.wait_ge(g1_psum, h + 1)
                        dve.wait_ge(const_set, 7)
                        for j in range(2):
                            q = slice(64 * j, 64 * j + 64)
                            dve.copy_predicated(AT[q, :, q], GLA_MASK[q, :, :],
                                                C[q, 1, 256:384].rearrange("p (t c) -> p t c", t=T))
                        dve.wait_ge(g1_s1, h + 1)
                        for n in (1, 2):
                            r = dve.scalar_tensor_tensor(S[:, n, :], S[:, n - 1, :], DEC[:, h, n:n + 1],
                                                         KV_of(n), ALU.mult, ALU.add)
                            if n == 1:
                                chain(r)
                        r.then_inc(g1_ready, 1)
                    if u == 10 + 2 * h:
                        dve.wait_ge(g2_rstd, h + 1)
                        dve.wait_ge(gr_ready, 1 + h // 2)
                        if h >= 1:
                            dve.wait_ge(g3_psum, h)
                        for t in range(T):
                            r = dve.scalar_tensor_tensor(OTOK[:, t, :], C[:, 2, 256 * t:256 * t + 256], GSS[:, t:t + 1],
                                                         GRt[:, t, GLA_DV * h:GLA_DV * h + GLA_DV], ALU.mult, ALU.mult)
                        r.then_inc(g2_ready, 1)
                    if u == 11 + 2 * h:
                        for j in range(2):
                            dve.wait_ge(g3_hi, 2 * h + 2)
                            dve.scalar_tensor_tensor(HT_l[:, 2 * h + j, :], C[:, 3, 256 * j:256 * j + 256],
                                                     vec(V_GLA + 2 * h + j), HT_h[:, 2 * h + j, :].bitcast(f32),
                                                     ALU.mult, ALU.subtract).then_inc(g3_lo, 1)
                if u == 16:
                    moba_sums(MQt, 0, 6)
                if u == 17:
                    moba_norm(MQt, 0)
                if u == 20:
                    moba_sums(MKt, 1, 8)
                    moba_norm(MKt, 1)
                h = u - 21
                if 0 <= h < HEADS:
                    dve.wait_ge(m2_q, h + 1)
                    dve.tensor_scalar(QKT[:, h % 2, 256:512], C[:, 0, 256:512], vec(V_KN), float(DH) ** -0.5,
                                      ALU.mult, ALU.mult).then_inc(m2_k, 1)
                if 1 <= h < HEADS + 1:
                    att_scores(h - 1, DIST, 2.0 ** (-h))
                    att_norm(h - 1)
                if 3 <= h < HEADS + 3:
                    att_low(h - 3)

            add_to_x(0, U_FF0 - 1)
            rms_apply(1, 2)
            feed_forward(0, U_FF0)
            add_to_x(1, U_PLE - 1)
            rms_apply(2, 3)
            for q in range(5):
                low_at(U_PLE + q + SLOTS)
            for t in range(T):
                dve.wait_ge(pg_exp, t + 1)
                s = SG[:, t, :]
                chain(dve.tensor_scalar(s, s, 1.0, None, ALU.add))
                chain(dve.reciprocal(s, s))
                dve.wait_ge(ple_sb, 1)
                chain(dve.tensor_tensor(s, s, PLEO[:, t, :], ALU.mult))
                dve.tensor_tensor(X[:, t, :], X[:, t, :], s, ALU.add).then_inc(x_ready, 1)
            for t in range(T):
                xt_low(4, t)
            chain(dve.memset(Z[:, :, 0:2], 0.0))
            for q in range(12):
                n, pair, part = U_CONV + q, q // 3, q % 3
                dve.wait_ge(unit_used, n + 1)
                bank = C[:, q % 4, :].rearrange("p (a s) -> p a s", a=2)
                if part == 1:
                    dve.wait_ge(cv_c, pair + 1)
                    dve.tensor_tensor(Z[:, :, 2:258], bank, CS[:, pair % 2, :].rearrange("p (a s) -> p a s", a=2),
                                      ALU.mult).then_inc(cv_z, 1)
                    dve.wait_ge(cv_z, pair + 1)
                    if pair:
                        dve.wait_ge(cv_hi, pair)
                    for tap in (2, 1, 0):
                        for j in range(2):
                            w = vec(V_CONV + 8 * tap + 2 * pair + j)
                            z = Z[:, j, tap:tap + 256]
                            if tap == 2:
                                r = dve.tensor_scalar(VB[:, j, :], z, w, None, ALU.mult)
                            else:
                                r = dve.scalar_tensor_tensor(VB[:, j, :], z, w, VB[:, j, :], ALU.mult, ALU.add)
                        chain(r)
                low_at(n + SLOTS)
                if part == 2:
                    dve.tensor_tensor(VB, VB, bank, ALU.mult).then_inc(cv_v, 1)
                    dve.wait_ge(cv_v, pair + 1)
                    dve.wait_ge(cv_hi, pair + 1)
                    dve.tensor_tensor(OT_l[:, 2 * pair:2 * pair + 2, :], VB, OT_h[:, 2 * pair:2 * pair + 2, :].bitcast(f32),
                                      ALU.subtract).then_inc(cv_lo, 1)
            for q in range(4):
                low_at(U_CONVO + q + SLOTS)
            layer_norm(0, U_FF1 - 1)
            for t in range(T):
                xt_low(5, t)
            feed_forward(1, U_FF1)
            layer_norm(1, U_MLA - 1)
            for t in range(T):
                xt_low(6, t)
            for q in range(4):
                low_at(U_MLA + q + SLOTS)
            for i, (dst, src, width) in enumerate(((CQ, 0, QL), (CKV, 2, KVL))):
                dve.wait_ge(l_rstd, i + 1)
                for t in range(T):
                    dve.tensor_scalar(dst[:, t, :], ACC[:, src + t, 0:width], RQ[:, 2 * i + t:2 * i + t + 1], None,
                                      ALU.mult).then_inc(l_norm, 1)

            def rope(dst, x1, x2, cos, sin):
                shape = list(x1.shape)
                n = shape[1] * shape[2] * (shape[3] if len(shape) == 4 else 1)
                tmp = [RT[:, i, 0:n] for i in range(2)]
                if len(shape) == 4:
                    tmp = [v.rearrange("p (t h c) -> p t h c", h=shape[2], c=32) for v in tmp]
                    cos, sin = (v.unsqueeze(2).broadcast_to(shape) for v in (cos, sin))
                else:
                    tmp = [v.rearrange("p (t c) -> p t c", c=32) for v in tmp]
                for d, f1, f2, op in ((dst[0], cos, sin, ALU.subtract), (dst[1], sin, cos, ALU.add)):
                    dve.tensor_tensor(tmp[0], x1, f1, ALU.mult)
                    chain(dve.tensor_tensor(tmp[1], x2, f2, ALU.mult))
                    r = dve.tensor_tensor(d, tmp[0], tmp[1], op)
                    if d is dst[0]:
                        chain(r)
                return r

            kp = KPK.rearrange("p t (u c) -> p t u c", u=2)
            chain(rope((kp[:, :, 0, 0:32], kp[:, :, 0, 32:64]), ACC[:, 2:4, KVL:KVL + 32],
                       ACC[:, 2:4, KVL + 32:KVL + 64], COS, SIN))
            dve.tensor_copy(kp[:, :, 1, :], kp[:, :, 0, :]).then_inc(l_norm, 1)
            for k in range(5):
                dve.wait_ge(l_hi, (2, 2, 3, 5, 5)[k])
                src = C[:, k // 2, 256 * (k % 2):256 * (k % 2) + 256] if k < 3 else C[:, 2, 256 * (k - 3):256 * (k - 3) + 256]
                dve.scalar_tensor_tensor(HT_l[:, k, :], src, vec(V_GQ + k), HT_h[:, k, :].bitcast(f32), ALU.mult,
                                         ALU.subtract).then_inc(l_lo, 1)
            low_at(U_MLA + 4 + SLOTS)
            low_at(U_MLA + 5 + SLOTS)
            for q in range(4):
                n = U_MLA + 6 + q
                dve.wait_ge(unit_used, n + 1)
                if q:
                    dve.wait_ge(uq_rope, q)
                pe_part = ACC[:, 2 * (q % 2) + 1, 0:256].rearrange("p (t h c) -> p t h c", t=T, c=ROPE)
                qp = QPK.rearrange("p t (g h c) -> p t g h c", h=2, c=ROPE)[:, :, q]
                rope((qp[:, :, :, 0:32], qp[:, :, :, 32:64]), pe_part[:, :, :, 0:32], pe_part[:, :, :, 32:64], COS,
                     SIN).then_inc(uq_rope, 1)
                low_at(n + SLOTS)
            for s in range(HEADS + 2):
                if s < HEADS:
                    att_scores(HEADS + s, CHUNK_MASK, 1.0)
                    att_norm(HEADS + s)
                if s >= 2:
                    att_low(HEADS + s - 2)
            for q in range(4):
                low_at(U_WO + q + SLOTS)
            layer_norm(2, U_FF2 - 1)
            for t in range(T):
                xt_low(7, t)
            feed_forward(2, U_FF2)
            layer_norm(3, N_UNITS - 1)

        @block.tensor
        def _(pe):
            def three(dst, s_h, s_l, m_h, m_l, first, last):
                pe.matmul(dst, s_h, m_h, start=first, stop=False, skip_group_check=True)
                pe.matmul(dst, s_h, m_l, start=False, stop=False, skip_group_check=True)
                return pe.matmul(dst, s_l, m_h, start=False, stop=last, skip_group_check=True)

            def tokens_out(n, src_h, src_l, k0, bank, first, last, nk=4, width=512):
                slot = n % SLOTS
                pe.wait_ge(lo_ready, n + 1)
                for t in range(T):
                    s = slice(128 * t, 128 * t + 128)
                    for k in range(nk):
                        w = slice(k * width, k * width + width)
                        m = three(bank(t), src_h[:, k0 + k, s], src_l[:, k0 + k, s], HI[:, slot, w], LO[:, slot, w],
                                  first and k == 0, last and k == nk - 1)
                m.then_inc(unit_used, 1)

            def features_out(n, slot, dst, src_h, src_l, k0=0, nk=KD, width=256, tiles=(0, 1), inc=True):
                pe.wait_ge(lo_ready, n + 1)
                for i, j in enumerate(tiles):
                    for k in range(nk):
                        w = slice(k * width + 128 * j, k * width + 128 * j + 128)
                        m = three(dst(i), HI[:, slot, w], LO[:, slot, w], src_h[:, k0 + k, :], src_l[:, k0 + k, :],
                                  k == 0, k == nk - 1)
                if inc:
                    m.then_inc(unit_used, 1)
                return m

            def transpose_x(e, src, ready):
                for t in range(T):
                    pe.wait_ge(*ready(t))
                    for k in range(KD):
                        m = pe.transpose(C[:, 2 * t + k // 4, 128 * (k % 4):128 * (k % 4) + 128],
                                         src[:, t, 128 * k:128 * k + 128], IDENT)
                    m.then_inc(xt_psum, 1)

            def att_score(j, parts):
                if j:
                    pe.wait_ge(sc_max, j)
                for t in range(T):
                    dst = C[:, 1, 0:128] if t == 0 else C[:, 1, 128:384]
                    for i, (q, k) in enumerate(parts):
                        m = pe.matmul(dst, q[:, 128 * t:128 * t + 128], k[:, 0:128 * (t + 1)], start=(i == 0),
                                      stop=(i == len(parts) - 1), skip_group_check=True)
                m.then_inc(sc_psum, 1)

            def att_transpose(j):
                pe.wait_ge(sc_norm, j + 1)
                if j:
                    pe.wait_ge(pt_sb, j)
                for i in range(3):
                    m = pe.transpose(C[:, 2, 128 * i:128 * i + 128], PROBS[j // HEADS][:, j % 2, 128 * i:128 * i + 128], IDENT)
                m.then_inc(pt_psum, 1)

            def att_values(j, v, h):
                pe.wait_ge(pt_sb, j + 1)
                if j:
                    pe.wait_ge(o_lo, j)
                p = PRTS[j // HEADS][:, j % 2, :]
                pe.matmul(C[:, 3, 0:256], v[:, 0, 128 * h:128 * h + 128], p[:, 0:256], start=True, stop=False,
                          skip_group_check=True)
                pe.matmul(C[:, 3, 128:256], v[:, 1, 128 * h:128 * h + 128], p[:, 256:384], start=False, stop=True,
                          skip_group_check=True).then_inc(o_psum, 1)

            def feed_forward(f, base, e):
                pe.wait_ge(const_set, 8)
                for bank in range(4):
                    pe.matmul(ACC[:, bank, :], ZERO[:, 0:128], ZERO[:, 128:640], start=True, stop=False,
                              skip_group_check=True)
                pe.wait_ge(xt_lo, 2 * e + 2)

                def up(c, slot0, n0, first=False):
                    for half in range(2):
                        if not first:
                            pe.wait_ge(ff_relu, c * 2 + (16 * f + half - 1))
                        features_out(n0 + half, (slot0 + half) % SLOTS, lambda i: C[:, half, 256 * i:256 * i + 256], XT_h, XT_l)

                def down(c, par, slot0, n0, last=False):
                    for half in range(2):
                        pe.wait_ge(ff_lo, c * 2 + (16 * f + 2))
                        pe.wait_ge(lo_ready, n0 + half + 1)
                        slot = (slot0 + half) % SLOTS
                        for t in range(T):
                            s = slice(128 * t, 128 * t + 128)
                            for k in range(4):
                                w = slice(512 * k, 512 * k + 512)
                                m = three(ACC[:, 2 * t + half, :], HT_h[:, 4 * par + k, s], HT_l[:, 4 * par + k, s],
                                          HI[:, slot, w], LO[:, slot, w], False, last and k == 3)
                        m.then_inc(unit_used, 1)

                up(0, base % SLOTS, base, first=True)
                with pe.Fori(0, 3) as j:
                    for d in range(2):
                        up(j * 2 + (d + 1), (base + 2) % SLOTS, j * 8 + (base + 2 + 4 * d))
                        down(j * 2 + d, d, (base + 4) % SLOTS, j * 8 + (base + 4 + 4 * d))
                up(7, (base + 26) % SLOTS, base + 26)
                down(6, 0, (base + 28) % SLOTS, base + 28)
                down(7, 1, (base + 30) % SLOTS, base + 30, last=True)

            pe.wait_ge(cst_loaded, 16)
            pe.wait_ge(rows_loaded, 16 * 6)
            pe.transpose(ACC[:, 2, 0:N_VEC], ROWS, IDENT[0:N_VEC, 0:N_VEC]).then_inc(cols_psum, 1)
            pe.wait_ge(p_loaded, 16)
            for k in range(2):
                for t in range(T):
                    m = pe.transpose(ACC[:, 3, 256 * k + 128 * t:256 * k + 128 * t + 128],
                                     P_RAW[:, t, 128 * k:128 * k + 128], IDENT)
            m.then_inc(p_psum, 1)
            transpose_x(0, XN0, lambda t: (xn_ready, t + 1))
            pe.wait_ge(xt_lo, 2)
            pe.wait_ge(lr_split, 2)
            for t in range(T):
                s = slice(128 * t, 128 * t + 128)
                for k in range(KD):
                    m = three(C[:, 0, GLA_RANK * t:GLA_RANK * t + GLA_RANK], XT_h[:, k, s], XT_l[:, k, s],
                              LR_h[:, k, :], LR_l[:, k, :], k == 0, k == KD - 1)
            m.then_inc(lr_psum, 1)

            for u in range(N_MIX):
                b = u // 2
                if u < 36:
                    if u % 2 == 0:
                        if b >= 2:
                            pe.wait_ge(*block_read(b - 2))
                        if b == 1:
                            pe.wait_ge(cols_ready, 1)
                            pe.wait_ge(p_lo, 1)
                    src_h, src_l = (HT_h, HT_l) if b in (13, 15) else (XT_h, XT_l)
                    if b == 13 and u % 2 == 0:
                        pe.wait_ge(g3_lo, 2 * GLA_H)
                    tokens_out(u, src_h, src_l, 4 * (u % 2), lambda t: ACC[:, 2 * (b % 2) + t, :], u % 2 == 0, u % 2 == 1)
                elif u < 40:
                    c, kh = (u - 36) % 2, (u - 36) // 2
                    if kh == 0:
                        pe.wait_ge(*block_read(16 + c))
                        pe.wait_ge(o_lo, 4)
                    else:
                        pe.wait_ge(o_lo, HEADS)
                    tokens_out(u, OT_h, OT_l, 4 * kh, lambda t: ACC[:, 2 * c + t, :], kh == 0, kh == 1)
                else:
                    c, kh = (u - 40) % 2, (u - 40) // 2
                    pe.wait_ge(xt_lo, 2 + kh + 1)
                    pe.wait_ge(y_ready, 4)
                    tokens_out(u, XT_h, XT_l, 4 * kh, lambda t: ACC[:, 2 * t + c, :], kh == 0, kh == 1)
                if u == 0:
                    pe.wait_ge(lr_sb, 1)
                    for t in range(T):
                        m = pe.transpose(C[0:GLA_RANK, 1, 128 * t:128 * t + 128], GLR[:, t, :], IDENT)
                    m.then_inc(lrt_psum, 1)
                if u == 1:
                    pe.wait_ge(lrt_sb, 1)
                    pe.wait_ge(w2_loaded, 32)
                    for t in range(T):
                        m = pe.matmul(C[:, t, :], GLRT[:, 128 * t:128 * t + 128], W2E, start=True, stop=True)
                    m.then_inc(z_psum, 1)
                if u == 3:
                    pe.wait_ge(la_ready, 1)
                    for h in range(GLA_H):
                        for t in range(T):
                            pe.matmul(C[:, h // 2, 256 * (h % 2) + 128 * t:256 * (h % 2) + 128 * t + 128],
                                      LA[:, t, 128 * h:128 * h + 128], TRI, start=True, stop=True, skip_group_check=True)
                    for t in range(T):
                        m = pe.matmul(C[:, 2 + t, :], REM, LA[:, t, :], start=True, stop=True)
                    m.then_inc(cum_psum, 1)
                for at, src, bank, done, before in ((4, GQ, 2, qt_psum, 1), (5, GK, 0, kt_psum, 2)):
                    if u == at:
                        pe.wait_ge(blk_sb, before)
                        pe.wait_ge(cum_exp, 1)
                        for h in range(GLA_H):
                            for t in range(T):
                                m = pe.transpose(C[:, bank + h // 2, 256 * (h % 2) + 128 * t:256 * (h % 2) + 128 * t + 128],
                                                 src[:, t, 128 * h:128 * h + 128], IDENT)
                        m.then_inc(done, 1)
                for h in range(GLA_H):
                    if u == 9 + 2 * h:
                        pe.wait_ge(kd_ready, 2)
                        pe.wait_ge(qd_ready, 1)
                        pe.wait_ge(blk_sb, 3 + h // 2)
                        if h:
                            pe.wait_ge(g1_ready, h)
                        for n in range(4):
                            t, j = n // 2, n % 2
                            c = slice(GLA_CHUNK * n, GLA_CHUNK * n + GLA_CHUNK)
                            pe.matmul(C[64 * j:64 * j + 64, 1, 256 + 64 * t:256 + 64 * t + 64], KDT[:, h, c], QD[:, h, c],
                                      start=True, stop=True, skip_group_check=True)
                        for n in (0, 2, 1):
                            t, q = n // 2, slice(64 * (n % 2), 64 * (n % 2) + 64)
                            m = pe.matmul(KV_of(n), GK[q, t, 128 * h:128 * h + 128],
                                          GV_head(q, h, t), start=True, stop=True, skip_group_check=True)
                        m.then_inc(g1_psum, 1)
                    if u == 10 + 2 * h:
                        pe.wait_ge(g1_ready, h + 1)
                        if h:
                            pe.wait_ge(g2_ready, h)
                        for t in range(T):
                            dst = slice(256 * t, 256 * t + 256)
                            m = pe.matmul(C[:, 2, dst], AT[:, t, :], GV_head(slice(0, 128), h, t), start=True, stop=False,
                                          skip_group_check=True)
                            for n in range(max(1, 2 * t), 2 * t + 2):
                                j = n % 2
                                m = pe.matmul(C[64 * j:64 * j + 64, 2, dst], QD[:, h, 64 * n:64 * n + 64], S[:, n - 1, :],
                                              start=False, stop=(j == 1), skip_group_check=True)
                        m.then_inc(g2_psum, 1)
                    if u == 11 + 2 * h:
                        pe.wait_ge(g2_ready, h + 1)
                        if h:
                            pe.wait_ge(g3_lo, 2 * h)
                        for j in range(2):
                            for t in range(T):
                                m = pe.transpose(C[:, 3, 256 * j + 128 * t:256 * j + 128 * t + 128],
                                                 OTOK[:, t, 128 * j:128 * j + 128], IDENT)
                        m.then_inc(g3_psum, 1)
                h = u - 21
                if 0 <= h < HEADS:
                    if h == 0:
                        pe.wait_ge(m_norm, 2)
                        pe.wait_ge(g3_lo, 2 * GLA_H)
                    else:
                        pe.wait_ge(m2_k, h)
                        pe.wait_ge(m2_q, h)
                    for i, src in enumerate((MQ, MK)):
                        for t in range(T):
                            m = pe.transpose(C[:, 0, 256 * i + 128 * t:256 * i + 128 * t + 128],
                                             src[:, h // 4, t, 128 * (h % 4):128 * (h % 4) + 128], IDENT)
                    m.then_inc(m2_psum, 1)
                if 1 <= h < HEADS + 1:
                    j = h - 1
                    pe.wait_ge(m2_q, j + 1)
                    pe.wait_ge(m2_k, j + 1)
                    att_score(j, [(QKT[:, j % 2, 0:256], QKT[:, j % 2, 256:512])])
                if 2 <= h < HEADS + 2:
                    att_transpose(h - 2)
                if 3 <= h < HEADS + 3:
                    j = h - 3
                    pe.wait_ge(blk_sb, 9 + j // 4)
                    att_values(j, MVt, j)
                if u in (39, 40):
                    y, k0 = (Y0, 0) if u == 39 else (Y1, 4)
                    pe.wait_ge(y_ready, 3 + u - 39)
                    for k in range(4):
                        for t in range(T):
                            m = pe.transpose(C[:, (k0 + k) // 2, 256 * (k % 2) + 128 * t:256 * (k % 2) + 128 * t + 128],
                                             y[:, t, 128 * k:128 * k + 128], IDENT)
                    m.then_inc(xt_psum, 1)

            transpose_x(2, XN, lambda t: (xn_ready, 2 + t + 1))
            feed_forward(0, U_FF0, 2)
            transpose_x(3, XN, lambda t: (xn_ready, 4 + t + 1))
            pe.wait_ge(lo_ready, U_PLE + 1)
            pe.wait_ge(x_ready, 4)
            for t in range(T):
                s = slice(128 * t, 128 * t + 128)
                for c in range(2):
                    for k in range(2):
                        w = slice(1024 * k + 512 * c, 1024 * k + 512 * c + 512)
                        m = three(ACC[:, 2 * t + c, :], PT_h[:, k, s], PT_l[:, k, s], HI[:, U_PLE % SLOTS, w],
                                  LO[:, U_PLE % SLOTS, w], k == 0, k == 1)
            m.then_inc(unit_used, 1)
            pe.wait_ge(ple_sb, 1)
            pe.wait_ge(xt_lo, 8)
            for q in range(4):
                c, kh = q % 2, q // 2
                tokens_out(U_PLE + 1 + q, XT_h, XT_l, 4 * kh, lambda t: ACC[:, 2 * t + c, :], kh == 0, kh == 1)
            transpose_x(4, X, lambda t: (x_ready, 4 + t + 1))
            pe.wait_ge(xt_lo, 10)
            for q in range(12):
                n, pair, part = U_CONV + q, q // 3, q % 3
                if q >= 4:
                    old, opart = (q - 4) // 3, (q - 4) % 3
                    pe.wait_ge((cv_c, cv_z, cv_v)[opart], old + 1)
                features_out(n, n % SLOTS, lambda i: C[:, q % 4, 256 * i:256 * i + 256], XT_h, XT_l)
            for q in range(4):
                c, kh = q % 2, q // 2
                pe.wait_ge(cv_lo, 2 * kh + 2)
                tokens_out(U_CONVO + q, OT_h, OT_l, 4 * kh, lambda t: ACC[:, 2 * t + c, :], kh == 0, kh == 1)
            transpose_x(5, X, lambda t: (x_ready, 6 + t + 1))
            feed_forward(1, U_FF1, 5)
            transpose_x(6, X, lambda t: (x_ready, 8 + t + 1))

            pe.wait_ge(xt_lo, 14)
            for k in range(2):
                tokens_out(U_MLA + k, XT_h, XT_l, 4 * k, lambda t: ACC[:, t, 0:QL], k == 0, k == 1, width=QL)
            for k in range(2):
                tokens_out(U_MLA + 2 + k, XT_h, XT_l, 4 * k, lambda t: ACC[:, 2 + t, 0:KVL + ROPE], k == 0, k == 1,
                           width=KVL + ROPE)
            pe.wait_ge(l_norm, 2)
            for k in range(3):
                for t in range(T):
                    m = pe.transpose(C[:, k // 2, 256 * (k % 2) + 128 * t:256 * (k % 2) + 128 * t + 128],
                                     CQ[:, t, 128 * k:128 * k + 128], IDENT)
            m.then_inc(l_psum, 1)
            pe.wait_ge(l_norm, 4)
            for k in range(2):
                for t in range(T):
                    m = pe.transpose(C[:, 2, 256 * k + 128 * t:256 * k + 128 * t + 128], CKV[:, t, 128 * k:128 * k + 128],
                                     IDENT)
            m.then_inc(l_psum, 1)
            pe.wait_ge(l_norm, 5)
            for t in range(T):
                m = pe.transpose(C[:, 3, 128 * t:128 * t + 128], KPK[:, t, :], IDENT)
            m.then_inc(kp_psum, 1)
            pe.wait_ge(l_lo, 5)
            for g in range(4):
                features_out(U_MLA + 4, (U_MLA + 4) % SLOTS, lambda i: ACC[:, g, 256 * i:256 * i + 256], HT_h, HT_l, k0=3,
                             nk=2, width=1024, tiles=(2 * g, 2 * g + 1), inc=(g == 3))
            pe.wait_ge(kp_sb, 1)
            n = U_MLA + 5
            pe.wait_ge(lo_ready, n + 1)
            for t in range(T):
                s = slice(128 * t, 128 * t + 128)
                for c in range(2):
                    for k in range(2):
                        w = slice(1024 * k + 512 * c, 1024 * k + 512 * c + 512)
                        m = three(C[:, 2 * t + c, :], HT_h[:, 3 + k, s], HT_l[:, 3 + k, s], HI[:, n % SLOTS, w],
                                  LO[:, n % SLOTS, w], k == 0, k == 1)
            m.then_inc(unit_used, 1)

            def rope_transpose(q):
                pe.wait_ge(uq_rope, q + 1)
                pe.wait_ge(v_sb, 1)
                if q:
                    pe.wait_ge(qp_sb, q)
                for t in range(T):
                    m = pe.transpose(C[:, 0, 128 * t:128 * t + 128], QPK[:, t, 128 * q:128 * q + 128], IDENT)
                m.then_inc(qp_psum, 1)

            for q in range(4):
                n = U_MLA + 6 + q
                slot = n % SLOTS
                if q < 2:
                    pe.wait_ge(kn_sb, 1)
                else:
                    pe.wait_ge(uq_nope, q - 1)
                    pe.wait_ge(uq_rope, q - 1)
                pe.wait_ge(lo_ready, n + 1)
                nope, rot = ACC[:, 2 * (q % 2), :], ACC[:, 2 * (q % 2) + 1, :]
                for i in range(2):
                    for k in range(3):
                        w = slice(384 * k + 192 * i, 384 * k + 192 * i + 128)
                        three(nope[:, 256 * i:256 * i + 256], HI[:, slot, w], LO[:, slot, w], HT_h[:, k, :], HT_l[:, k, :],
                              k == 0, k == 2)
                for t in range(T):
                    s = slice(128 * t, 128 * t + 128)
                    for k in range(3):
                        hi_w, lo_w = (W[:, slot, 384 * k:384 * k + 384].rearrange("p (h c) -> p h c", c=192)[:, :, 128:192]
                                      for W in (HI, LO))
                        m = three(rot[:, 128 * t:128 * t + 128], HT_h[:, k, s], HT_l[:, k, s], hi_w, lo_w, k == 0, k == 2)
                m.then_inc(unit_used, 1)
                if q:
                    rope_transpose(q - 1)
            rope_transpose(3)
            pe.wait_ge(qp_sb, 4)
            pe.wait_ge(uq_nope, 4)
            for s in range(HEADS + 2):
                if s < HEADS:
                    r = slice(ROPE * (s % 2), ROPE * (s % 2) + ROPE)
                    att_score(HEADS + s, [(QNT[:, s, :], KNT[:, s, :]), (QPT[r, s // 2, :], KPT[r, :])])
                if 1 <= s < HEADS + 1:
                    att_transpose(HEADS + s - 1)
                if s >= 2:
                    att_values(HEADS + s - 2, VT, s - 2)
            for q in range(4):
                c, kh = q % 2, q // 2
                pe.wait_ge(o_lo, HEADS + 4 * kh + 4)
                tokens_out(U_WO + q, OT_h, OT_l, 4 * kh, lambda t: ACC[:, 2 * t + c, :], kh == 0, kh == 1)
            transpose_x(7, X, lambda t: (x_ready, 10 + t + 1))
            feed_forward(2, U_FF2, 7)


_INS = ["x", "p", "norm_mix", "w_in", "gla_gate_w2", "gla_gate_b", "gla_out_norm", "moba_q_norm", "moba_k_norm",
        "w_branch_a", "w_branch_b", "w_out", "norm_mlp", "w_up", "w_down", "norm_ple", "w_ple_gate", "w_ple",
        "sc_w_in_2", "sc_conv_w_2", "sc_w_out_2", "mla_w_dq_2", "mla_g_q_2", "mla_w_uq_2", "mla_w_dkv_2",
        "mla_g_kv_2", "mla_w_uk_2", "mla_w_uv_2", "mla_w_o_2", "ff_w1_2", "ff_w2_2", "ln_mix_g_2", "ln_mix_b_2",
        "ln_ff_g_2", "ln_ff_b_2"]


def _constants(np):
    c = np.zeros((128, N_CONST), np.float32)
    i, j = np.arange(128)[:, None], np.arange(128)[None, :]
    same = i // GLA_CHUNK == j // GLA_CHUNK
    c[:, C_ID:C_ID + 128] = i == j
    c[:, C_TRI:C_TRI + 128] = (same & (i <= j)) / 16.0
    c[:, C_REM:C_REM + 128] = (same & (i > j)) / 16.0
    for o, tq, tk in ((0, 0, 0), (128, 1, 0), (256, 1, 1)):
        q, k = 128 * tq + i, 128 * tk + j
        c[:, C_DIST + o:C_DIST + o + 128] = np.where(q >= k, k - q, MASKED)
        c[:, C_CHM + o:C_CHM + o + 128] = np.where(k // 64 <= q // 64, 0.0, MASKED)
    freq = np.float32(10000.0) ** (-np.arange(0, ROPE, 2, dtype=np.float32) / np.float32(ROPE))
    ang = (np.arange(SEQ, dtype=np.float32)[:, None] * freq[None, :].astype(np.float32)).astype(np.float32)
    for o, f in ((C_COS, np.cos), (C_SIN, np.sin)):
        c[:, o:o + 64] = f(ang).astype(np.float32).reshape(T, 128, 32).transpose(1, 0, 2).reshape(128, 64)
    mask = (np.arange(128)[:, None] % 64 <= np.arange(64)[None, :]).astype(np.float32)
    c[:, C_GM:C_GM + 128] = np.concatenate([mask, mask], axis=1)
    return c


def kernel(**inputs):
    import numpy as _np
    import concourse.bacc as _bacc
    from concourse import mybir as _mybir
    from concourse.bass_utils import run_bass_kernel_spmd as _run

    nc = _bacc.Bacc("TRN2", target_bir_lowering=False, num_devices=1)
    arrays, args = {}, {}
    for name in _INS + ["consts"]:
        v = _constants(_np) if name == "consts" else _np.ascontiguousarray(inputs[name])
        arrays[f"in_{name}"] = v
        args[name] = nc.dram_tensor(f"in_{name}", v.shape, _mybir.dt.from_np(v.dtype), kind="ExternalInput").ap()
    out = nc.dram_tensor("out", (1, SEQ, D), _mybir.dt.float32, kind="ExternalOutput").ap()
    program(nc, args, out)
    r = _run(nc, [arrays], core_ids=[0])
    return r.results[0]["out"]
```

```python
import concourse.bass as bass
from concourse import mybir
from contextlib import ExitStack

SEQ, D, D_FF = 256, 1024, 4096
T = SEQ // 128
KD = D // 128
GLA_H, GLA_DK, GLA_DV, GLA_RANK, GLA_CHUNK = 4, 128, 256, 16, 64
HEADS, DH = 8, 128
PLE = 256
QL, KVL, NOPE, ROPE = 384, 256, 128, 64
CONV = 3
EPS, LN_EPS = 1e-6, 1e-5
ALPHA = 4.0 ** 0.25
MASKED = -1e30

O_GQ, O_GK, O_GV, O_LR, O_GR = 0, 512, 1024, 2048, 2064
O_MQ, O_MK, O_MV, O_GA, O_GB = 3088, 4112, 5136, 6160, 7184

UNIT, SLOTS = 2048, 4
N_MIX = 44
N_FF = 32
U_FF0 = N_MIX
U_PLE = U_FF0 + N_FF
U_CONV = U_PLE + 5
U_CONVO = U_CONV + 12
U_FF1 = U_CONVO + 4
U_MLA = U_FF1 + N_FF
U_WO = U_MLA + 10
U_FF2 = U_WO + 4
N_UNITS = U_FF2 + N_FF

C_ID, C_TRI, C_REM, C_DIST, C_CHM = 0, 128, 256, 384, 768
C_COS, C_SIN, C_GM = 1152, 1216, 1280
N_CONST = 1408
V_CONV, V_GLA, V_QN, V_KN, V_GQ, V_GKV, N_VEC = 0, 24, 32, 33, 34, 37, 39


def program(nc, a, out):
    f32, f32r, bf16, i32 = mybir.dt.float32, mybir.dt.float32r, mybir.dt.bfloat16, mybir.dt.int32
    ALU, ACT, AX = mybir.AluOpType, mybir.ActivationFunctionType, mybir.AxisListType
    ctx = ExitStack()

    def rows4(w, k0, c0, width, nk=4):
        return w[k0:k0 + nk * 128, c0:c0 + width].rearrange("(k p) c -> p k c", p=128)

    w_in, w_a, w_b, w_o = a["w_in"][0], a["w_branch_a"][0], a["w_branch_b"][0], a["w_out"][0]
    two = lambda w, c: [rows4(w, 0, c, 512), rows4(w, 512, c, 512)]
    four = lambda w: [rows4(w, 0, 0, 512), rows4(w, 0, 512, 512), rows4(w, 512, 0, 512), rows4(w, 512, 512, 512)]
    mix_cols = [O_GQ, O_GK, O_GV, O_GV + 512, O_GR, O_GR + 512, O_MQ, O_MQ + 512, O_MK, O_MK + 512, O_MV, O_MV + 512]
    units = []
    for c in mix_cols:
        units += two(w_in, c)
    units += two(w_in, O_GA) + two(w_a, 0) + two(w_in, O_GA + 512) + two(w_a, 512)
    units += two(w_in, O_GB) + two(w_in, O_GB + 512) + two(w_b, 0) + two(w_b, 512) + four(w_o)
    assert len(units) == N_MIX

    def up_unit(w, chunk, half):
        col = chunk * 512 + half * 256
        return w[:, bass.ds(col, 256)].rearrange("(k p) c -> p k c", p=128)

    def down_unit(w, chunk, half):
        return w[bass.ds(chunk * 512, 512), 512 * half:512 * half + 512].rearrange("(k p) c -> p k c", p=128)

    ffs = [(U_FF0, a["w_up"][0], a["w_down"][0]), (U_FF1, a["ff_w1_2"][0], a["ff_w2_2"][0]),
           (U_FF2, a["ff_w1_2"][1], a["ff_w2_2"][1])]
    units += [None] * N_FF
    units += [rows4(a["w_ple"][0], 0, 0, 1024, nk=2)] + four(a["w_ple_gate"][0])
    for pair in range(KD // 2):
        for part in (1, 2, 0):
            col = part * D + pair * 256
            units.append(a["sc_w_in_2"][0][:, col:col + 256].rearrange("(k p) c -> p k c", p=128))
    units += four(a["sc_w_out_2"][0]) + [None] * N_FF
    units += [rows4(a["mla_w_dkv_2"][0], 512 * k, 0, KVL + ROPE) for k in range(2)]
    units += [rows4(a["mla_w_dq_2"][0], 512 * k, 0, QL) for k in range(2)]
    units += [a[n][0].rearrange("(k p) h d -> p k (h d)", p=128) for n in ("mla_w_uk_2", "mla_w_uv_2")]
    units += [rows4(a["mla_w_uq_2"][0], 0, 384 * q, 384, nk=3) for q in range(4)]
    units += four(a["mla_w_o_2"][0]) + [None] * N_FF
    assert len(units) == N_UNITS
    UNIT_K = [None if u is None else u.shape[1] for u in units]
    UNIT_C = [None if u is None else u.shape[2] for u in units]

    with ctx:
        def sb(name, cols, dt=f32, rows=128):
            return ctx.enter_context(nc.sbuf_tensor(name, [rows] + list(cols), dt))

        def sem(name):
            return ctx.enter_context(nc.semaphore(name))

        RAW = sb("RAW", [SLOTS, UNIT])
        HI = sb("HI", [SLOTS, UNIT], f32r)
        LO = sb("LO", [SLOTS, UNIT], f32r)
        X = sb("X", [T, D])
        XT_h = sb("XT_h", [KD, SEQ], f32r)
        XT_l = sb("XT_l", [KD, SEQ], f32r)
        HT_h = sb("HT_h", [KD, SEQ], f32r)
        HT_l = sb("HT_l", [KD, SEQ], f32r)
        PT_h = sb("PT_h", [PLE // 128, SEQ], f32r)
        PT_l = sb("PT_l", [PLE // 128, SEQ], f32r)
        LR_h = sb("LR_h", [KD, GLA_RANK], f32r)
        LR_l = sb("LR_l", [KD, GLA_RANK], f32r)
        CST = sb("CST", [N_CONST])
        COLS = sb("COLS", [N_VEC + 1])
        ST = sb("ST", [160])
        R = sb("R", [11264])
        overlay = ExitStack()
        with overlay:
            G = overlay.enter_context(nc.sbuf_tensor("G", [128, 4096], f32))
        OT_h = sb("OT_h", [KD, SEQ], f32r)
        OT_l = sb("OT_l", [KD, SEQ], f32r)
        ACC = ctx.enter_context(nc.psum_tensor("ACC", [128, 4, 512], f32))
        C = ctx.enter_context(nc.psum_tensor("C", [128, 4, 512], f32))

        def cut(base, lo_, *dims):
            n = 1
            for d in dims:
                n *= d
            v = base[:, lo_:lo_ + n]
            if len(dims) == 2:
                v = v.rearrange("p (a b) -> p a b", b=dims[1])
            if len(dims) == 3:
                v = v.rearrange("p (a b c) -> p a b c", b=dims[1], c=dims[2])
            return v

        IDENT = CST[:, C_ID:C_ID + 128]
        TRI = CST[:, C_TRI:C_TRI + 128]
        REM = CST[:, C_REM:C_REM + 128]
        DIST = CST[:, C_DIST:C_DIST + 384]
        CHUNK_MASK = CST[:, C_CHM:C_CHM + 384]
        COS = cut(CST, C_COS, T, 32)
        SIN = cut(CST, C_SIN, T, 32)
        GLA_MASK = cut(CST, C_GM, T, 64).bitcast(i32)
        vec = lambda i: COLS[:, i:i + 1]
        GQ, LA, GK, GV = cut(R, 0, T, 512), cut(R, 1024, T, 512), cut(R, 2048, T, 512), cut(R, 3072, T, 2, 512)
        GR, MQ = cut(R, 5120, T, 2, 512), cut(R, 0, T, 2, 512)
        GV, GR, MQ = (v.rearrange("p t b c -> p b t c") for v in (GV, GR, MQ))
        MK = cut(R, 7168, T, 2, 512).rearrange("p t b c -> p b t c")
        MV = cut(R, 3072, T, 2, 512).rearrange("p t b c -> p b t c")
        flat = lambda o: cut(R, o, T, 1024)
        GVt, GRt, MQt, MKt, MVt = flat(3072), flat(5120), flat(0), flat(7168), flat(3072)
        QKT = cut(R, 2048, 2, 512)
        PROBS, PRTS = (cut(R, 5120, 2, 384), cut(R, 8704, 2, 384)), (cut(R, 5888, 2, 384), cut(R, 9472, 2, 256 + 128))
        DIAGS = ((cut(R, 6656, 2, 128), cut(R, 6912, 2, 128)), (cut(R, 8448, 2, 128), cut(R, 10496, 2, 128)))
        SG0, Y0, Y1, SG1 = cut(R, 9216, T, 512), cut(R, 10240, T, 512), cut(R, 0, T, 512), cut(R, 1024, T, 512)
        MSQ = cut(R, 9216, T, 512)
        W2E, GLRT = R[0:33, 9216:9728], R[0:33, 9728:9984]
        GLR, LR_RAW = cut(R, 9984, T, GLA_RANK), cut(R, 10016, KD, GLA_RANK)
        QD, KDT, AT = cut(G, 0, GLA_H, SEQ), cut(G, 1024, GLA_H, SEQ), cut(G, 2048, T, 128)
        S = cut(G, 2304, 3, GLA_DV)
        OTOK = cut(G, 3072, T, GLA_DV)
        SQJ = cut(G, 3584, T, GLA_DV)
        RELU, SQ, XN = cut(R, 0, 2, 512), cut(R, 1024, 2, 512), cut(R, 2048, T, D)
        GAIN, BIAS, PLEO, SG = R[:, 4096:5120], R[:, 5120:6144], cut(R, 6144, T, D), cut(R, 8192, T, D)
        ZERO = R[:, 10880:11200].bitcast(bf16)
        CS, VB = cut(R, 0, 2, 512), cut(R, 1024, 2, 256)
        Z = cut(R, 1536, 2, 258)
        P_RAW, ROWS, XN0, GAIN0 = cut(R, 7168, T, PLE), R[0:N_VEC, 7680:7808], cut(R, 2048, T, D), R[:, 4096:5120]
        QNT, KNT, VT = cut(R, 0, HEADS, SEQ), cut(R, 2048, HEADS, SEQ), cut(R, 4096, T, D)
        QPT, QPK = cut(R, 6144, 4, SEQ), cut(R, 7168, T, HEADS * ROPE)
        KPT, KPK = R[:, 8192:8448], cut(R, 8448, T, 2 * ROPE)
        CQ, CKV = cut(R, 8704, T, QL), cut(R, 9472, T, KVL)
        RT = cut(R, 9984, 2, 256)

        LATENT_GAIN = (V_GQ, V_GQ + 1, V_GQ + 2, V_GKV, V_GKV + 1)

        RSTD, SS, MVAR = ST[:, 0:2], ST[:, 2:4], cut(ST, 4, T, 2)
        BN = cut(ST, 8, T, 12)
        EPSC, LNEPSC, ONEC = ST[:, 32:33], ST[:, 33:34], ST[:, 34:35]
        NMAX, RSUM, RINV = cut(ST, 36, 2, 2), cut(ST, 40, 2, 2), cut(ST, 44, 2, 2)
        SSQ, RQ = ST[:, 48:64], ST[:, 64:80]
        DEC = cut(ST, 80, GLA_H, 4)
        GSS = ST[:, 96:98]

        raw_ready = [sem(f"raw_ready{s}") for s in range(SLOTS)]
        hi_ready, lo_ready = sem("hi_ready"), sem("lo_ready")
        unit_used = sem("unit_used")
        tail = sem("tail")
        x_loaded, cst_loaded, rows_loaded, p_loaded = [sem("x_loaded0"), sem("x_loaded1")], sem("cst_loaded"), sem("rows_loaded"), sem("p_loaded")
        ident_loaded = sem("ident_loaded")
        lr_loaded, w2_loaded, gain_loaded = sem("lr_loaded"), sem("w2_loaded"), sem("gain_loaded")
        const_set = sem("const_set")
        act_self, dve_self = sem("act_self"), sem("dve_self")
        rstd_ready, xn_ready = sem("rstd_ready"), sem("xn_ready")
        xt_psum, xt_hi, xt_lo = sem("xt_psum"), sem("xt_hi"), sem("xt_lo")
        x_ready, mv_ready = sem("x_ready"), sem("mv_ready")
        cols_psum, cols_ready = sem("cols_psum"), sem("cols_ready")
        p_psum, p_hi, p_lo = sem("p_psum"), sem("p_hi"), sem("p_lo")
        lr_split, lr_psum, lr_sb, lrt_psum, lrt_sb = (sem("lr_split"), sem("lr_psum"), sem("lr_sb"),
                                                      sem("lrt_psum"), sem("lrt_sb"))
        z_psum, z_l, la_ready = sem("z_psum"), sem("z_l"), sem("la_ready")
        blk_sb = sem("blk_sb")
        cum_psum, cum_exp = sem("cum_psum"), sem("cum_exp")
        qt_psum, qd_ready, kt_psum, kd_ready = sem("qt_psum"), sem("qd_ready"), sem("kt_psum"), sem("kd_ready")
        g1_psum, g1_s1, g1_ready = sem("g1_psum"), sem("g1_s1"), sem("g1_ready")
        g2_psum, g2_rstd, g2_ready = sem("g2_psum"), sem("g2_rstd"), sem("g2_ready")
        g3_psum, g3_hi, g3_lo = sem("g3_psum"), sem("g3_hi"), sem("g3_lo")
        sig_e, gr_ready = sem("sig_e"), sem("gr_ready")
        m_sq, m_ssq, m_rstd, m_norm = sem("m_sq"), sem("m_ssq"), sem("m_rstd"), sem("m_norm")
        m2_psum, m2_q, m2_k = sem("m2_psum"), sem("m2_q"), sem("m2_k")
        sc_psum, sc_max, sc_exp, diag_ready = sem("sc_psum"), sem("sc_max"), sem("sc_exp"), sem("diag_ready")
        pt_psum, pt_sb, o_psum, o_hi, o_lo = sem("pt_psum"), sem("pt_sb"), sem("o_psum"), sem("o_hi"), sem("o_lo")
        y_ready = sem("y_ready")
        ff_relu, ff_sq, ff_hi, ff_lo = sem("ff_relu"), sem("ff_sq"), sem("ff_hi"), sem("ff_lo")
        ple_sb, pg_sig = sem("ple_sb"), sem("pg_sig")
        cv_c, cv_z, cv_v, cv_hi, cv_lo = sem("cv_c"), sem("cv_z"), sem("cv_v"), sem("cv_hi"), sem("cv_lo")
        l_rstd, l_norm, l_psum, l_hi, l_lo = sem("l_rstd"), sem("l_norm"), sem("l_psum"), sem("l_hi"), sem("l_lo")
        kp_psum, kp_sb = sem("kp_psum"), sem("kp_sb")
        kn_sb, v_sb, uq_nope, uq_rope, qp_psum, qp_sb = (sem("kn_sb"), sem("v_sb"), sem("uq_nope"), sem("uq_rope"),
                                                         sem("qp_psum"), sem("qp_sb"))
        stored = sem("stored")

        def block_read(b):
            if b in (4, 5):
                return gr_ready, b - 3
            if b in (13, 15):
                return y_ready, (b - 11) // 2
            if b >= 12:
                return sig_e, {12: 3, 14: 4, 16: 5, 17: 6}[b]
            return blk_sb, b + 1 if b < 4 else b - 1

        def KV_of(n):
            return C[:, n % 2, 128 * n:128 * n + 256] if n != 1 else C[:, 1, 0:256]

        def GV_head(rows, h, t):
            return GVt[rows, t, GLA_DV * h:GLA_DV * h + GLA_DV]

        block = ctx.enter_context(nc.Block())

        @block.sync
        def _(sp):
            def load(n, slot, view):
                nk, width = view.shape[1], view.shape[2]
                dst = RAW[:, slot, 0:nk * width].rearrange("p (k c) -> p k c", c=width)
                sp.dma_start(dst, view).then_inc(raw_ready[slot], 16)

            sp.dma_start(IDENT, a["consts"][:, C_ID:C_ID + 128]).then_inc(ident_loaded, 16)
            for t in range(T):
                sp.dma_start(X[:, t, :], a["x"][0, 128 * t:128 * t + 128, :]).then_inc(x_loaded[t], 16)
            sp.dma_start(LR_RAW, w_in[:, O_LR:O_LR + GLA_RANK].rearrange("(k p) c -> p k c", p=128)).then_inc(lr_loaded, 16)
            for n in range(N_UNITS):
                if units[n] is None:
                    continue
                if n >= SLOTS:
                    sp.wait_ge(lo_ready, n - SLOTS + 1)
                load(n, n % SLOTS, units[n])
                if n == 1:
                    sp.dma_start(CST[:, C_ID + 128:N_CONST], a["consts"][:, C_ID + 128:N_CONST]).then_inc(cst_loaded, 16)
                if n + 1 in (U_FF0, U_FF1, U_FF2):
                    base, up, down = ffs[(U_FF0, U_FF1, U_FF2).index(n + 1)]
                    for half in range(2):
                        sp.wait_ge(lo_ready, base + half - SLOTS + 1)
                        load(None, (base + half) % SLOTS, up_unit(up, 0, half))
                    with sp.Fori(0, 7) as i:
                        for q in range(4):
                            sp.wait_ge(lo_ready, i * 4 + (base + 2 + q - SLOTS + 1))
                            v = up_unit(up, i + 1, q) if q < 2 else down_unit(down, i, q - 2)
                            load(None, (base + 2 + q) % SLOTS, v)
                    for half in range(2):
                        sp.wait_ge(lo_ready, base + 30 + half - SLOTS + 1)
                        load(None, (base + 30 + half) % SLOTS, down_unit(down, 7, half))
            for t in range(T):
                sp.wait_ge(x_ready, 12 + t + 1)
                sp.dma_start(out[0, 128 * t:128 * t + 128, :], X[:, t, :]).then_inc(stored, 16)
            sp.wait_ge(stored, 16 * T)

        @block.gpsimd
        def _(pool):
            def gain(dst, row):
                pool.dma_start(dst, row.partition_broadcast(128)).then_inc(gain_loaded, 16)

            gain(GAIN0, a["norm_mix"][0])
            pool.memset(EPSC, EPS).then_inc(const_set, 1)
            pool.memset(LNEPSC, LN_EPS).then_inc(const_set, 1)
            pool.memset(ONEC, 1.0).then_inc(const_set, 1)
            for row, v in ((V_CONV, a["sc_conv_w_2"][0].rearrange("k (j p) -> (k j) p", p=128)),
                           (V_GLA, a["gla_out_norm"][0].rearrange("h (j p) -> (h j) p", p=128)),
                           (V_QN, a["moba_q_norm"]), (V_KN, a["moba_k_norm"]),
                           (V_GQ, a["mla_g_q_2"][0].rearrange("(j p) -> j p", p=128)),
                           (V_GKV, a["mla_g_kv_2"][0].rearrange("(j p) -> j p", p=128))):
                pool.dma_start(R[row:row + v.shape[0], 7680:7808], v).then_inc(rows_loaded, 16)
            pool.dma_start(P_RAW, a["p"][0, 0].rearrange("(t p) c -> p t c", p=128)).then_inc(p_loaded, 16)
            pool.memset(W2E, 0.0).then_inc(const_set, 1)
            pool.memset(GLRT, 0.0).then_inc(const_set, 1)
            pool.wait_ge(const_set, 5)
            pool.memset(GLRT[32:33, :], 1.0).then_inc(const_set, 1)
            pool.dma_start(W2E[0:GLA_RANK, :], a["gla_gate_w2"][0]).then_inc(w2_loaded, 16)
            pool.dma_start(W2E[32:33, :], a["gla_gate_b"]).then_inc(w2_loaded, 16)
            pool.wait_ge(const_set, 6)
            pool.memset(AT, 0.0).then_inc(const_set, 1)
            pool.wait_ge(o_lo, HEADS)
            gain(GAIN, a["norm_mlp"][0])
            pool.wait_ge(xt_lo, 4)
            pool.memset(ZERO, 0.0).then_inc(const_set, 1)
            pool.wait_ge(xn_ready, 4)
            gain(GAIN, a["norm_ple"][0])
            for j, (g, b) in enumerate((("ln_mix_g_2", "ln_mix_b_2"), ("ln_ff_g_2", "ln_ff_b_2")) * 2):
                if j == 0:
                    pool.wait_ge(xn_ready, 6)
                else:
                    pool.wait_ge(x_ready, 6 + 2 * j)
                if j == 2:
                    pool.wait_ge(o_psum, 2 * HEADS)
                gain(GAIN, a[g][j // 2])
                gain(BIAS, a[b][j // 2])
            pool.wait_ge(gain_loaded, 16 * 11)

        @block.scalar
        def _(act):
            own = [0]

            def chain(ins):
                own[0] += 1
                ins.then_inc(act_self, 1)
                act.wait_ge(act_self, own[0])

            def hi(n, slot, turn, width=UNIT, old=True):
                act.wait_ge(raw_ready[slot], turn)
                if old:
                    act.wait_ge(unit_used, n - SLOTS + 1)
                act.activation(HI[:, slot, 0:width], RAW[:, slot, 0:width], ACT.Copy).then_inc(hi_ready, 1)

            def hi_at(n):
                if n < N_UNITS:
                    w = UNIT if units[n] is None else UNIT_K[n] * UNIT_C[n]
                    hi(n, n % SLOTS, 16 * (n // SLOTS + 1), w, n >= SLOTS)

            def rstd(dst, src, scale, eps):
                chain(act.activation(dst, src, ACT.Ln, bias=eps, scale=scale))
                return act.activation(dst, dst, ACT.Exp, scale=-0.5)

            def xt_split(e, t):
                act.wait_ge(xt_psum, 2 * e + t + 1)
                act.activation(XT_h[:, :, 128 * t:128 * t + 128],
                               C[:, 2 * t:2 * t + 2, :].rearrange("p b (k s) -> p (b k) s", s=128), ACT.Copy).then_inc(xt_hi, 1)

            def rms(r, tiles=range(T)):
                for t in tiles:
                    if r == 0:
                        act.wait_ge(x_loaded[t], 16)
                        act.wait_ge(const_set, 3)
                    else:
                        act.wait_ge(x_ready, 2 * (r - 1) + t + 1)
                    junk = XN0 if r == 0 else XN
                    chain(act.activation(junk[:, t, :], X[:, t, :], ACT.Square, accum_out=SS[:, t:t + 1]))
                    rstd(RSTD[:, t:t + 1], SS[:, t:t + 1], 1.0 / D, EPSC).then_inc(rstd_ready, 1)

            def ln(j, tiles=range(T)):
                for t in tiles:
                    act.wait_ge(mv_ready, 2 * j + t + 1)
                    rstd(RSTD[:, t:t + 1], MVAR[:, t, 1:2], 1.0, LNEPSC).then_inc(rstd_ready, 1)

            def att_exp(j):
                p, PROB = j % 2, PROBS[j // HEADS]
                act.wait_ge(sc_max, j + 1)
                act.activation(PROB[:, p, 0:128], PROB[:, p, 0:128], ACT.Exp, bias=NMAX[:, p, 0:1],
                               accum_out=RSUM[:, p, 0:1])
                act.activation(PROB[:, p, 128:384], PROB[:, p, 128:384], ACT.Exp, bias=NMAX[:, p, 1:2],
                               accum_out=RSUM[:, p, 1:2]).then_inc(sc_exp, 1)

            def att_pt(j):
                act.wait_ge(pt_psum, j + 1)
                if j >= 2:
                    act.wait_ge(o_psum, j - 1)
                act.activation(PRTS[j // HEADS][:, j % 2, :], C[:, 2, 0:384], ACT.Copy).then_inc(pt_sb, 1)

            def att_out(j):
                act.wait_ge(o_psum, j + 1)
                act.activation(OT_h[:, j % HEADS, :], C[:, 3, 0:SEQ], ACT.Copy).then_inc(o_hi, 1)

            def feed_forward(f, base):
                def squares(c, half, slot_unit):
                    if not (isinstance(c, int) and c == 0 and f == 0):
                        act.wait_ge(ff_sq, c * 2 + (16 * f + half - 1))
                    act.wait_ge(unit_used, slot_unit + 1)
                    act.activation(RELU[:, half, :], C[:, half, :], ACT.Relu).then_inc(ff_relu, 1)
                    act.wait_ge(ff_relu, c * 2 + (16 * f + half + 1))

                def square(par, half):
                    k = 4 * par + 2 * half
                    act.activation(HT_h[:, k:k + 2, :].rearrange("p a b -> p (a b)"), RELU[:, half, :],
                                   ACT.Square).then_inc(ff_hi, 1)

                for half in range(2):
                    squares(0, half, base + half)
                    square(0, half)
                    hi_at(base + half + SLOTS)

                def step(i, i_unit, par, peel):
                    for q in range(4):
                        if q < 2:
                            squares(i + 1, q, i_unit + (base + 2 + q))
                            square(par, q)
                        if peel:
                            hi_at(base + 2 + 4 * i + q + SLOTS)
                        else:
                            n0 = base + 2 + q + SLOTS
                            hi(i_unit + n0, n0 % SLOTS, i * 16 + 16 * (n0 // SLOTS + 1))

                with act.Fori(0, 3) as j:
                    for d in range(2):
                        step(j * 2 + d, j * 8 + 4 * d, (d + 1) % 2, False)
                step(6, 24, 1, True)

            rms(0)
            hi_at(0)
            for t in range(T):
                xt_split(0, t)
            act.wait_ge(lr_loaded, 16)
            act.activation(LR_h[:], LR_RAW, ACT.Copy).then_inc(lr_split, 1)
            for n in range(1, SLOTS):
                hi_at(n)

            def setup_rest():
                act.wait_ge(lr_psum, 1)
                act.activation(GLR, C[:, 0, 0:T * GLA_RANK].rearrange("p (t c) -> p t c", t=T), ACT.Copy).then_inc(lr_sb, 1)
                act.wait_ge(lrt_psum, 1)
                act.wait_ge(const_set, 6)
                act.activation(GLRT[0:GLA_RANK, :], C[0:GLA_RANK, 1, 0:SEQ], ACT.Copy).then_inc(lrt_sb, 1)
                act.wait_ge(cols_psum, 1)
                act.activation(COLS[:, 0:N_VEC], C[:, 2, 0:N_VEC], ACT.Copy).then_inc(cols_ready, 1)
                act.wait_ge(p_psum, 1)
                act.activation(PT_h[:].rearrange("p a b -> p (a b)"), C[:, 3, :], ACT.Copy).then_inc(p_hi, 1)

            blocks = [GQ, GK, GV[:, 0], GV[:, 1], None, None, MQ[:, 0], MQ[:, 1], MK[:, 0], MK[:, 1], MV[:, 0], MV[:, 1]]
            sig_of = {4: GR[:, 0], 5: GR[:, 1], 12: SG0, 14: SG0, 16: SG1, 17: SG0}

            def moba_scales(b, i):
                act.wait_ge(blk_sb, i + 5)
                if i:
                    act.wait_ge(m_ssq, i)
                act.activation(MSQ, blocks[b], ACT.Square).then_inc(m_sq, 1)
                act.wait_ge(m_ssq, i + 1)
                r = slice(8 * (i % 2), 8 * (i % 2) + 8)
                rstd(RQ[:, r], SSQ[:, r], 1.0 / DH, EPSC).then_inc(m_rstd, 1)

            for u in range(N_MIX):
                b = u // 2
                if u % 2 and b < 18:
                    src = ACC[:, 2 * (b % 2):2 * (b % 2) + 2, :]
                    if b in sig_of:
                        act.wait_ge(unit_used, u + 1)
                        if b in (14, 17):
                            act.wait_ge(y_ready, 1 if b == 14 else 2)
                        act.activation(sig_of[b], src, ACT.Sigmoid).then_inc(sig_e, 1)
                    elif b < 12:
                        act.wait_ge(unit_used, u + 1)
                        if b == 6:
                            act.wait_ge(kd_ready, 2)
                        if b == 10:
                            act.wait_ge(g2_psum, GLA_H)
                        act.activation(blocks[b], src, ACT.Copy).then_inc(blk_sb, 1)
                if u == 0:
                    setup_rest()
                if u == 1:
                    act.wait_ge(z_psum, 1)
                    zz = C[:, 0:2, :]
                    chain(act.activation(LA, zz, ACT.Abs))
                    chain(act.activation(LA, LA, ACT.Exp, scale=-1.0))
                    act.activation(LA, LA, ACT.Ln, bias=ONEC, scale=1.0).then_inc(z_l, 1)
                if u == 3:
                    act.wait_ge(cum_psum, 1)
                    cb = C[:, 0:2, :].rearrange("p b (h s) -> p (b h) s", s=SEQ)
                    act.activation(QD, cb, ACT.Exp)
                    act.activation(KDT, cb, ACT.Exp, scale=-1.0)
                    act.activation(LA, C[:, 2:4, :], ACT.Exp).then_inc(cum_exp, 1)
                for h in range(GLA_H):
                    if u == 10 + 2 * h:
                        act.wait_ge(g1_psum, h + 1)
                        act.activation(S[:, 0, :], C[:, 0, 0:GLA_DV], ACT.Copy).then_inc(g1_s1, 1)
                    if u == 11 + 2 * h:
                        act.wait_ge(g2_psum, h + 1)
                        for t in range(T):
                            r = act.activation(SQJ[:, t, :], C[:, 2, 256 * t:256 * t + 256], ACT.Square,
                                               accum_out=GSS[:, t:t + 1])
                        chain(r)
                        rstd(GSS, GSS, 1.0 / GLA_DV, EPSC).then_inc(g2_rstd, 1)
                    if u == 12 + 2 * h:
                        act.wait_ge(g3_psum, h + 1)
                        for j in range(2):
                            act.activation(HT_h[:, 2 * h + j, :], C[:, 3, 256 * j:256 * j + 256], ACT.Copy,
                                           scale=vec(V_GLA + 2 * h + j)).then_inc(g3_hi, 1)
                if u in (14, 16, 18, 20):
                    moba_scales(u // 2 - 1, u // 2 - 7)
                h = u - 22
                if 0 <= h < HEADS:
                    act.wait_ge(m2_psum, h + 1)
                    act.activation(QKT[:, h % 2, 0:256], C[:, 0, 0:256], ACT.Copy, scale=vec(V_QN)).then_inc(m2_q, 1)
                if 1 <= h < HEADS + 1:
                    att_exp(h - 1)
                if 2 <= h < HEADS + 2:
                    att_pt(h - 2)
                if 3 <= h < HEADS + 3:
                    att_out(h - 3)
                if u in (38, 40):
                    k = 2 * (u - 38)
                    act.wait_ge(xt_psum, 3 + (u - 38) // 2)
                    act.activation(XT_h[:, k:k + 4, :], C[:, k // 2:k // 2 + 2, :].rearrange("p b (k s) -> p (b k) s", s=SEQ),
                                   ACT.Copy).then_inc(xt_hi, 1)
                if u < N_MIX - 2:
                    hi_at(u + SLOTS)

            def finish_pair(last, e, scales=None):
                for t in range(T):
                    if scales is not None:
                        scales[0](scales[1], (t,))
                    xt_split(e, t)
                    if scales is None:
                        hi_at(last - 1 + t + SLOTS)
                if scales is not None:
                    hi_at(last - 1 + SLOTS)
                    hi_at(last + SLOTS)

            finish_pair(U_FF0 - 1, 2, (rms, 1))
            feed_forward(0, U_FF0)
            rms(2)
            for t in range(T):
                act.wait_ge(tail, 3) if t == 0 else act.wait_ge(unit_used, U_PLE + 1)
                act.activation(PLEO[:, t, :], C[:, 2 * t:2 * t + 2, :].rearrange("p b c -> p (b c)"), ACT.Copy).then_inc(ple_sb, 1)
            finish_pair(U_PLE - 1, 3)
            for q in range(3):
                hi_at(U_PLE + q + SLOTS)
            for t in range(T):
                act.wait_ge(tail, 4) if t == 0 else act.wait_ge(unit_used, U_CONV)
                act.activation(SG[:, t, :], ACC[:, 2 * t:2 * t + 2, :].rearrange("p b c -> p (b c)"),
                               ACT.Sigmoid).then_inc(pg_sig, 1)
            finish_pair(U_CONV - 1, 4)
            for q in range(12):
                n, pair, part = U_CONV + q, q // 3, q % 3
                act.wait_ge(unit_used, n + 1)
                if part == 0:
                    if pair >= 2:
                        act.wait_ge(cv_z, pair - 1)
                    act.activation(CS[:, pair % 2, :], C[:, q % 4, :], ACT.Copy).then_inc(cv_c, 1)
                hi_at(n + SLOTS)
                if part == 2:
                    act.wait_ge(cv_v, pair + 1)
                    act.activation(OT_h[:, 2 * pair:2 * pair + 2, :].rearrange("p a b -> p (a b)"),
                                   VB.rearrange("p a b -> p (a b)"), ACT.Copy).then_inc(cv_hi, 1)
            for q in range(2):
                hi_at(U_CONVO + q + SLOTS)
            finish_pair(U_FF1 - 1, 5, (ln, 0))
            feed_forward(1, U_FF1)
            finish_pair(U_MLA - 1, 6, (ln, 1))

            def latent(i, junk, bank, width, last):
                act.wait_ge(unit_used, last + 1)
                for t in range(T):
                    r = act.activation(junk[:, t, :], ACC[:, bank + t, 0:width], ACT.Square,
                                       accum_out=GSS[:, t:t + 1])
                chain(r)
                rstd(RQ[:, 2 * i:2 * i + 2], GSS, 1.0 / width, EPSC).then_inc(l_rstd, 1)
                act.wait_ge(l_rstd, i + 1)

            def latent_high(ks, psum, bank0):
                act.wait_ge(l_psum, psum)
                for i, k in enumerate(ks):
                    act.activation(HT_h[:, k, :], C[:, bank0 + i // 2, 256 * (i % 2):256 * (i % 2) + 256], ACT.Copy,
                                   scale=vec(LATENT_GAIN[k])).then_inc(l_hi, 1)

            latent(0, CKV, 0, KVL, U_MLA + 1)
            hi_at(U_MLA + SLOTS)
            latent_high((3, 4), 1, 2)
            act.wait_ge(kp_psum, 1)
            act.activation(KPT, C[:, 3, 0:256], ACT.Copy).then_inc(kp_sb, 1)
            hi_at(U_MLA + 1 + SLOTS)
            latent(1, CQ, 2, QL, U_MLA + 3)
            latent_high((0, 1, 2), 2, 0)
            for q in range(2, 4):
                hi_at(U_MLA + q + SLOTS)
            act.wait_ge(unit_used, U_MLA + 5)
            act.activation(KNT, ACC[:].rearrange("p b (h s) -> p (b h) s", s=SEQ), ACT.Copy).then_inc(kn_sb, 1)
            hi_at(U_MLA + 4 + SLOTS)
            act.wait_ge(unit_used, U_MLA + 6)
            act.activation(VT, C[:].rearrange("p (t b) c -> p t (b c)", t=T), ACT.Copy).then_inc(v_sb, 1)
            hi_at(U_MLA + 5 + SLOTS)
            scale = float(NOPE + ROPE) ** -0.5
            for s in range(4 + HEADS + 2):
                if s < 4:
                    n = U_MLA + 6 + s
                    act.wait_ge(unit_used, n + 1)
                    act.activation(QNT[:, 2 * s:2 * s + 2, :].rearrange("p a b -> p (a b)"), ACC[:, 2 * (s % 2), :],
                                   ACT.Copy, scale=scale).then_inc(uq_nope, 1)
                if 1 <= s < 5:
                    act.wait_ge(qp_psum, s)
                    act.activation(QPT[:, s - 1, :], C[:, 0, 0:256], ACT.Copy, scale=scale).then_inc(qp_sb, 1)
                if 2 <= s < HEADS + 2:
                    att_exp(HEADS + s - 2)
                if 3 <= s < HEADS + 3:
                    att_pt(HEADS + s - 3)
                if 4 <= s < HEADS + 4:
                    att_out(HEADS + s - 4)
                if s < 4:
                    hi_at(n + SLOTS)
                if s in (8, 9):
                    hi_at(U_WO + s - 8 + SLOTS)
            finish_pair(U_FF2 - 1, 7, (ln, 2))
            feed_forward(2, U_FF2)
            ln(3)

        @block.vector
        def _(dve):
            own = [0]

            def chain(ins):
                own[0] += 1
                ins.then_inc(dve_self, 1)
                dve.wait_ge(dve_self, own[0])

            def low(n, slot, width=UNIT):
                dve.wait_ge(hi_ready, n + 1)
                dve.tensor_tensor(LO[:, slot, 0:width], RAW[:, slot, 0:width], HI[:, slot, 0:width].bitcast(f32),
                                  ALU.subtract).then_inc(lo_ready, 1)

            def low_at(n):
                if n < N_UNITS:
                    low(n, n % SLOTS, UNIT if units[n] is None else UNIT_K[n] * UNIT_C[n])

            def xt_low(e, t):
                dve.wait_ge(xt_hi, 2 * e + t + 1)
                s = slice(128 * t, 128 * t + 128)
                dve.tensor_tensor(XT_l[:, :, s], C[:, 2 * t:2 * t + 2, :].rearrange("p b (k s) -> p (b k) s", s=128),
                                  XT_h[:, :, s].bitcast(f32), ALU.subtract).then_inc(xt_lo, 1)

            gains = [0]

            def rms_apply(r, e=None):
                gains[0] += 1
                dve.wait_ge(gain_loaded, 16 * gains[0])
                dst, g = (XN0, GAIN0) if r == 0 else (XN, GAIN)
                for t in range(T):
                    dve.wait_ge(rstd_ready, 2 * r + t + 1)
                    dve.scalar_tensor_tensor(dst[:, t, :], X[:, t, :], RSTD[:, t:t + 1], g, ALU.mult,
                                             ALU.mult).then_inc(xn_ready, 1)
                    if e is not None:
                        xt_low(e, t)

            def finish_pair(last, e):
                for t in range(T):
                    xt_low(e, t)
                    low_at(last - 1 + t + SLOTS)

            def add_to_x(pair, last_unit):
                for t in range(T):
                    dve.wait_ge(tail, pair) if t == 0 else dve.wait_ge(unit_used, last_unit + 1)
                    dve.tensor_tensor(X[:, t, :], X[:, t, :], ACC[:, 2 * t:2 * t + 2, :].rearrange("p b c -> p (b c)"),
                                      ALU.add).then_inc(x_ready, 1)

            def layer_norm(j, pair, last_unit, e=None):
                gains[0] += 2
                for t in range(T):
                    x = X[:, t, :]
                    dve.wait_ge(tail, pair) if t == 0 else dve.wait_ge(unit_used, last_unit + 1)
                    if t == 1 and e is not None:
                        xt_low(e, 0)
                    chain(dve.scalar_tensor_tensor(x, x, ALPHA, ACC[:, 2 * t:2 * t + 2, :].rearrange("p b c -> p (b c)"),
                                                   ALU.mult, ALU.add))
                    dve.bn_stats(BN[:, t, 0:6], X[:, t, 0:512])
                    chain(dve.bn_stats(BN[:, t, 6:12], X[:, t, 512:1024]))
                    dve.bn_aggr(MVAR[:, t, :], BN[:, t, :]).then_inc(mv_ready, 1)
                    dve.wait_ge(mv_ready, 2 * j + t + 1)
                    dve.wait_ge(gain_loaded, 16 * gains[0])
                    chain(dve.scalar_tensor_tensor(x, x, MVAR[:, t, 0:1], GAIN, ALU.subtract, ALU.mult))
                    dve.wait_ge(rstd_ready, 6 + 2 * j + t + 1)
                    dve.scalar_tensor_tensor(x, x, RSTD[:, t:t + 1], BIAS, ALU.mult, ALU.add).then_inc(x_ready, 1)
                if e is not None:
                    xt_low(e, 1)
                    low_at(last_unit - 1 + SLOTS)
                    low_at(last_unit + SLOTS)

            def att_scores(j, table, slope):
                p, PROB = j % 2, PROBS[j // HEADS]
                dve.wait_ge(sc_psum, j + 1)
                if j >= 2:
                    dve.wait_ge(pt_psum, j - 1)
                chain(dve.scalar_tensor_tensor(PROB[:, p, :], table, slope, C[:, 1, 0:384], ALU.mult, ALU.add))
                dve.tensor_reduce(NMAX[:, p, 0:1], PROB[:, p, 0:128], AX.X, ALU.max, negate=True)
                dve.tensor_reduce(NMAX[:, p, 1:2], PROB[:, p, 128:384], AX.X, ALU.max, negate=True).then_inc(sc_max, 1)

            def att_inverse(j):
                p = j % 2
                dve.wait_ge(sc_exp, j + 1)
                chain(dve.reciprocal(RINV[:, p, :], RSUM[:, p, :]))
                if j == 0:
                    dve.wait_ge(g2_psum, GLA_H)
                if j >= 2:
                    dve.wait_ge(pt_psum, j - 1)
                for t in range(T):
                    r = dve.tensor_scalar(DIAGS[j // HEADS][p][:, t, :], IDENT, RINV[:, p, t:t + 1], None, ALU.mult)
                r.then_inc(diag_ready, 1)

            def att_low(j):
                dve.wait_ge(o_hi, j + 1)
                dve.tensor_tensor(OT_l[:, j % HEADS, :], C[:, 3, 0:SEQ], OT_h[:, j % HEADS, :].bitcast(f32),
                                  ALU.subtract).then_inc(o_lo, 1)

            def feed_forward(f, base):
                def square(c, par, half):
                    k = 4 * par + 2 * half
                    dve.wait_ge(ff_relu, c * 2 + (16 * f + half + 1))
                    dve.tensor_tensor(SQ[:, half, :], RELU[:, half, :], RELU[:, half, :], ALU.mult).then_inc(ff_sq, 1)
                    dve.wait_ge(ff_hi, c * 2 + (16 * f + half + 1))
                    dve.wait_ge(ff_sq, c * 2 + (16 * f + half + 1))
                    dve.tensor_tensor(HT_l[:, k:k + 2, :].rearrange("p a b -> p (a b)"), SQ[:, half, :],
                                      HT_h[:, k:k + 2, :].rearrange("p a b -> p (a b)").bitcast(f32),
                                      ALU.subtract).then_inc(ff_lo, 1)

                for half in range(2):
                    square(0, 0, half)
                    low_at(base + half + SLOTS)
                with dve.Fori(0, 3) as j:
                    for d in range(2):
                        for q in range(4):
                            if q < 2:
                                square(j * 2 + (d + 1), (d + 1) % 2, q)
                            n0 = base + 2 + q + SLOTS + 4 * d
                            low(j * 8 + n0, n0 % SLOTS)
                for q in range(4):
                    if q < 2:
                        square(7, 1, q)
                    low_at(base + 26 + q + SLOTS)

            rms_apply(0)
            low_at(0)
            for t in range(T):
                xt_low(0, t)
            dve.wait_ge(lr_split, 1)
            dve.tensor_tensor(LR_l[:], LR_RAW, LR_h[:].bitcast(f32), ALU.subtract).then_inc(lr_split, 1)
            for n in range(1, SLOTS):
                low_at(n)

            moba_blocks = [MQ[:, 0], MQ[:, 1], MK[:, 0], MK[:, 1]]

            def moba_norm(i):
                r = slice(8 * (i % 2), 8 * (i % 2) + 8)
                dve.wait_ge(m_sq, i + 1)
                dve.tensor_reduce(SSQ[:, r], MSQ.rearrange("p t (h d) -> p t h d", d=DH), AX.X, ALU.add).then_inc(m_ssq, 1)
                dve.wait_ge(m_rstd, i + 1)
                v = moba_blocks[i].rearrange("p t (h d) -> p t h d", d=DH)
                scales = RQ[:, r].rearrange("p (t h) -> p t h", t=T).unsqueeze(3).broadcast_to([128, T, 4, DH])
                dve.tensor_tensor(v, v, scales, ALU.mult).then_inc(m_norm, 1)

            for u in range(N_MIX):
                b = u // 2
                if u % 2 and b in (13, 15):
                    dve.wait_ge(unit_used, u + 1)
                    dve.wait_ge(sig_e, 3 if b == 13 else 4)
                    dve.tensor_tensor(Y0 if b == 13 else Y1, SG0, ACC[:, 2:4, :], ALU.mult).then_inc(y_ready, 1)
                if u in (37, 39):
                    y, s, p = (Y0, SG1, 0) if u == 37 else (Y1, SG0, 1)
                    dve.wait_ge(unit_used, u + 1)
                    dve.wait_ge(sig_e, 5 if u == 37 else 6)
                    chain(dve.tensor_tensor(s, s, ACC[:, 2 * p:2 * p + 2, :], ALU.mult))
                    dve.tensor_tensor(y, y, s, ALU.add).then_inc(y_ready, 1)
                if u in (38, 40):
                    k = 2 * (u - 38)
                    dve.wait_ge(xt_hi, 3 + (u - 38) // 2)
                    dve.tensor_tensor(XT_l[:, k:k + 4, :], C[:, k // 2:k // 2 + 2, :].rearrange("p b (k s) -> p (b k) s", s=SEQ),
                                      XT_h[:, k:k + 4, :].bitcast(f32), ALU.subtract).then_inc(xt_lo, 1)
                if u == 0:
                    dve.wait_ge(p_hi, 1)
                    dve.tensor_tensor(PT_l[:].rearrange("p a b -> p (a b)"), C[:, 3, :],
                                      PT_h[:].rearrange("p a b -> p (a b)").bitcast(f32), ALU.subtract).then_inc(p_lo, 1)
                if u == 1:
                    dve.wait_ge(z_l, 1)
                    dve.scalar_tensor_tensor(LA, C[:, 0:2, :], 0.0, LA, ALU.min, ALU.subtract).then_inc(la_ready, 1)
                if u == 4:
                    dve.wait_ge(cum_exp, 1)
                    dec = QD.rearrange("p h (n c) -> p h n c", c=GLA_CHUNK)[:, :, :, GLA_CHUNK - 1]
                    chain(dve.tensor_copy(DEC, dec))
                    dve.wait_ge(qt_psum, 1)
                    dve.scalar_tensor_tensor(QD, C[:, 2:4, :].rearrange("p b (h s) -> p (b h) s", s=SEQ),
                                             float(GLA_DK) ** -0.5, QD, ALU.mult, ALU.mult).then_inc(qd_ready, 1)
                if u == 5:
                    dve.wait_ge(kt_psum, 1)
                    dve.tensor_tensor(KDT, C[:, 0:2, :].rearrange("p b (h s) -> p (b h) s", s=SEQ), KDT,
                                      ALU.mult).then_inc(kd_ready, 1)
                    dve.tensor_tensor(GK, GK, LA, ALU.mult).then_inc(kd_ready, 1)
                for h in range(GLA_H):
                    if u == 10 + 2 * h:
                        dve.wait_ge(g1_psum, h + 1)
                        dve.wait_ge(const_set, 7)
                        dve.wait_ge(cst_loaded, 16)
                        for j in range(2):
                            q = slice(64 * j, 64 * j + 64)
                            dve.copy_predicated(AT[q, :, q], GLA_MASK[q, :, :],
                                                C[q, 1, 256:384].rearrange("p (t c) -> p t c", t=T))
                        dve.wait_ge(g1_s1, h + 1)
                        for n in (1, 2):
                            r = dve.scalar_tensor_tensor(S[:, n, :], S[:, n - 1, :], DEC[:, h, n:n + 1],
                                                         KV_of(n), ALU.mult, ALU.add)
                            if n == 1:
                                chain(r)
                        r.then_inc(g1_ready, 1)
                    if u == 11 + 2 * h:
                        dve.wait_ge(g2_rstd, h + 1)
                        dve.wait_ge(gr_ready, 1 + h // 2)
                        if h >= 1:
                            dve.wait_ge(g3_psum, h)
                        for t in range(T):
                            r = dve.scalar_tensor_tensor(OTOK[:, t, :], C[:, 2, 256 * t:256 * t + 256], GSS[:, t:t + 1],
                                                         GRt[:, t, GLA_DV * h:GLA_DV * h + GLA_DV], ALU.mult, ALU.mult)
                        r.then_inc(g2_ready, 1)
                    if u == 12 + 2 * h:
                        for j in range(2):
                            dve.wait_ge(g3_hi, 2 * h + 2)
                            dve.scalar_tensor_tensor(HT_l[:, 2 * h + j, :], C[:, 3, 256 * j:256 * j + 256],
                                                     vec(V_GLA + 2 * h + j), HT_h[:, 2 * h + j, :].bitcast(f32),
                                                     ALU.mult, ALU.subtract).then_inc(g3_lo, 1)
                if u in (14, 16, 18, 20):
                    moba_norm(u // 2 - 7)
                h = u - 22
                if 0 <= h < HEADS:
                    dve.wait_ge(m2_q, h + 1)
                    dve.tensor_scalar(QKT[:, h % 2, 256:512], C[:, 0, 256:512], vec(V_KN), float(DH) ** -0.5,
                                      ALU.mult, ALU.mult).then_inc(m2_k, 1)
                if 1 <= h < HEADS + 1:
                    att_scores(h - 1, DIST, 2.0 ** (-h))
                if 3 <= h < HEADS + 3:
                    att_low(h - 3)
                if 1 <= h < HEADS + 1:
                    att_inverse(h - 1)
                if u < N_MIX - 2:
                    low_at(u + SLOTS)
                if u in (9, 11):
                    dve.wait_ge(sig_e, b - 3)
                    g = GR[:, b - 4]
                    dve.tensor_tensor(g, g, ACC[:, 2 * (b % 2):2 * (b % 2) + 2, :], ALU.mult).then_inc(gr_ready, 1)

            add_to_x(1, U_FF0 - 1)
            rms_apply(1, 2)
            for half in range(2):
                low_at(U_FF0 - 2 + half + SLOTS)
            feed_forward(0, U_FF0)
            add_to_x(2, U_PLE - 1)
            rms_apply(2)
            finish_pair(U_PLE - 1, 3)
            for q in range(3):
                low_at(U_PLE + q + SLOTS)
            for t in range(T):
                dve.wait_ge(pg_sig, t + 1)
                s = SG[:, t, :]
                dve.wait_ge(ple_sb, 2)
                chain(dve.tensor_tensor(s, s, PLEO[:, t, :], ALU.mult))
                dve.tensor_tensor(X[:, t, :], X[:, t, :], s, ALU.add).then_inc(x_ready, 1)
            finish_pair(U_CONV - 1, 4)
            chain(dve.memset(Z[:, :, 0:2], 0.0))
            for q in range(12):
                n, pair, part = U_CONV + q, q // 3, q % 3
                dve.wait_ge(unit_used, n + 1)
                bank = C[:, q % 4, :].rearrange("p (a s) -> p a s", a=2)
                if part == 1:
                    dve.wait_ge(cv_c, pair + 1)
                    dve.tensor_tensor(Z[:, :, 2:258], bank, CS[:, pair % 2, :].rearrange("p (a s) -> p a s", a=2),
                                      ALU.mult).then_inc(cv_z, 1)
                    dve.wait_ge(cv_z, pair + 1)
                    if pair:
                        dve.wait_ge(cv_hi, pair)
                    for tap in (2, 1, 0):
                        for j in range(2):
                            w = vec(V_CONV + 8 * tap + 2 * pair + j)
                            z = Z[:, j, tap:tap + 256]
                            if tap == 2:
                                r = dve.tensor_scalar(VB[:, j, :], z, w, None, ALU.mult)
                            else:
                                r = dve.scalar_tensor_tensor(VB[:, j, :], z, w, VB[:, j, :], ALU.mult, ALU.add)
                        chain(r)
                low_at(n + SLOTS)
                if part == 2:
                    dve.tensor_tensor(VB, VB, bank, ALU.mult).then_inc(cv_v, 1)
                    dve.wait_ge(cv_v, pair + 1)
                    dve.wait_ge(cv_hi, pair + 1)
                    dve.tensor_tensor(OT_l[:, 2 * pair:2 * pair + 2, :], VB, OT_h[:, 2 * pair:2 * pair + 2, :].bitcast(f32),
                                      ALU.subtract).then_inc(cv_lo, 1)
            for q in range(2):
                low_at(U_CONVO + q + SLOTS)
            layer_norm(0, 5, U_FF1 - 1, 5)
            feed_forward(1, U_FF1)
            layer_norm(1, 6, U_MLA - 1, 6)

            def latent(i, dst, bank, width):
                dve.wait_ge(l_rstd, i + 1)
                for t in range(T):
                    dve.tensor_scalar(dst[:, t, :], ACC[:, bank + t, 0:width], RQ[:, 2 * i + t:2 * i + t + 1], None,
                                      ALU.mult).then_inc(l_norm, 1)

            def latent_low(ks, high, low_bank):
                for i, k in enumerate(ks):
                    dve.wait_ge(l_hi, high[i])
                    dve.scalar_tensor_tensor(HT_l[:, k, :], C[:, low_bank + i // 2, 256 * (i % 2):256 * (i % 2) + 256],
                                             vec(LATENT_GAIN[k]), HT_h[:, k, :].bitcast(f32), ALU.mult,
                                             ALU.subtract).then_inc(l_lo, 1)

            def rope(dst, x1, x2, cos, sin):
                shape = list(x1.shape)
                n = shape[1] * shape[2] * (shape[3] if len(shape) == 4 else 1)
                tmp = [RT[:, i, 0:n] for i in range(2)]
                if len(shape) == 4:
                    tmp = [v.rearrange("p (t h c) -> p t h c", h=shape[2], c=32) for v in tmp]
                    cos, sin = (v.unsqueeze(2).broadcast_to(shape) for v in (cos, sin))
                else:
                    tmp = [v.rearrange("p (t c) -> p t c", c=32) for v in tmp]
                for d, f1, f2, op in ((dst[0], cos, sin, ALU.subtract), (dst[1], sin, cos, ALU.add)):
                    dve.tensor_tensor(tmp[0], x1, f1, ALU.mult)
                    chain(dve.tensor_tensor(tmp[1], x2, f2, ALU.mult))
                    r = dve.tensor_tensor(d, tmp[0], tmp[1], op)
                    if d is dst[0]:
                        chain(r)
                return r

            latent(0, CKV, 0, KVL)
            kp = KPK.rearrange("p t (u c) -> p t u c", u=2)
            chain(rope((kp[:, :, 0, 0:32], kp[:, :, 0, 32:64]), ACC[:, 0:2, KVL:KVL + 32],
                       ACC[:, 0:2, KVL + 32:KVL + 64], COS, SIN))
            dve.tensor_copy(kp[:, :, 1, :], kp[:, :, 0, :]).then_inc(l_norm, 1)
            low_at(U_MLA + SLOTS)
            latent_low((3, 4), (2, 2), 2)
            low_at(U_MLA + 1 + SLOTS)
            latent(1, CQ, 2, QL)
            latent_low((0, 1, 2), (4, 4, 5), 0)
            for q in range(2, 6):
                low_at(U_MLA + q + SLOTS)
            for s in range(4 + HEADS + 2):
                if s < 4:
                    n = U_MLA + 6 + s
                    dve.wait_ge(unit_used, n + 1)
                    if s:
                        dve.wait_ge(uq_rope, s)
                    pe_part = ACC[:, 2 * (s % 2) + 1, 0:256].rearrange("p (t h c) -> p t h c", t=T, c=ROPE)
                    qp = QPK.rearrange("p t (g h c) -> p t g h c", h=2, c=ROPE)[:, :, s]
                    rope((qp[:, :, :, 0:32], qp[:, :, :, 32:64]), pe_part[:, :, :, 0:32], pe_part[:, :, :, 32:64], COS,
                         SIN).then_inc(uq_rope, 1)
                if 2 <= s < HEADS + 2:
                    att_scores(HEADS + s - 2, CHUNK_MASK, 1.0)
                if 4 <= s < HEADS + 4:
                    att_low(HEADS + s - 4)
                if 2 <= s < HEADS + 2:
                    att_inverse(HEADS + s - 2)
                if s < 4:
                    low_at(n + SLOTS)
                if s in (8, 9):
                    low_at(U_WO + s - 8 + SLOTS)
            layer_norm(2, 7, U_FF2 - 1, 7)
            feed_forward(2, U_FF2)
            layer_norm(3, 8, N_UNITS - 1)

        @block.tensor
        def _(pe):
            def three(dst, s_h, s_l, m_h, m_l, first, last):
                pe.matmul(dst, s_h, m_h, start=first, stop=False, skip_group_check=True)
                pe.matmul(dst, s_h, m_l, start=False, stop=False, skip_group_check=True)
                return pe.matmul(dst, s_l, m_h, start=False, stop=last, skip_group_check=True)

            def tokens_out(n, src_h, src_l, k0, bank, first, last, nk=4, width=512):
                slot = n % SLOTS
                pe.wait_ge(lo_ready, n + 1)
                for t in range(T):
                    s = slice(128 * t, 128 * t + 128)
                    for k in range(nk):
                        w = slice(k * width, k * width + width)
                        m = three(bank(t), src_h[:, k0 + k, s], src_l[:, k0 + k, s], HI[:, slot, w], LO[:, slot, w],
                                  first and k == 0, last and k == nk - 1)
                m.then_inc(unit_used, 1)

            def tokens_pair(ns, src_h, src_l, k0s, banks, first, last, inputs=None, ends_stage=False, width=512, nk=4):
                for t in range(T):
                    s = slice(128 * t, 128 * t + 128)
                    if inputs is not None:
                        inputs(t)
                    for i, n in enumerate(ns):
                        if t == 0:
                            pe.wait_ge(lo_ready, n + 1)
                        for k in range(nk):
                            w = slice(k * width, k * width + width)
                            m = three(banks(t, i), src_h[:, k0s[i] + k, s], src_l[:, k0s[i] + k, s],
                                      HI[:, n % SLOTS, w], LO[:, n % SLOTS, w], first[i] and k == 0,
                                      last[i] and k == nk - 1)
                        if t == 1:
                            m.then_inc(unit_used, 1)
                    if t == 0 and ends_stage:
                        m.then_inc(tail, 1)

            def last_four(base, src_h, src_l, ready):
                for c in range(2):
                    pe.wait_ge(*ready(0))
                    tokens_out(base + c, src_h, src_l, 0, lambda t: ACC[:, 2 * t + c, :], True, False)
                pe.wait_ge(*ready(1))
                tokens_pair((base + 2, base + 3), src_h, src_l, (4, 4), lambda t, i: ACC[:, 2 * t + i, :], (False, False),
                            (True, True), ends_stage=True)

            def features_out(n, slot, dst, src_h, src_l, k0=0, nk=KD, width=256, tiles=(0, 1), inc=True):
                pe.wait_ge(lo_ready, n + 1)
                for i, j in enumerate(tiles):
                    for k in range(nk):
                        w = slice(k * width + 128 * j, k * width + 128 * j + 128)
                        m = three(dst(i), HI[:, slot, w], LO[:, slot, w], src_h[:, k0 + k, :], src_l[:, k0 + k, :],
                                  k == 0, k == nk - 1)
                if inc:
                    m.then_inc(unit_used, 1)
                return m

            def transpose_x(e, src, ready, free=None, tiles=range(T)):
                for t in tiles:
                    pe.wait_ge(*ready(t))
                    if free is not None:
                        pe.wait_ge(*free(t))
                    for k in range(KD):
                        m = pe.transpose(C[:, 2 * t + k // 4, 128 * (k % 4):128 * (k % 4) + 128],
                                         src[:, t, 128 * k:128 * k + 128], IDENT)
                    m.then_inc(xt_psum, 1)

            def next_input(e, src, ready, t):
                transpose_x(e, src, lambda t: ready, tiles=(t,))
                pe.wait_ge(xt_lo, 2 * e + t + 1)

            def att_score(j, parts):
                if j:
                    pe.wait_ge(sc_max, j)
                for t in range(T):
                    dst = C[:, 1, 0:128] if t == 0 else C[:, 1, 128:384]
                    for i, (q, k) in enumerate(parts):
                        m = pe.matmul(dst, q[:, 128 * t:128 * t + 128], k[:, 0:128 * (t + 1)], start=(i == 0),
                                      stop=(i == len(parts) - 1), skip_group_check=True)
                m.then_inc(sc_psum, 1)

            def att_transpose(j):
                pe.wait_ge(diag_ready, j + 1)
                if j:
                    pe.wait_ge(pt_sb, j)
                for i in range(3):
                    m = pe.matmul(C[:, 2, 128 * i:128 * i + 128], PROBS[j // HEADS][:, j % 2, 128 * i:128 * i + 128],
                                  DIAGS[j // HEADS][j % 2][:, min(i, 1), :], start=True, stop=True, skip_group_check=True)
                m.then_inc(pt_psum, 1)

            def att_values(j, v, h):
                pe.wait_ge(pt_sb, j + 1)
                if j:
                    pe.wait_ge(o_lo, j)
                p = PRTS[j // HEADS][:, j % 2, :]
                pe.matmul(C[:, 3, 0:256], v[:, 0, 128 * h:128 * h + 128], p[:, 0:256], start=True, stop=False,
                          skip_group_check=True)
                pe.matmul(C[:, 3, 128:256], v[:, 1, 128 * h:128 * h + 128], p[:, 256:384], start=False, stop=True,
                          skip_group_check=True).then_inc(o_psum, 1)

            def feed_forward(f, base, e):
                pe.wait_ge(const_set, 8)
                for bank in range(4):
                    pe.matmul(ACC[:, bank, :], ZERO[:, 0:128], ZERO[:, 128:640], start=True, stop=False,
                              skip_group_check=True)

                def up(c, slot0, n0):
                    for half in range(2):
                        pe.wait_ge(ff_relu, c * 2 + (16 * f + half - 1))
                        features_out(n0 + half, (slot0 + half) % SLOTS, lambda i: C[:, half, 256 * i:256 * i + 256], XT_h, XT_l)

                def down(c, par, slot0, n0):
                    for half in range(2):
                        pe.wait_ge(ff_lo, c * 2 + (16 * f + 2))
                        pe.wait_ge(lo_ready, n0 + half + 1)
                        slot = (slot0 + half) % SLOTS
                        for t in range(T):
                            s = slice(128 * t, 128 * t + 128)
                            for k in range(4):
                                w = slice(512 * k, 512 * k + 512)
                                m = three(ACC[:, 2 * t + half, :], HT_h[:, 4 * par + k, s], HT_l[:, 4 * par + k, s],
                                          HI[:, slot, w], LO[:, slot, w], False, False)
                        m.then_inc(unit_used, 1)

                pe.wait_ge(xt_lo, 2 * e + 2)
                for half in range(2):
                    features_out(base + half, (base + half) % SLOTS, lambda i: C[:, half, 256 * i:256 * i + 256], XT_h, XT_l)
                with pe.Fori(0, 3) as j:
                    for d in range(2):
                        up(j * 2 + (d + 1), (base + 2) % SLOTS, j * 8 + (base + 2 + 4 * d))
                        down(j * 2 + d, d, (base + 4) % SLOTS, j * 8 + (base + 4 + 4 * d))
                up(7, (base + 26) % SLOTS, base + 26)
                down(6, 0, (base + 28) % SLOTS, base + 28)
                pe.wait_ge(ff_lo, 16 * f + 16)
                tokens_pair((base + 30, base + 31), HT_h, HT_l, (4, 4), lambda t, i: ACC[:, 2 * t + i, :], (False, False),
                            (True, True), ends_stage=True)

            pe.wait_ge(ident_loaded, 16)
            transpose_x(0, XN0, lambda t: (xn_ready, t + 1))
            pe.wait_ge(xt_lo, 2)

            for u in range(N_MIX):
                b = u // 2
                if u < 36:
                    if u % 2 == 0:
                        if b >= 2:
                            pe.wait_ge(*block_read(b - 2))
                    src_h, src_l = (HT_h, HT_l) if b in (13, 15) else (XT_h, XT_l)
                    if b == 13 and u % 2 == 0:
                        pe.wait_ge(g3_lo, 2 * GLA_H)
                    tokens_out(u, src_h, src_l, 4 * (u % 2), lambda t: ACC[:, 2 * (b % 2) + t, :], u % 2 == 0, u % 2 == 1)
                elif u < 40:
                    c, kh = (u - 36) // 2, (u - 36) % 2
                    pe.wait_ge(*block_read(16 + c))
                    pe.wait_ge(o_lo, HEADS)
                    tokens_out(u, OT_h, OT_l, 4 * kh, lambda t: ACC[:, 2 * c + t, :], kh == 0, kh == 1)
                elif u < 42:
                    pe.wait_ge(xt_lo, 3)
                    pe.wait_ge(y_ready, 4)
                    tokens_out(u, XT_h, XT_l, 0, lambda t: ACC[:, 2 * t + u - 40, :], True, False)
                elif u == 42:
                    pe.wait_ge(xt_lo, 4)
                    tokens_pair((42, 43), XT_h, XT_l, (4, 4), lambda t, i: ACC[:, 2 * t + i, :], (False, False),
                                (True, True), ends_stage=True)
                if u == 0:
                    pe.wait_ge(lr_split, 2)
                    for t in range(T):
                        s = slice(128 * t, 128 * t + 128)
                        for k in range(KD):
                            m = three(C[:, 0, GLA_RANK * t:GLA_RANK * t + GLA_RANK], XT_h[:, k, s], XT_l[:, k, s],
                                      LR_h[:, k, :], LR_l[:, k, :], k == 0, k == KD - 1)
                    m.then_inc(lr_psum, 1)
                    pe.wait_ge(rows_loaded, 16 * 6)
                    pe.transpose(C[:, 2, 0:N_VEC], ROWS, IDENT[0:N_VEC, 0:N_VEC]).then_inc(cols_psum, 1)
                    pe.wait_ge(p_loaded, 16)
                    for k in range(2):
                        for t in range(T):
                            m = pe.transpose(C[:, 3, 256 * k + 128 * t:256 * k + 128 * t + 128],
                                             P_RAW[:, t, 128 * k:128 * k + 128], IDENT)
                    m.then_inc(p_psum, 1)
                    pe.wait_ge(lr_sb, 1)
                    for t in range(T):
                        m = pe.transpose(C[0:GLA_RANK, 1, 128 * t:128 * t + 128], GLR[:, t, :], IDENT)
                    m.then_inc(lrt_psum, 1)
                if u == 1:
                    pe.wait_ge(lrt_sb, 1)
                    pe.wait_ge(w2_loaded, 32)
                    for t in range(T):
                        m = pe.matmul(C[:, t, :], GLRT[:, 128 * t:128 * t + 128], W2E, start=True, stop=True)
                    m.then_inc(z_psum, 1)
                if u == 3:
                    pe.wait_ge(la_ready, 1)
                    pe.wait_ge(cst_loaded, 16)
                    pe.wait_ge(cols_ready, 1)
                    pe.wait_ge(p_lo, 1)
                    for h in range(GLA_H):
                        for t in range(T):
                            pe.matmul(C[:, h // 2, 256 * (h % 2) + 128 * t:256 * (h % 2) + 128 * t + 128],
                                      LA[:, t, 128 * h:128 * h + 128], TRI, start=True, stop=True, skip_group_check=True)
                    for t in range(T):
                        m = pe.matmul(C[:, 2 + t, :], REM, LA[:, t, :], start=True, stop=True)
                    m.then_inc(cum_psum, 1)
                for at, src, bank, done, before in ((4, GQ, 2, qt_psum, 1), (5, GK, 0, kt_psum, 2)):
                    if u == at:
                        pe.wait_ge(blk_sb, before)
                        pe.wait_ge(cum_exp, 1)
                        for h in range(GLA_H):
                            for t in range(T):
                                m = pe.transpose(C[:, bank + h // 2, 256 * (h % 2) + 128 * t:256 * (h % 2) + 128 * t + 128],
                                                 src[:, t, 128 * h:128 * h + 128], IDENT)
                        m.then_inc(done, 1)
                for h in range(GLA_H):
                    if u == 10 + 2 * h:
                        pe.wait_ge(kd_ready, 2)
                        pe.wait_ge(qd_ready, 1)
                        pe.wait_ge(blk_sb, 3 + h // 2)
                        if h:
                            pe.wait_ge(g1_ready, h)
                        for n in range(4):
                            t, j = n // 2, n % 2
                            c = slice(GLA_CHUNK * n, GLA_CHUNK * n + GLA_CHUNK)
                            pe.matmul(C[64 * j:64 * j + 64, 1, 256 + 64 * t:256 + 64 * t + 64], KDT[:, h, c], QD[:, h, c],
                                      start=True, stop=True, skip_group_check=True)
                        for n in (0, 2, 1):
                            t, q = n // 2, slice(64 * (n % 2), 64 * (n % 2) + 64)
                            m = pe.matmul(KV_of(n), GK[q, t, 128 * h:128 * h + 128],
                                          GV_head(q, h, t), start=True, stop=True, skip_group_check=True)
                        m.then_inc(g1_psum, 1)
                    if u == 11 + 2 * h:
                        pe.wait_ge(g1_ready, h + 1)
                        if h:
                            pe.wait_ge(g2_ready, h)
                        for t in range(T):
                            dst = slice(256 * t, 256 * t + 256)
                            m = pe.matmul(C[:, 2, dst], AT[:, t, :], GV_head(slice(0, 128), h, t), start=True, stop=False,
                                          skip_group_check=True)
                            for n in range(max(1, 2 * t), 2 * t + 2):
                                j = n % 2
                                m = pe.matmul(C[64 * j:64 * j + 64, 2, dst], QD[:, h, 64 * n:64 * n + 64], S[:, n - 1, :],
                                              start=False, stop=(j == 1), skip_group_check=True)
                        m.then_inc(g2_psum, 1)
                    if u == 12 + 2 * h:
                        pe.wait_ge(g2_ready, h + 1)
                        if h:
                            pe.wait_ge(g3_lo, 2 * h)
                        for j in range(2):
                            for t in range(T):
                                m = pe.transpose(C[:, 3, 256 * j + 128 * t:256 * j + 128 * t + 128],
                                                 OTOK[:, t, 128 * j:128 * j + 128], IDENT)
                        m.then_inc(g3_psum, 1)
                h = u - 22
                if 0 <= h < HEADS:
                    if h == 0:
                        pe.wait_ge(m_norm, 4)
                        pe.wait_ge(g3_lo, 2 * GLA_H)
                    else:
                        pe.wait_ge(m2_k, h)
                        pe.wait_ge(m2_q, h)
                    for i, src in enumerate((MQ, MK)):
                        for t in range(T):
                            m = pe.transpose(C[:, 0, 256 * i + 128 * t:256 * i + 128 * t + 128],
                                             src[:, h // 4, t, 128 * (h % 4):128 * (h % 4) + 128], IDENT)
                    m.then_inc(m2_psum, 1)
                if 1 <= h < HEADS + 1:
                    j = h - 1
                    pe.wait_ge(m2_q, j + 1)
                    pe.wait_ge(m2_k, j + 1)
                    att_score(j, [(QKT[:, j % 2, 0:256], QKT[:, j % 2, 256:512])])
                if 2 <= h < HEADS + 2:
                    att_transpose(h - 2)
                if 3 <= h < HEADS + 3:
                    j = h - 3
                    pe.wait_ge(blk_sb, 9 + j // 4)
                    att_values(j, MVt, j)
                if u in (38, 40):
                    y, k0 = (Y0, 0) if u == 38 else (Y1, 4)
                    pe.wait_ge(y_ready, 3 if u == 38 else 4)
                    for k in range(4):
                        for t in range(T):
                            m = pe.transpose(C[:, (k0 + k) // 2, 256 * (k % 2) + 128 * t:256 * (k % 2) + 128 * t + 128],
                                             y[:, t, 128 * k:128 * k + 128], IDENT)
                    m.then_inc(xt_psum, 1)

            transpose_x(2, XN, lambda t: (xn_ready, 2 + t + 1))
            feed_forward(0, U_FF0, 2)
            pe.wait_ge(lo_ready, U_PLE + 1)
            for t in range(T):
                s = slice(128 * t, 128 * t + 128)
                for c in range(2):
                    for k in range(2):
                        w = slice(1024 * k + 512 * c, 1024 * k + 512 * c + 512)
                        m = three(C[:, 2 * t + c, :], PT_h[:, k, s], PT_l[:, k, s], HI[:, U_PLE % SLOTS, w],
                                  LO[:, U_PLE % SLOTS, w], k == 0, k == 1)
                m.then_inc(unit_used if t else tail, 1)

            def gate_input(t):
                pe.wait_ge(ple_sb, t + 1)
                next_input(3, XN, (xn_ready, 4 + t + 1), t)

            tokens_pair((U_PLE + 1, U_PLE + 2), XT_h, XT_l, (0, 0), lambda t, i: ACC[:, 2 * t + i, :], (True, True),
                        (False, False), inputs=gate_input)
            tokens_pair((U_PLE + 3, U_PLE + 4), XT_h, XT_l, (4, 4), lambda t, i: ACC[:, 2 * t + i, :], (False, False),
                        (True, True), ends_stage=True)
            transpose_x(4, X, lambda t: (x_ready, 4 + t + 1))
            pe.wait_ge(xt_lo, 10)
            for q in range(12):
                n, pair, part = U_CONV + q, q // 3, q % 3
                if q >= 4:
                    old, opart = (q - 4) // 3, (q - 4) % 3
                    pe.wait_ge((cv_c, cv_z, cv_v)[opart], old + 1)
                features_out(n, n % SLOTS, lambda i: C[:, q % 4, 256 * i:256 * i + 256], XT_h, XT_l)
            last_four(U_CONVO, OT_h, OT_l, lambda kh: (cv_lo, 2 * kh + 2))
            transpose_x(5, X, lambda t: (x_ready, 6 + t + 1), lambda t: (cv_v, 4))
            feed_forward(1, U_FF1, 5)

            tokens_pair((U_MLA, U_MLA + 1), XT_h, XT_l, (0, 4), lambda t, i: ACC[:, t, 0:KVL + ROPE], (True, False),
                        (False, True), inputs=lambda t: next_input(6, X, (x_ready, 8 + t + 1), t), width=KVL + ROPE)
            for k in range(2):
                tokens_out(U_MLA + 2 + k, XT_h, XT_l, 4 * k, lambda t: ACC[:, 2 + t, 0:QL], k == 0, k == 1, width=QL)
                if k == 0:
                    pe.wait_ge(l_norm, 3)
                    for i in range(2):
                        for t in range(T):
                            m = pe.transpose(C[:, 2, 256 * i + 128 * t:256 * i + 128 * t + 128],
                                             CKV[:, t, 128 * i:128 * i + 128], IDENT)
                    m.then_inc(l_psum, 1)
                    for t in range(T):
                        m = pe.transpose(C[:, 3, 128 * t:128 * t + 128], KPK[:, t, :], IDENT)
                    m.then_inc(kp_psum, 1)

            def latent_q():
                pe.wait_ge(l_norm, 5)
                for k in range(3):
                    for t in range(T):
                        m = pe.transpose(C[:, k // 2, 256 * (k % 2) + 128 * t:256 * (k % 2) + 128 * t + 128],
                                         CQ[:, t, 128 * k:128 * k + 128], IDENT)
                m.then_inc(l_psum, 1)

            pe.wait_ge(l_lo, 2)
            for g in range(4):
                if g == 2:
                    latent_q()
                features_out(U_MLA + 4, (U_MLA + 4) % SLOTS, lambda i: ACC[:, g, 256 * i:256 * i + 256], HT_h, HT_l, k0=3,
                             nk=2, width=1024, tiles=(2 * g, 2 * g + 1), inc=(g == 3))
            n = U_MLA + 5
            pe.wait_ge(kp_sb, 1)
            pe.wait_ge(lo_ready, n + 1)
            for t in (1, 0):
                if t == 0:
                    pe.wait_ge(l_lo, 5)
                s = slice(128 * t, 128 * t + 128)
                for c in range(2):
                    for k in range(2):
                        w = slice(1024 * k + 512 * c, 1024 * k + 512 * c + 512)
                        m = three(C[:, 2 * t + c, :], HT_h[:, 3 + k, s], HT_l[:, 3 + k, s], HI[:, n % SLOTS, w],
                                  LO[:, n % SLOTS, w], k == 0, k == 1)
            m.then_inc(unit_used, 1)

            def project_q(q):
                n = U_MLA + 6 + q
                slot = n % SLOTS
                if q < 2:
                    pe.wait_ge(kn_sb, 1)
                else:
                    pe.wait_ge(uq_nope, q - 1)
                    pe.wait_ge(uq_rope, q - 1)
                pe.wait_ge(lo_ready, n + 1)
                nope, rot = ACC[:, 2 * (q % 2), :], ACC[:, 2 * (q % 2) + 1, :]
                for i in range(2):
                    for k in range(3):
                        w = slice(384 * k + 192 * i, 384 * k + 192 * i + 128)
                        three(nope[:, 256 * i:256 * i + 256], HI[:, slot, w], LO[:, slot, w], HT_h[:, k, :], HT_l[:, k, :],
                              k == 0, k == 2)
                for t in range(T):
                    s = slice(128 * t, 128 * t + 128)
                    for k in range(3):
                        hi_w, lo_w = (W[:, slot, 384 * k:384 * k + 384].rearrange("p (h c) -> p h c", c=192)[:, :, 128:192]
                                      for W in (HI, LO))
                        m = three(rot[:, 128 * t:128 * t + 128], HT_h[:, k, s], HT_l[:, k, s], hi_w, lo_w, k == 0, k == 2)
                m.then_inc(unit_used, 1)

            def rope_transpose(q):
                pe.wait_ge(uq_rope, q + 1)
                pe.wait_ge(v_sb, 1)
                if q:
                    pe.wait_ge(qp_sb, q)
                for t in range(T):
                    m = pe.transpose(C[:, 0, 128 * t:128 * t + 128], QPK[:, t, 128 * q:128 * q + 128], IDENT)
                m.then_inc(qp_psum, 1)

            for s in range(4 + HEADS + 2):
                if s < 4:
                    project_q(s)
                if 1 <= s < 5:
                    rope_transpose(s - 1)
                h = s - 2
                if 0 <= h < HEADS:
                    pe.wait_ge(qp_sb, h // 2 + 1)
                    pe.wait_ge(uq_nope, h // 2 + 1)
                    r = slice(ROPE * (h % 2), ROPE * (h % 2) + ROPE)
                    att_score(HEADS + h, [(QNT[:, h, :], KNT[:, h, :]), (QPT[r, h // 2, :], KPT[r, :])])
                if 1 <= h < HEADS + 1:
                    att_transpose(HEADS + h - 1)
                if 2 <= h < HEADS + 2:
                    att_values(HEADS + h - 2, VT, h - 2)
                if s in (8, 9):
                    pe.wait_ge(o_lo, HEADS + 4)
                    pe.wait_ge(uq_rope, 4)
                    tokens_out(U_WO + s - 8, OT_h, OT_l, 0, lambda t: ACC[:, 2 * t + s - 8, :], True, False)
            pe.wait_ge(o_lo, 2 * HEADS)
            tokens_pair((U_WO + 2, U_WO + 3), OT_h, OT_l, (4, 4), lambda t, i: ACC[:, 2 * t + i, :], (False, False),
                        (True, True), ends_stage=True)
            transpose_x(7, X, lambda t: (x_ready, 10 + t + 1))
            feed_forward(2, U_FF2, 7)


_INS = ["x", "p", "norm_mix", "w_in", "gla_gate_w2", "gla_gate_b", "gla_out_norm", "moba_q_norm", "moba_k_norm",
        "w_branch_a", "w_branch_b", "w_out", "norm_mlp", "w_up", "w_down", "norm_ple", "w_ple_gate", "w_ple",
        "sc_w_in_2", "sc_conv_w_2", "sc_w_out_2", "mla_w_dq_2", "mla_g_q_2", "mla_w_uq_2", "mla_w_dkv_2",
        "mla_g_kv_2", "mla_w_uk_2", "mla_w_uv_2", "mla_w_o_2", "ff_w1_2", "ff_w2_2", "ln_mix_g_2", "ln_mix_b_2",
        "ln_ff_g_2", "ln_ff_b_2"]


def _constants(np):
    c = np.zeros((128, N_CONST), np.float32)
    i, j = np.arange(128)[:, None], np.arange(128)[None, :]
    same = i // GLA_CHUNK == j // GLA_CHUNK
    c[:, C_ID:C_ID + 128] = i == j
    c[:, C_TRI:C_TRI + 128] = (same & (i <= j)) / 16.0
    c[:, C_REM:C_REM + 128] = (same & (i > j)) / 16.0
    for o, tq, tk in ((0, 0, 0), (128, 1, 0), (256, 1, 1)):
        q, k = 128 * tq + i, 128 * tk + j
        c[:, C_DIST + o:C_DIST + o + 128] = np.where(q >= k, k - q, MASKED)
        c[:, C_CHM + o:C_CHM + o + 128] = np.where(k // 64 <= q // 64, 0.0, MASKED)
    freq = np.float32(10000.0) ** (-np.arange(0, ROPE, 2, dtype=np.float32) / np.float32(ROPE))
    ang = (np.arange(SEQ, dtype=np.float32)[:, None] * freq[None, :].astype(np.float32)).astype(np.float32)
    for o, f in ((C_COS, np.cos), (C_SIN, np.sin)):
        c[:, o:o + 64] = f(ang).astype(np.float32).reshape(T, 128, 32).transpose(1, 0, 2).reshape(128, 64)
    mask = (np.arange(128)[:, None] % 64 <= np.arange(64)[None, :]).astype(np.float32)
    c[:, C_GM:C_GM + 128] = np.concatenate([mask, mask], axis=1)
    return c


def kernel(**inputs):
    import numpy as _np
    import concourse.bacc as _bacc
    from concourse import mybir as _mybir
    from concourse.bass_utils import run_bass_kernel_spmd as _run

    nc = _bacc.Bacc("TRN2", target_bir_lowering=False, num_devices=1)
    arrays, args = {}, {}
    for name in _INS + ["consts"]:
        v = _constants(_np) if name == "consts" else _np.ascontiguousarray(inputs[name])
        arrays[f"in_{name}"] = v
        args[name] = nc.dram_tensor(f"in_{name}", v.shape, _mybir.dt.from_np(v.dtype), kind="ExternalInput").ap()
    out = nc.dram_tensor("out", (1, SEQ, D), _mybir.dt.float32, kind="ExternalOutput").ap()
    program(nc, args, out)
    r = _run(nc, [arrays], core_ids=[0])
    return r.results[0]["out"]
```

```python
import concourse.bass as bass
from concourse import mybir
from contextlib import ExitStack

SEQ, D, D_FF = 256, 1024, 4096
T = SEQ // 128
KD = D // 128
GLA_H, GLA_DK, GLA_DV, GLA_RANK, GLA_CHUNK = 4, 128, 256, 16, 64
HEADS, DH = 8, 128
PLE = 256
QL, KVL, NOPE, ROPE = 384, 256, 128, 64
CONV = 3
EPS, LN_EPS = 1e-6, 1e-5
ALPHA = 4.0 ** 0.25
MASKED = -1e30

O_GQ, O_GK, O_GV, O_LR, O_GR = 0, 512, 1024, 2048, 2064
O_MQ, O_MK, O_MV, O_GA, O_GB = 3088, 4112, 5136, 6160, 7184

UNIT, SLOTS = 2048, 4
N_MIX = 44
N_FF = 32
U_FF0 = N_MIX
U_PLE = U_FF0 + N_FF
U_CONV = U_PLE + 5
U_CONVO = U_CONV + 12
U_FF1 = U_CONVO + 4
U_MLA = U_FF1 + N_FF
U_WO = U_MLA + 10
U_FF2 = U_WO + 4
N_UNITS = U_FF2 + N_FF

C_ID, C_TRI, C_REM, C_DIST, C_CHM = 0, 128, 256, 384, 768
C_COS, C_SIN, C_GM = 1152, 1216, 1280
N_CONST = 1408
V_CONV, V_GLA, V_QN, V_KN, V_GQ, V_GKV, N_VEC = 0, 24, 32, 33, 34, 37, 39


def program(nc, a, out):
    f32, f32r, bf16, i32 = mybir.dt.float32, mybir.dt.float32r, mybir.dt.bfloat16, mybir.dt.int32
    ALU, ACT, AX = mybir.AluOpType, mybir.ActivationFunctionType, mybir.AxisListType
    ctx = ExitStack()

    def rows4(w, k0, c0, width, nk=4):
        return w[k0:k0 + nk * 128, c0:c0 + width].rearrange("(k p) c -> p k c", p=128)

    w_in, w_a, w_b, w_o = a["w_in"][0], a["w_branch_a"][0], a["w_branch_b"][0], a["w_out"][0]
    two = lambda w, c: [rows4(w, 0, c, 512), rows4(w, 512, c, 512)]
    four = lambda w: [rows4(w, 0, 0, 512), rows4(w, 0, 512, 512), rows4(w, 512, 0, 512), rows4(w, 512, 512, 512)]
    mix_cols = [O_GQ, O_GK, O_GV, O_GV + 512, O_GR, O_GR + 512, O_MQ, O_MQ + 512, O_MK, O_MK + 512, O_MV, O_MV + 512]
    units = []
    for c in mix_cols:
        units += two(w_in, c)
    units += two(w_in, O_GA) + two(w_a, 0) + two(w_in, O_GA + 512) + two(w_a, 512)
    units += two(w_in, O_GB) + two(w_in, O_GB + 512) + two(w_b, 0) + two(w_b, 512) + four(w_o)
    assert len(units) == N_MIX

    def up_unit(w, chunk, half):
        col = chunk * 512 + half * 256
        return w[:, bass.ds(col, 256)].rearrange("(k p) c -> p k c", p=128)

    def down_unit(w, chunk, half):
        return w[bass.ds(chunk * 512, 512), 512 * half:512 * half + 512].rearrange("(k p) c -> p k c", p=128)

    ffs = [(U_FF0, a["w_up"][0], a["w_down"][0]), (U_FF1, a["ff_w1_2"][0], a["ff_w2_2"][0]),
           (U_FF2, a["ff_w1_2"][1], a["ff_w2_2"][1])]
    units += [None] * N_FF
    units += [rows4(a["w_ple"][0], 0, 0, 1024, nk=2)] + four(a["w_ple_gate"][0])
    for pair in range(KD // 2):
        for part in (1, 2, 0):
            col = part * D + pair * 256
            units.append(a["sc_w_in_2"][0][:, col:col + 256].rearrange("(k p) c -> p k c", p=128))
    units += four(a["sc_w_out_2"][0]) + [None] * N_FF
    units += [rows4(a["mla_w_dkv_2"][0], 512 * k, 0, KVL + ROPE) for k in range(2)]
    units += [rows4(a["mla_w_dq_2"][0], 512 * k, 0, QL) for k in range(2)]
    units += [a[n][0].rearrange("(k p) h d -> p k (h d)", p=128) for n in ("mla_w_uk_2", "mla_w_uv_2")]
    units += [rows4(a["mla_w_uq_2"][0], 0, 384 * q, 384, nk=3) for q in range(4)]
    units += four(a["mla_w_o_2"][0]) + [None] * N_FF
    assert len(units) == N_UNITS
    UNIT_K = [None if u is None else u.shape[1] for u in units]
    UNIT_C = [None if u is None else u.shape[2] for u in units]

    with ctx:
        def sb(name, cols, dt=f32, rows=128):
            return ctx.enter_context(nc.sbuf_tensor(name, [rows] + list(cols), dt))

        def sem(name):
            return ctx.enter_context(nc.semaphore(name))

        RAW = sb("RAW", [SLOTS, UNIT])
        HI = sb("HI", [SLOTS, UNIT], f32r)
        LO = sb("LO", [SLOTS, UNIT], f32r)
        X = sb("X", [T, D])
        XT_h = sb("XT_h", [KD, SEQ], f32r)
        XT_l = sb("XT_l", [KD, SEQ], f32r)
        HT_h = sb("HT_h", [KD, SEQ], f32r)
        HT_l = sb("HT_l", [KD, SEQ], f32r)
        PT_h = sb("PT_h", [PLE // 128, SEQ], f32r)
        PT_l = sb("PT_l", [PLE // 128, SEQ], f32r)
        LR_h = sb("LR_h", [KD, GLA_RANK], f32r)
        LR_l = sb("LR_l", [KD, GLA_RANK], f32r)
        CST = sb("CST", [N_CONST])
        COLS = sb("COLS", [N_VEC + 1])
        ST = sb("ST", [160])
        R = sb("R", [11264])
        overlay = ExitStack()
        with overlay:
            G = overlay.enter_context(nc.sbuf_tensor("G", [128, 4096], f32))
        OT_h = sb("OT_h", [KD, SEQ], f32r)
        OT_l = sb("OT_l", [KD, SEQ], f32r)
        ACC = ctx.enter_context(nc.psum_tensor("ACC", [128, 4, 512], f32))
        C = ctx.enter_context(nc.psum_tensor("C", [128, 4, 512], f32))

        def cut(base, lo_, *dims):
            n = 1
            for d in dims:
                n *= d
            v = base[:, lo_:lo_ + n]
            if len(dims) == 2:
                v = v.rearrange("p (a b) -> p a b", b=dims[1])
            if len(dims) == 3:
                v = v.rearrange("p (a b c) -> p a b c", b=dims[1], c=dims[2])
            return v

        IDENT = CST[:, C_ID:C_ID + 128]
        TRI = CST[:, C_TRI:C_TRI + 128]
        REM = CST[:, C_REM:C_REM + 128]
        DIST = CST[:, C_DIST:C_DIST + 384]
        CHUNK_MASK = CST[:, C_CHM:C_CHM + 384]
        COS = cut(CST, C_COS, T, 32)
        SIN = cut(CST, C_SIN, T, 32)
        GLA_MASK = cut(CST, C_GM, T, 64).bitcast(i32)
        vec = lambda i: COLS[:, i:i + 1]
        GQ, LA, GK, GV = cut(R, 0, T, 512), cut(R, 1024, T, 512), cut(R, 2048, T, 512), cut(R, 3072, T, 2, 512)
        GR, MQ = cut(R, 5120, T, 2, 512), cut(R, 0, T, 2, 512)
        GV, GR, MQ = (v.rearrange("p t b c -> p b t c") for v in (GV, GR, MQ))
        MK = cut(R, 7168, T, 2, 512).rearrange("p t b c -> p b t c")
        MV = cut(R, 3072, T, 2, 512).rearrange("p t b c -> p b t c")
        flat = lambda o: cut(R, o, T, 1024)
        GVt, GRt, MQt, MKt, MVt = flat(3072), flat(5120), flat(0), flat(7168), flat(3072)
        QKT = cut(R, 2048, 2, 512)
        PRTS = (cut(R, 5888, 2, 384), cut(R, 9472, 2, 256 + 128))
        MLA_PROBS = (R[:, 8704:9088], R[:, 9088:9472], DIST)
        MLA_DIAGS = (cut(R, 8448, 2, 128), cut(R, 10496, 2, 128), cut(CST, C_TRI, 2, 128))

        def depth(j):
            return 2 if j < HEADS else 3

        def prob(j):
            if j < HEADS:
                return R[:, 5120 + 384 * (j % 2):5504 + 384 * (j % 2)]
            return MLA_PROBS[(j - HEADS) % 3]

        def diag(j):
            if j < HEADS:
                return cut(R, 6656 + 256 * (j % 2), 2, 128)
            return MLA_DIAGS[(j - HEADS) % 3]

        SG0, Y0, Y1, SG1 = cut(R, 9216, T, 512), cut(R, 10240, T, 512), cut(R, 0, T, 512), cut(R, 1024, T, 512)
        MSQ = cut(R, 9216, T, 512)
        W2E, GLRT = R[0:33, 9216:9728], R[0:33, 9728:9984]
        GLR, LR_RAW = cut(R, 9984, T, GLA_RANK), cut(R, 10016, KD, GLA_RANK)
        QD, KDT, AT = cut(G, 0, GLA_H, SEQ), cut(G, 1024, GLA_H, SEQ), cut(G, 2048, T, 128)
        S = cut(G, 2304, 3, GLA_DV)
        OTOK = cut(G, 3072, T, GLA_DV)
        SQJ = cut(G, 3584, T, GLA_DV)
        RELU, SQ, XN = cut(R, 0, 2, 512), cut(R, 1024, 2, 512), cut(R, 2048, T, D)
        GAIN, BIAS, PLEO, SG = R[:, 4096:5120], R[:, 5120:6144], cut(R, 6144, T, D), cut(R, 8192, T, D)
        ZERO = R[:, 10880:11200].bitcast(bf16)
        CS, VB = cut(R, 0, 2, 512), cut(R, 1024, 2, 256)
        Z = cut(R, 1536, 2, 258)
        P_RAW, ROWS, XN0, GAIN0 = cut(R, 7168, T, PLE), R[0:N_VEC, 7680:7808], cut(R, 2048, T, D), R[:, 4096:5120]
        QNT, KNT, VT = cut(R, 0, HEADS, SEQ), cut(R, 2048, HEADS, SEQ), cut(R, 4096, T, D)
        QPT, QPK = cut(R, 6144, 4, SEQ), cut(R, 7168, T, HEADS * ROPE)
        KPT, KPK = R[:, 8192:8448], cut(R, 8448, T, 2 * ROPE)
        CQ, CKV = cut(R, 8704, T, QL), cut(R, 9472, T, KVL)
        RT = cut(R, 9984, 2, 256)

        LATENT_GAIN = (V_GQ, V_GQ + 1, V_GQ + 2, V_GKV, V_GKV + 1)

        RSTD, SS, MVAR = ST[:, 0:2], ST[:, 2:4], cut(ST, 4, T, 2)
        BN = cut(ST, 8, T, 12)
        EPSC, LNEPSC, ONEC = ST[:, 32:33], ST[:, 33:34], ST[:, 34:35]
        NMAX, RSUM, RINV = cut(ST, 36, 2, 2), cut(ST, 40, 2, 2), cut(ST, 44, 2, 2)
        SSQ, RQ = ST[:, 48:64], ST[:, 64:80]
        DEC = cut(ST, 80, GLA_H, 4)
        GSS = ST[:, 96:98]

        raw_ready = [sem(f"raw_ready{s}") for s in range(SLOTS)]
        hi_ready, lo_ready = sem("hi_ready"), sem("lo_ready")
        unit_used = sem("unit_used")
        tail = sem("tail")
        x_loaded, cst_loaded, rows_loaded, p_loaded = [sem("x_loaded0"), sem("x_loaded1")], sem("cst_loaded"), sem("rows_loaded"), sem("p_loaded")
        ident_loaded = sem("ident_loaded")
        lr_loaded, w2_loaded, gain_loaded = sem("lr_loaded"), sem("w2_loaded"), sem("gain_loaded")
        const_set = sem("const_set")
        act_self, dve_self = sem("act_self"), sem("dve_self")
        root_ready, xn_ready = sem("root_ready"), sem("xn_ready")
        xt_psum, xt_hi, xt_lo = sem("xt_psum"), sem("xt_hi"), sem("xt_lo")
        x_ready, mv_ready = sem("x_ready"), sem("mv_ready")
        cols_psum, cols_ready = sem("cols_psum"), sem("cols_ready")
        p_psum, p_hi, p_lo = sem("p_psum"), sem("p_hi"), sem("p_lo")
        lr_split, lr_psum, lr_sb, lrt_psum, lrt_sb = (sem("lr_split"), sem("lr_psum"), sem("lr_sb"),
                                                      sem("lrt_psum"), sem("lrt_sb"))
        z_psum, z_l, la_ready = sem("z_psum"), sem("z_l"), sem("la_ready")
        blk_sb = sem("blk_sb")
        cum_psum, cum_exp = sem("cum_psum"), sem("cum_exp")
        qt_psum, qd_ready, kt_psum, kd_ready = sem("qt_psum"), sem("qd_ready"), sem("kt_psum"), sem("kd_ready")
        g1_psum, g1_s1, g1_ready = sem("g1_psum"), sem("g1_s1"), sem("g1_ready")
        g2_psum, g2_root, g2_ready = sem("g2_psum"), sem("g2_root"), sem("g2_ready")
        g3_psum, g3_hi, g3_lo = sem("g3_psum"), sem("g3_hi"), sem("g3_lo")
        sig_e, gr_ready = sem("sig_e"), sem("gr_ready")
        m_sq, m_ssq, m_root, m_norm = sem("m_sq"), sem("m_ssq"), sem("m_root"), sem("m_norm")
        m2_psum, m2_q, m2_k = sem("m2_psum"), sem("m2_q"), sem("m2_k")
        sc_read = sem("sc_read")
        sc_psum, sc_max, sc_exp, diag_ready = sem("sc_psum"), sem("sc_max"), sem("sc_exp"), sem("diag_ready")
        pt_psum, pt_sb, o_psum, o_hi, o_lo = sem("pt_psum"), sem("pt_sb"), sem("o_psum"), sem("o_hi"), sem("o_lo")
        y_ready = sem("y_ready")
        ff_relu, ff_sq, ff_hi, ff_lo = sem("ff_relu"), sem("ff_sq"), sem("ff_hi"), sem("ff_lo")
        ple_sb, pg_sig = sem("ple_sb"), sem("pg_sig")
        cv_c, cv_z, cv_v, cv_hi, cv_lo = sem("cv_c"), sem("cv_z"), sem("cv_v"), sem("cv_hi"), sem("cv_lo")
        l_root, l_norm, l_psum, l_hi, l_lo = sem("l_root"), sem("l_norm"), sem("l_psum"), sem("l_hi"), sem("l_lo")
        kp_psum, kp_sb = sem("kp_psum"), sem("kp_sb")
        kn_sb, v_sb, uq_nope, uq_rope, qp_psum, qp_sb = (sem("kn_sb"), sem("v_sb"), sem("uq_nope"), sem("uq_rope"),
                                                         sem("qp_psum"), sem("qp_sb"))
        stored = sem("stored")

        def block_read(b):
            if b in (4, 5):
                return gr_ready, b - 3
            if b in (13, 15):
                return y_ready, (b - 11) // 2
            if b >= 12:
                return sig_e, {12: 3, 14: 4, 16: 5, 17: 6}[b]
            return blk_sb, b + 1 if b < 4 else b - 1

        def halves(event, t, b=1):
            return 4 * event + 2 * t + b + 1

        def KV_of(n):
            return C[:, n % 2, 128 * n:128 * n + 256] if n != 1 else C[:, 1, 0:256]

        def GV_head(rows, h, t):
            return GVt[rows, t, GLA_DV * h:GLA_DV * h + GLA_DV]

        block = ctx.enter_context(nc.Block())

        @block.sync
        def _(sp):
            def load(n, slot, view):
                nk, width = view.shape[1], view.shape[2]
                dst = RAW[:, slot, 0:nk * width].rearrange("p (k c) -> p k c", c=width)
                sp.dma_start(dst, view).then_inc(raw_ready[slot], 16)

            sp.dma_start(IDENT, a["consts"][:, C_ID:C_ID + 128]).then_inc(ident_loaded, 16)
            for t in range(T):
                sp.dma_start(X[:, t, :], a["x"][0, 128 * t:128 * t + 128, :]).then_inc(x_loaded[t], 16)
            sp.dma_start(LR_RAW, w_in[:, O_LR:O_LR + GLA_RANK].rearrange("(k p) c -> p k c", p=128)).then_inc(lr_loaded, 16)
            for n in range(N_UNITS):
                if units[n] is None:
                    continue
                if n >= SLOTS:
                    sp.wait_ge(lo_ready, n - SLOTS + 1)
                load(n, n % SLOTS, units[n])
                if n == 1:
                    sp.dma_start(CST[:, C_ID + 128:N_CONST], a["consts"][:, C_ID + 128:N_CONST]).then_inc(cst_loaded, 16)
                if n + 1 in (U_FF0, U_FF1, U_FF2):
                    base, up, down = ffs[(U_FF0, U_FF1, U_FF2).index(n + 1)]
                    for half in range(2):
                        sp.wait_ge(lo_ready, base + half - SLOTS + 1)
                        load(None, (base + half) % SLOTS, up_unit(up, 0, half))
                    with sp.Fori(0, 7) as i:
                        for q in range(4):
                            sp.wait_ge(lo_ready, i * 4 + (base + 2 + q - SLOTS + 1))
                            v = up_unit(up, i + 1, q) if q < 2 else down_unit(down, i, q - 2)
                            load(None, (base + 2 + q) % SLOTS, v)
                    for half in range(2):
                        sp.wait_ge(lo_ready, base + 30 + half - SLOTS + 1)
                        load(None, (base + 30 + half) % SLOTS, down_unit(down, 7, half))
            for t in range(T):
                for b in range(2):
                    c = slice(512 * b, 512 * b + 512)
                    sp.wait_ge(x_ready, halves(6, t, b))
                    sp.dma_start(out[0, 128 * t:128 * t + 128, c], X[:, t, c]).then_inc(stored, 16)
            sp.wait_ge(stored, 16 * 2 * T)

        @block.gpsimd
        def _(pool):
            def gain(dst, row):
                pool.dma_start(dst, row.partition_broadcast(128)).then_inc(gain_loaded, 16)

            gain(GAIN0, a["norm_mix"][0])
            pool.memset(EPSC, EPS).then_inc(const_set, 1)
            pool.memset(LNEPSC, LN_EPS).then_inc(const_set, 1)
            pool.memset(ONEC, 1.0).then_inc(const_set, 1)
            for row, v in ((V_CONV, a["sc_conv_w_2"][0].rearrange("k (j p) -> (k j) p", p=128)),
                           (V_GLA, a["gla_out_norm"][0].rearrange("h (j p) -> (h j) p", p=128)),
                           (V_QN, a["moba_q_norm"]), (V_KN, a["moba_k_norm"]),
                           (V_GQ, a["mla_g_q_2"][0].rearrange("(j p) -> j p", p=128)),
                           (V_GKV, a["mla_g_kv_2"][0].rearrange("(j p) -> j p", p=128))):
                pool.dma_start(R[row:row + v.shape[0], 7680:7808], v).then_inc(rows_loaded, 16)
            pool.wait_ge(raw_ready[0], 16)
            pool.dma_start(P_RAW, a["p"][0, 0].rearrange("(t p) c -> p t c", p=128)).then_inc(p_loaded, 16)
            pool.memset(W2E, 0.0).then_inc(const_set, 1)
            pool.memset(GLRT, 0.0).then_inc(const_set, 1)
            pool.wait_ge(const_set, 5)
            pool.memset(GLRT[32:33, :], 1.0).then_inc(const_set, 1)
            pool.dma_start(W2E[0:GLA_RANK, :], a["gla_gate_w2"][0]).then_inc(w2_loaded, 16)
            pool.dma_start(W2E[32:33, :], a["gla_gate_b"]).then_inc(w2_loaded, 16)
            pool.wait_ge(const_set, 6)
            pool.memset(AT, 0.0).then_inc(const_set, 1)
            pool.wait_ge(o_lo, HEADS)
            gain(GAIN, a["norm_mlp"][0])
            pool.wait_ge(xt_lo, halves(1, 1))
            pool.memset(ZERO, 0.0).then_inc(const_set, 1)
            pool.wait_ge(xn_ready, halves(1, 1))
            gain(GAIN, a["norm_ple"][0])
            for j, (g, b) in enumerate((("ln_mix_g_2", "ln_mix_b_2"), ("ln_ff_g_2", "ln_ff_b_2")) * 2):
                if j == 0:
                    pool.wait_ge(xn_ready, halves(2, 1))
                else:
                    pool.wait_ge(x_ready, halves(2 + j, 1))
                if j == 2:
                    pool.wait_ge(o_psum, 2 * HEADS)
                gain(GAIN, a[g][j // 2])
                gain(BIAS, a[b][j // 2])
            pool.wait_ge(gain_loaded, 16 * 11)

        @block.scalar
        def _(act):
            own = [0]

            def chain(ins):
                own[0] += 1
                ins.then_inc(act_self, 1)
                act.wait_ge(act_self, own[0])

            def hi(n, slot, turn, width=UNIT, old=True):
                act.wait_ge(raw_ready[slot], turn)
                if old:
                    act.wait_ge(unit_used, n - SLOTS + 1)
                act.activation(HI[:, slot, 0:width], RAW[:, slot, 0:width], ACT.Copy).then_inc(hi_ready, 1)

            def hi_at(n):
                if n < N_UNITS:
                    w = UNIT if units[n] is None else UNIT_K[n] * UNIT_C[n]
                    hi(n, n % SLOTS, 16 * (n // SLOTS + 1), w, n >= SLOTS)

            def root(dst, src, scale, eps):
                return act.activation(dst, src, ACT.Sqrt, bias=eps, scale=scale)

            def xt_split(e, t):
                for b in range(2):
                    act.wait_ge(xt_psum, halves(e, t, b))
                    act.activation(XT_h[:, 4 * b:4 * b + 4, 128 * t:128 * t + 128],
                                   C[:, 2 * t + b, :].rearrange("p (k s) -> p k s", s=128), ACT.Copy).then_inc(xt_hi, 1)

            def rms(r, tiles=range(T)):
                for t in tiles:
                    if r == 0:
                        act.wait_ge(x_loaded[t], 16)
                        act.wait_ge(const_set, 3)
                    else:
                        act.wait_ge(x_ready, halves(r - 1, t))
                    junk = XN0 if r == 0 else XN
                    chain(act.activation(junk[:, t, :], X[:, t, :], ACT.Square, accum_out=SS[:, t:t + 1]))
                    root(RSTD[:, t:t + 1], SS[:, t:t + 1], 1.0 / D, EPSC).then_inc(root_ready, 1)

            def ln(j, tiles=range(T)):
                for t in tiles:
                    act.wait_ge(mv_ready, 2 * j + t + 1)
                    root(RSTD[:, t:t + 1], MVAR[:, t, 1:2], 1.0, LNEPSC).then_inc(root_ready, 1)

            def att_exp(j):
                p, PROB = j % 2, prob(j)
                act.wait_ge(sc_max, j + 1)
                act.activation(PROB[:, 0:128], PROB[:, 0:128], ACT.Exp, bias=NMAX[:, p, 0:1],
                               accum_out=RSUM[:, p, 0:1])
                act.activation(PROB[:, 128:384], PROB[:, 128:384], ACT.Exp, bias=NMAX[:, p, 1:2],
                               accum_out=RSUM[:, p, 1:2]).then_inc(sc_exp, 1)

            def att_pt(j):
                act.wait_ge(pt_psum, j + 1)
                if j >= 2:
                    act.wait_ge(o_psum, j - 1)
                act.activation(PRTS[j // HEADS][:, j % 2, :], C[:, 2, 0:384], ACT.Copy).then_inc(pt_sb, 1)

            def att_out(j):
                act.wait_ge(o_psum, j + 1)
                act.activation(OT_h[:, j % HEADS, :], C[:, 3, 0:SEQ], ACT.Copy).then_inc(o_hi, 1)

            def feed_forward(f, base):
                def squares(c, half, slot_unit):
                    if not (isinstance(c, int) and c == 0 and f == 0):
                        act.wait_ge(ff_sq, c * 2 + (16 * f + half - 1))
                    act.wait_ge(unit_used, slot_unit + 1)
                    act.activation(RELU[:, half, :], C[:, half, :], ACT.Relu).then_inc(ff_relu, 1)
                    act.wait_ge(ff_relu, c * 2 + (16 * f + half + 1))

                def square(par, half):
                    k = 4 * par + 2 * half
                    act.activation(HT_h[:, k:k + 2, :].rearrange("p a b -> p (a b)"), RELU[:, half, :],
                                   ACT.Square).then_inc(ff_hi, 1)

                for half in range(2):
                    squares(0, half, base + half)
                    square(0, half)
                    hi_at(base + half + SLOTS)

                def step(i, i_unit, par, peel):
                    for q in range(4):
                        if q < 2:
                            squares(i + 1, q, i_unit + (base + 2 + q))
                            square(par, q)
                        if peel:
                            hi_at(base + 2 + 4 * i + q + SLOTS)
                        else:
                            n0 = base + 2 + q + SLOTS
                            hi(i_unit + n0, n0 % SLOTS, i * 16 + 16 * (n0 // SLOTS + 1))

                with act.Fori(0, 3) as j:
                    for d in range(2):
                        step(j * 2 + d, j * 8 + 4 * d, (d + 1) % 2, False)
                step(6, 24, 1, True)

            rms(0)
            xt_split(0, 0)
            hi_at(0)
            xt_split(0, 1)
            act.wait_ge(lr_loaded, 16)
            act.activation(LR_h[:], LR_RAW, ACT.Copy).then_inc(lr_split, 1)
            for n in range(1, SLOTS):
                hi_at(n)

            def setup_rest():
                act.wait_ge(lr_psum, 1)
                act.activation(GLR, C[:, 0, 0:T * GLA_RANK].rearrange("p (t c) -> p t c", t=T), ACT.Copy).then_inc(lr_sb, 1)
                act.wait_ge(lrt_psum, 1)
                act.wait_ge(const_set, 6)
                act.activation(GLRT[0:GLA_RANK, :], C[0:GLA_RANK, 1, 0:SEQ], ACT.Copy).then_inc(lrt_sb, 1)
                act.wait_ge(cols_psum, 1)
                act.activation(COLS[:, 0:N_VEC], C[:, 2, 0:N_VEC], ACT.Copy).then_inc(cols_ready, 1)
                act.wait_ge(p_psum, 1)
                act.activation(PT_h[:].rearrange("p a b -> p (a b)"), C[:, 3, :], ACT.Copy).then_inc(p_hi, 1)

            blocks = [GQ, GK, GV[:, 0], GV[:, 1], None, None, MQ[:, 0], MQ[:, 1], MK[:, 0], MK[:, 1], MV[:, 0], MV[:, 1]]
            sig_of = {4: GR[:, 0], 5: GR[:, 1], 12: SG0, 14: SG0, 16: SG1, 17: SG0}

            def moba_scales(b, i):
                act.wait_ge(blk_sb, i + 5)
                if i:
                    act.wait_ge(m_ssq, i)
                act.activation(MSQ, blocks[b], ACT.Square).then_inc(m_sq, 1)
                act.wait_ge(m_ssq, i + 1)
                r = slice(8 * (i % 2), 8 * (i % 2) + 8)
                root(RQ[:, r], SSQ[:, r], 1.0 / DH, EPSC).then_inc(m_root, 1)

            for u in range(N_MIX):
                b = u // 2
                if u % 2 and b < 18:
                    src = ACC[:, 2 * (b % 2):2 * (b % 2) + 2, :]
                    if b in sig_of:
                        act.wait_ge(unit_used, u + 1)
                        if b in (14, 17):
                            act.wait_ge(y_ready, 1 if b == 14 else 2)
                        act.activation(sig_of[b], src, ACT.Sigmoid).then_inc(sig_e, 1)
                    elif b < 12:
                        act.wait_ge(unit_used, u + 1)
                        if b == 6:
                            act.wait_ge(kd_ready, 2)
                        if b == 10:
                            act.wait_ge(g2_psum, GLA_H)
                        act.activation(blocks[b], src, ACT.Copy).then_inc(blk_sb, 1)
                if u == 0:
                    setup_rest()
                if u == 1:
                    act.wait_ge(z_psum, 1)
                    zz = C[:, 0:2, :]
                    chain(act.activation(LA, zz, ACT.Abs))
                    chain(act.activation(LA, LA, ACT.Exp, scale=-1.0))
                    act.activation(LA, LA, ACT.Ln, bias=ONEC, scale=1.0).then_inc(z_l, 1)
                if u == 3:
                    act.wait_ge(cum_psum, 1)
                    cb = C[:, 0:2, :].rearrange("p b (h s) -> p (b h) s", s=SEQ)
                    act.activation(QD, cb, ACT.Exp)
                    act.activation(KDT, cb, ACT.Exp, scale=-1.0)
                    act.activation(LA, C[:, 2:4, :], ACT.Exp).then_inc(cum_exp, 1)
                for h in range(GLA_H):
                    if u == 10 + 2 * h:
                        act.wait_ge(g1_psum, h + 1)
                        act.activation(S[:, 0, :], C[:, 0, 0:GLA_DV], ACT.Copy).then_inc(g1_s1, 1)
                    if u == 11 + 2 * h:
                        act.wait_ge(g2_psum, h + 1)
                        for t in range(T):
                            r = act.activation(SQJ[:, t, :], C[:, 2, 256 * t:256 * t + 256], ACT.Square,
                                               accum_out=GSS[:, t:t + 1])
                        chain(r)
                        root(GSS, GSS, 1.0 / GLA_DV, EPSC).then_inc(g2_root, 1)
                    if u == 12 + 2 * h:
                        act.wait_ge(g3_psum, h + 1)
                        for j in range(2):
                            act.activation(HT_h[:, 2 * h + j, :], C[:, 3, 256 * j:256 * j + 256], ACT.Copy,
                                           scale=vec(V_GLA + 2 * h + j)).then_inc(g3_hi, 1)
                if u in (14, 16, 18, 20):
                    moba_scales(u // 2 - 1, u // 2 - 7)
                h = u - 22
                if 0 <= h < HEADS:
                    act.wait_ge(m2_psum, h + 1)
                    act.activation(QKT[:, h % 2, 0:256], C[:, 0, 0:256], ACT.Copy, scale=vec(V_QN)).then_inc(m2_q, 1)
                if 1 <= h < HEADS + 1:
                    att_exp(h - 1)
                if 2 <= h < HEADS + 2:
                    att_pt(h - 2)
                if 3 <= h < HEADS + 3:
                    att_out(h - 3)
                if u in (38, 40):
                    k = 2 * (u - 38)
                    act.wait_ge(xt_psum, halves(1, (u - 38) // 2))
                    act.activation(XT_h[:, k:k + 4, :], C[:, k // 2:k // 2 + 2, :].rearrange("p b (k s) -> p (b k) s", s=SEQ),
                                   ACT.Copy).then_inc(xt_hi, 2)
                if u < N_MIX - 2:
                    hi_at(u + SLOTS)

            def finish_pair(last, e, scales=None):
                for t in range(T):
                    if scales is not None:
                        scales[0](scales[1], (t,))
                    xt_split(e, t)
                    if e == 3:
                        hi_at(last - 1 + t + SLOTS)
                if e != 3:
                    hi_at(last - 1 + SLOTS)
                    hi_at(last + SLOTS)

            finish_pair(U_FF0 - 1, 2, (rms, 1))
            feed_forward(0, U_FF0)
            rms(2)
            for t in range(T):
                act.wait_ge(tail, 3) if t == 0 else act.wait_ge(unit_used, U_PLE + 1)
                act.activation(PLEO[:, t, :], C[:, 2 * t:2 * t + 2, :].rearrange("p b c -> p (b c)"), ACT.Copy).then_inc(ple_sb, 1)
            finish_pair(U_PLE - 1, 3)
            for q in range(3):
                hi_at(U_PLE + q + SLOTS)
            for t in range(T):
                act.wait_ge(tail, 4) if t == 0 else act.wait_ge(unit_used, U_CONV)
                act.activation(SG[:, t, :], ACC[:, 2 * t:2 * t + 2, :].rearrange("p b c -> p (b c)"),
                               ACT.Sigmoid).then_inc(pg_sig, 1)
            finish_pair(U_CONV - 1, 4)
            for q in range(12):
                n, pair, part = U_CONV + q, q // 3, q % 3
                act.wait_ge(unit_used, n + 1)
                if part == 0:
                    if pair >= 2:
                        act.wait_ge(cv_z, pair - 1)
                    act.activation(CS[:, pair % 2, :], C[:, q % 4, :], ACT.Copy).then_inc(cv_c, 1)
                hi_at(n + SLOTS)
                if part == 2:
                    act.wait_ge(cv_v, pair + 1)
                    act.activation(OT_h[:, 2 * pair:2 * pair + 2, :].rearrange("p a b -> p (a b)"),
                                   VB.rearrange("p a b -> p (a b)"), ACT.Copy).then_inc(cv_hi, 1)
            for q in range(2):
                hi_at(U_CONVO + q + SLOTS)
            finish_pair(U_FF1 - 1, 5, (ln, 0))
            feed_forward(1, U_FF1)
            finish_pair(U_MLA - 1, 6, (ln, 1))

            def latent(i, junk, bank, width, last):
                act.wait_ge(unit_used, last + 1)
                for t in range(T):
                    r = act.activation(junk[:, t, :], ACC[:, bank + t, 0:width], ACT.Square,
                                       accum_out=GSS[:, t:t + 1])
                chain(r)
                root(RQ[:, 2 * i:2 * i + 2], GSS, 1.0 / width, EPSC).then_inc(l_root, 1)
                act.wait_ge(l_root, i + 1)

            def latent_high(ks, psum, bank0):
                act.wait_ge(l_psum, psum)
                for i, k in enumerate(ks):
                    act.activation(HT_h[:, k, :], C[:, bank0 + i // 2, 256 * (i % 2):256 * (i % 2) + 256], ACT.Copy,
                                   scale=vec(LATENT_GAIN[k])).then_inc(l_hi, 1)

            latent(0, CKV, 0, KVL, U_MLA + 1)
            hi_at(U_MLA + SLOTS)
            latent_high((3, 4), 1, 2)
            hi_at(U_MLA + 1 + SLOTS)
            act.wait_ge(kp_psum, 1)
            act.activation(KPT, C[:, 3, 0:256], ACT.Copy).then_inc(kp_sb, 1)
            latent(1, CQ, 2, QL, U_MLA + 3)
            latent_high((0, 1, 2), 2, 0)
            for q in range(2, 4):
                hi_at(U_MLA + q + SLOTS)
            act.wait_ge(unit_used, U_MLA + 5)
            act.activation(KNT, ACC[:].rearrange("p b (h s) -> p (b h) s", s=SEQ), ACT.Copy).then_inc(kn_sb, 1)
            hi_at(U_MLA + 4 + SLOTS)
            act.wait_ge(unit_used, U_MLA + 6)
            act.activation(VT, C[:].rearrange("p (t b) c -> p t (b c)", t=T), ACT.Copy).then_inc(v_sb, 1)
            hi_at(U_MLA + 5 + SLOTS)
            scale = float(NOPE + ROPE) ** -0.5
            for s in range(4 + HEADS + 2):
                if s < 4:
                    n = U_MLA + 6 + s
                    act.wait_ge(unit_used, n + 1)
                    act.activation(QNT[:, 2 * s:2 * s + 2, :].rearrange("p a b -> p (a b)"), ACC[:, 2 * (s % 2), :],
                                   ACT.Copy, scale=scale).then_inc(uq_nope, 1)
                if 2 <= s < HEADS + 2:
                    att_exp(HEADS + s - 2)
                if 4 <= s < HEADS + 4:
                    att_pt(HEADS + s - 4)
                if 1 <= s < 5:
                    act.wait_ge(qp_psum, s)
                    act.activation(QPT[:, s - 1, :], C[:, 0, 0:256], ACT.Copy, scale=scale).then_inc(qp_sb, 1)
                if 5 <= s < HEADS + 5:
                    att_out(HEADS + s - 5)
                if s < 2:
                    hi_at(U_WO + s)
                if s in (8, 10, 11, 12):
                    hi_at(U_WO + 2 + (8, 10, 11, 12).index(s))
            finish_pair(U_FF2 - 1, 7, (ln, 2))
            feed_forward(2, U_FF2)
            ln(3)

        @block.vector
        def _(dve):
            own = [0]

            def chain(ins):
                own[0] += 1
                ins.then_inc(dve_self, 1)
                dve.wait_ge(dve_self, own[0])

            def low(n, slot, width=UNIT):
                dve.wait_ge(hi_ready, n + 1)
                dve.tensor_tensor(LO[:, slot, 0:width], RAW[:, slot, 0:width], HI[:, slot, 0:width].bitcast(f32),
                                  ALU.subtract).then_inc(lo_ready, 1)

            def low_at(n):
                if n < N_UNITS:
                    low(n, n % SLOTS, UNIT if units[n] is None else UNIT_K[n] * UNIT_C[n])

            def xt_low(e, t):
                s = slice(128 * t, 128 * t + 128)
                for b in range(2):
                    k = slice(4 * b, 4 * b + 4)
                    dve.wait_ge(xt_hi, halves(e, t, b))
                    dve.tensor_tensor(XT_l[:, k, s], C[:, 2 * t + b, :].rearrange("p (k s) -> p k s", s=128),
                                      XT_h[:, k, s].bitcast(f32), ALU.subtract).then_inc(xt_lo, 1)

            gains = [0]

            def rms_apply(r, e=None):
                gains[0] += 1
                dve.wait_ge(gain_loaded, 16 * gains[0])
                dst, g = (XN0, GAIN0) if r == 0 else (XN, GAIN)
                for t in range(T):
                    dve.wait_ge(root_ready, 2 * r + t + 1)
                    chain(dve.reciprocal(RSTD[:, t:t + 1], RSTD[:, t:t + 1]))
                    for b in range(2):
                        c = slice(512 * b, 512 * b + 512)
                        dve.scalar_tensor_tensor(dst[:, t, c], X[:, t, c], RSTD[:, t:t + 1], g[:, c], ALU.mult,
                                                 ALU.mult).then_inc(xn_ready, 1)
                for t in range(T):
                    if e is not None:
                        xt_low(e, t)

            def finish_pair(last, e):
                for t in range(T):
                    xt_low(e, t)
                    if e == 3:
                        low_at(last - 1 + t + SLOTS)
                if e != 3:
                    low_at(last - 1 + SLOTS)
                    low_at(last + SLOTS)

            def add_to_x(pair, last_unit):
                for t in range(T):
                    dve.wait_ge(tail, pair) if t == 0 else dve.wait_ge(unit_used, last_unit + 1)
                    dve.tensor_tensor(X[:, t, :], X[:, t, :], ACC[:, 2 * t:2 * t + 2, :].rearrange("p b c -> p (b c)"),
                                      ALU.add).then_inc(x_ready, 2)

            def layer_norm(j, pair, last_unit, e=None):
                gains[0] += 2
                for t in range(T):
                    x = X[:, t, :]
                    dve.wait_ge(tail, pair) if t == 0 else dve.wait_ge(unit_used, last_unit + 1)
                    if t == 1 and e == 6:
                        xt_low(e, 0)
                    chain(dve.scalar_tensor_tensor(x, x, ALPHA, ACC[:, 2 * t:2 * t + 2, :].rearrange("p b c -> p (b c)"),
                                                   ALU.mult, ALU.add))
                    dve.bn_stats(BN[:, t, 0:6], X[:, t, 0:512])
                    chain(dve.bn_stats(BN[:, t, 6:12], X[:, t, 512:1024]))
                    dve.bn_aggr(MVAR[:, t, :], BN[:, t, :]).then_inc(mv_ready, 1)
                    dve.wait_ge(mv_ready, 2 * j + t + 1)
                    dve.wait_ge(gain_loaded, 16 * gains[0])
                    chain(dve.scalar_tensor_tensor(x, x, MVAR[:, t, 0:1], GAIN, ALU.subtract, ALU.mult))
                    dve.wait_ge(root_ready, 6 + 2 * j + t + 1)
                    chain(dve.reciprocal(RSTD[:, t:t + 1], RSTD[:, t:t + 1]))
                    for b in range(2):
                        c = slice(512 * b, 512 * b + 512)
                        dve.scalar_tensor_tensor(x[:, c], x[:, c], RSTD[:, t:t + 1], BIAS[:, c], ALU.mult,
                                                 ALU.add).then_inc(x_ready, 1)
                if e is not None:
                    if e != 6:
                        xt_low(e, 0)
                    xt_low(e, 1)
                    low_at(last_unit - 1 + SLOTS)
                    low_at(last_unit + SLOTS)

            def att_scores(j, table, slope):
                p, PROB = j % 2, prob(j)
                dve.wait_ge(sc_psum, j + 1)
                if j >= 2:
                    dve.wait_ge(pt_psum, j - depth(j) + 1)
                dve.scalar_tensor_tensor(PROB, table, slope, C[:, 1, 0:384], ALU.mult, ALU.add).then_inc(sc_read, 1)
                dve.wait_ge(sc_read, j + 1)
                dve.tensor_reduce(NMAX[:, p, 0:1], PROB[:, 0:128], AX.X, ALU.max, negate=True)
                dve.tensor_reduce(NMAX[:, p, 1:2], PROB[:, 128:384], AX.X, ALU.max, negate=True).then_inc(sc_max, 1)

            def att_inverse(j):
                p = j % 2
                dve.wait_ge(sc_exp, j + 1)
                chain(dve.reciprocal(RINV[:, p, :], RSUM[:, p, :]))
                if j == 0:
                    dve.wait_ge(g2_psum, GLA_H)
                if j >= 2:
                    dve.wait_ge(pt_psum, j - depth(j) + 1)
                for t in range(T):
                    r = dve.tensor_scalar(diag(j)[:, t, :], IDENT, RINV[:, p, t:t + 1], None, ALU.mult)
                r.then_inc(diag_ready, 1)

            def att_low(j):
                dve.wait_ge(o_hi, j + 1)
                dve.tensor_tensor(OT_l[:, j % HEADS, :], C[:, 3, 0:SEQ], OT_h[:, j % HEADS, :].bitcast(f32),
                                  ALU.subtract).then_inc(o_lo, 1)

            def feed_forward(f, base):
                def square(c, par, half):
                    k = 4 * par + 2 * half
                    dve.wait_ge(ff_relu, c * 2 + (16 * f + half + 1))
                    dve.tensor_tensor(SQ[:, half, :], RELU[:, half, :], RELU[:, half, :], ALU.mult).then_inc(ff_sq, 1)
                    dve.wait_ge(ff_hi, c * 2 + (16 * f + half + 1))
                    dve.wait_ge(ff_sq, c * 2 + (16 * f + half + 1))
                    dve.tensor_tensor(HT_l[:, k:k + 2, :].rearrange("p a b -> p (a b)"), SQ[:, half, :],
                                      HT_h[:, k:k + 2, :].rearrange("p a b -> p (a b)").bitcast(f32),
                                      ALU.subtract).then_inc(ff_lo, 1)

                for half in range(2):
                    square(0, 0, half)
                    low_at(base + half + SLOTS)
                with dve.Fori(0, 3) as j:
                    for d in range(2):
                        for q in range(4):
                            if q < 2:
                                square(j * 2 + (d + 1), (d + 1) % 2, q)
                            n0 = base + 2 + q + SLOTS + 4 * d
                            low(j * 8 + n0, n0 % SLOTS)
                for q in range(4):
                    if q < 2:
                        square(7, 1, q)
                    low_at(base + 26 + q + SLOTS)

            rms_apply(0)
            xt_low(0, 0)
            low_at(0)
            xt_low(0, 1)
            dve.wait_ge(lr_split, 1)
            dve.tensor_tensor(LR_l[:], LR_RAW, LR_h[:].bitcast(f32), ALU.subtract).then_inc(lr_split, 1)
            for n in range(1, SLOTS):
                low_at(n)

            moba_blocks = [MQ[:, 0], MQ[:, 1], MK[:, 0], MK[:, 1]]

            def moba_norm(i):
                r = slice(8 * (i % 2), 8 * (i % 2) + 8)
                dve.wait_ge(m_sq, i + 1)
                dve.tensor_reduce(SSQ[:, r], MSQ.rearrange("p t (h d) -> p t h d", d=DH), AX.X, ALU.add).then_inc(m_ssq, 1)
                dve.wait_ge(m_root, i + 1)
                chain(dve.reciprocal(RQ[:, r], RQ[:, r]))
                v = moba_blocks[i].rearrange("p t (h d) -> p t h d", d=DH)
                scales = RQ[:, r].rearrange("p (t h) -> p t h", t=T).unsqueeze(3).broadcast_to([128, T, 4, DH])
                dve.tensor_tensor(v, v, scales, ALU.mult).then_inc(m_norm, 1)

            for u in range(N_MIX):
                b = u // 2
                if u % 2 and b in (13, 15):
                    dve.wait_ge(unit_used, u + 1)
                    dve.wait_ge(sig_e, 3 if b == 13 else 4)
                    dve.tensor_tensor(Y0 if b == 13 else Y1, SG0, ACC[:, 2:4, :], ALU.mult).then_inc(y_ready, 1)
                if u in (37, 39):
                    y, s, p = (Y0, SG1, 0) if u == 37 else (Y1, SG0, 1)
                    dve.wait_ge(unit_used, u + 1)
                    dve.wait_ge(sig_e, 5 if u == 37 else 6)
                    chain(dve.tensor_tensor(s, s, ACC[:, 2 * p:2 * p + 2, :], ALU.mult))
                    dve.tensor_tensor(y, y, s, ALU.add).then_inc(y_ready, 1)
                if u in (38, 40):
                    k = 2 * (u - 38)
                    dve.wait_ge(xt_hi, halves(1, (u - 38) // 2))
                    dve.tensor_tensor(XT_l[:, k:k + 4, :], C[:, k // 2:k // 2 + 2, :].rearrange("p b (k s) -> p (b k) s", s=SEQ),
                                      XT_h[:, k:k + 4, :].bitcast(f32), ALU.subtract).then_inc(xt_lo, 2)
                if u == 0:
                    dve.wait_ge(p_hi, 1)
                    dve.tensor_tensor(PT_l[:].rearrange("p a b -> p (a b)"), C[:, 3, :],
                                      PT_h[:].rearrange("p a b -> p (a b)").bitcast(f32), ALU.subtract).then_inc(p_lo, 1)
                if u == 1:
                    dve.wait_ge(z_l, 1)
                    dve.scalar_tensor_tensor(LA, C[:, 0:2, :], 0.0, LA, ALU.min, ALU.subtract).then_inc(la_ready, 1)
                if u == 4:
                    dve.wait_ge(cum_exp, 1)
                    dec = QD.rearrange("p h (n c) -> p h n c", c=GLA_CHUNK)[:, :, :, GLA_CHUNK - 1]
                    chain(dve.tensor_copy(DEC, dec))
                    dve.wait_ge(qt_psum, 1)
                    dve.scalar_tensor_tensor(QD, C[:, 2:4, :].rearrange("p b (h s) -> p (b h) s", s=SEQ),
                                             float(GLA_DK) ** -0.5, QD, ALU.mult, ALU.mult).then_inc(qd_ready, 1)
                if u == 5:
                    dve.wait_ge(kt_psum, 1)
                    dve.tensor_tensor(KDT, C[:, 0:2, :].rearrange("p b (h s) -> p (b h) s", s=SEQ), KDT,
                                      ALU.mult).then_inc(kd_ready, 1)
                    dve.tensor_tensor(GK, GK, LA, ALU.mult).then_inc(kd_ready, 1)
                for h in range(GLA_H):
                    if u == 10 + 2 * h:
                        dve.wait_ge(g1_psum, h + 1)
                        dve.wait_ge(const_set, 7)
                        dve.wait_ge(cst_loaded, 16)
                        for j in range(2):
                            q = slice(64 * j, 64 * j + 64)
                            dve.copy_predicated(AT[q, :, q], GLA_MASK[q, :, :],
                                                C[q, 1, 256:384].rearrange("p (t c) -> p t c", t=T))
                        dve.wait_ge(g1_s1, h + 1)
                        for n in (1, 2):
                            r = dve.scalar_tensor_tensor(S[:, n, :], S[:, n - 1, :], DEC[:, h, n:n + 1],
                                                         KV_of(n), ALU.mult, ALU.add)
                            if n == 1:
                                chain(r)
                        r.then_inc(g1_ready, 1)
                    if u == 11 + 2 * h:
                        dve.wait_ge(g2_root, h + 1)
                        dve.wait_ge(gr_ready, 1 + h // 2)
                        if h >= 1:
                            dve.wait_ge(g3_psum, h)
                        chain(dve.reciprocal(GSS, GSS))
                        for t in range(T):
                            r = dve.scalar_tensor_tensor(OTOK[:, t, :], C[:, 2, 256 * t:256 * t + 256], GSS[:, t:t + 1],
                                                         GRt[:, t, GLA_DV * h:GLA_DV * h + GLA_DV], ALU.mult, ALU.mult)
                        r.then_inc(g2_ready, 1)
                    if u == 12 + 2 * h:
                        for j in range(2):
                            dve.wait_ge(g3_hi, 2 * h + 2)
                            dve.scalar_tensor_tensor(HT_l[:, 2 * h + j, :], C[:, 3, 256 * j:256 * j + 256],
                                                     vec(V_GLA + 2 * h + j), HT_h[:, 2 * h + j, :].bitcast(f32),
                                                     ALU.mult, ALU.subtract).then_inc(g3_lo, 1)
                if u in (14, 16, 18, 20):
                    moba_norm(u // 2 - 7)
                h = u - 22
                if 0 <= h < HEADS:
                    dve.wait_ge(m2_q, h + 1)
                    dve.tensor_scalar(QKT[:, h % 2, 256:512], C[:, 0, 256:512], vec(V_KN), float(DH) ** -0.5,
                                      ALU.mult, ALU.mult).then_inc(m2_k, 1)
                if 1 <= h < HEADS + 1:
                    att_scores(h - 1, DIST, 2.0 ** (-h))
                if 3 <= h < HEADS + 3:
                    att_low(h - 3)
                if 1 <= h < HEADS + 1:
                    att_inverse(h - 1)
                if u < N_MIX - 2:
                    low_at(u + SLOTS)
                if u in (9, 11):
                    dve.wait_ge(sig_e, b - 3)
                    g = GR[:, b - 4]
                    dve.tensor_tensor(g, g, ACC[:, 2 * (b % 2):2 * (b % 2) + 2, :], ALU.mult).then_inc(gr_ready, 1)

            add_to_x(1, U_FF0 - 1)
            rms_apply(1, 2)
            for half in range(2):
                low_at(U_FF0 - 2 + half + SLOTS)
            feed_forward(0, U_FF0)
            add_to_x(2, U_PLE - 1)
            rms_apply(2)
            finish_pair(U_PLE - 1, 3)
            for q in range(3):
                low_at(U_PLE + q + SLOTS)
            for t in range(T):
                dve.wait_ge(pg_sig, t + 1)
                s = SG[:, t, :]
                dve.wait_ge(ple_sb, 2)
                chain(dve.tensor_tensor(s, s, PLEO[:, t, :], ALU.mult))
                for b in range(2):
                    c = slice(512 * b, 512 * b + 512)
                    dve.tensor_tensor(X[:, t, c], X[:, t, c], s[:, c], ALU.add).then_inc(x_ready, 1)
            finish_pair(U_CONV - 1, 4)
            chain(dve.memset(Z[:, :, 0:2], 0.0))
            for q in range(12):
                n, pair, part = U_CONV + q, q // 3, q % 3
                dve.wait_ge(unit_used, n + 1)
                bank = C[:, q % 4, :].rearrange("p (a s) -> p a s", a=2)
                if part == 1:
                    dve.wait_ge(cv_c, pair + 1)
                    dve.tensor_tensor(Z[:, :, 2:258], bank, CS[:, pair % 2, :].rearrange("p (a s) -> p a s", a=2),
                                      ALU.mult).then_inc(cv_z, 1)
                    dve.wait_ge(cv_z, pair + 1)
                    if pair:
                        dve.wait_ge(cv_hi, pair)
                    for tap in (2, 1, 0):
                        for j in range(2):
                            w = vec(V_CONV + 8 * tap + 2 * pair + j)
                            z = Z[:, j, tap:tap + 256]
                            if tap == 2:
                                r = dve.tensor_scalar(VB[:, j, :], z, w, None, ALU.mult)
                            else:
                                r = dve.scalar_tensor_tensor(VB[:, j, :], z, w, VB[:, j, :], ALU.mult, ALU.add)
                        chain(r)
                low_at(n + SLOTS)
                if part == 2:
                    dve.tensor_tensor(VB, VB, bank, ALU.mult).then_inc(cv_v, 1)
                    dve.wait_ge(cv_v, pair + 1)
                    dve.wait_ge(cv_hi, pair + 1)
                    dve.tensor_tensor(OT_l[:, 2 * pair:2 * pair + 2, :], VB, OT_h[:, 2 * pair:2 * pair + 2, :].bitcast(f32),
                                      ALU.subtract).then_inc(cv_lo, 1)
            for q in range(2):
                low_at(U_CONVO + q + SLOTS)
            layer_norm(0, 5, U_FF1 - 1, 5)
            feed_forward(1, U_FF1)
            layer_norm(1, 6, U_MLA - 1, 6)

            def latent(i, dst, bank, width):
                dve.wait_ge(l_root, i + 1)
                chain(dve.reciprocal(RQ[:, 2 * i:2 * i + 2], RQ[:, 2 * i:2 * i + 2]))
                for t in range(T):
                    dve.tensor_scalar(dst[:, t, :], ACC[:, bank + t, 0:width], RQ[:, 2 * i + t:2 * i + t + 1], None,
                                      ALU.mult).then_inc(l_norm, 1)

            def latent_low(ks, high, low_bank):
                for i, k in enumerate(ks):
                    dve.wait_ge(l_hi, high[i])
                    dve.scalar_tensor_tensor(HT_l[:, k, :], C[:, low_bank + i // 2, 256 * (i % 2):256 * (i % 2) + 256],
                                             vec(LATENT_GAIN[k]), HT_h[:, k, :].bitcast(f32), ALU.mult,
                                             ALU.subtract).then_inc(l_lo, 1)

            def rope(dst, x1, x2, cos, sin):
                shape = list(x1.shape)
                n = shape[1] * shape[2] * (shape[3] if len(shape) == 4 else 1)
                tmp = [RT[:, i, 0:n] for i in range(2)]
                if len(shape) == 4:
                    tmp = [v.rearrange("p (t h c) -> p t h c", h=shape[2], c=32) for v in tmp]
                    cos, sin = (v.unsqueeze(2).broadcast_to(shape) for v in (cos, sin))
                else:
                    tmp = [v.rearrange("p (t c) -> p t c", c=32) for v in tmp]
                for d, f1, f2, op in ((dst[0], cos, sin, ALU.subtract), (dst[1], sin, cos, ALU.add)):
                    dve.tensor_tensor(tmp[0], x1, f1, ALU.mult)
                    chain(dve.tensor_tensor(tmp[1], x2, f2, ALU.mult))
                    r = dve.tensor_tensor(d, tmp[0], tmp[1], op)
                    if d is dst[0]:
                        chain(r)
                return r

            latent(0, CKV, 0, KVL)
            kp = KPK.rearrange("p t (u c) -> p t u c", u=2)
            chain(rope((kp[:, :, 0, 0:32], kp[:, :, 0, 32:64]), ACC[:, 0:2, KVL:KVL + 32],
                       ACC[:, 0:2, KVL + 32:KVL + 64], COS, SIN))
            dve.tensor_copy(kp[:, :, 1, :], kp[:, :, 0, :]).then_inc(l_norm, 1)
            low_at(U_MLA + SLOTS)
            latent_low((3, 4), (2, 2), 2)
            low_at(U_MLA + 1 + SLOTS)
            latent(1, CQ, 2, QL)
            latent_low((0, 1, 2), (4, 4, 5), 0)
            for q in range(2, 6):
                low_at(U_MLA + q + SLOTS)
            for s in range(4 + HEADS + 2):
                if 2 <= s < HEADS + 2:
                    att_scores(HEADS + s - 2, CHUNK_MASK, 1.0)
                if s < 4:
                    n = U_MLA + 6 + s
                    dve.wait_ge(unit_used, n + 1)
                    if s:
                        dve.wait_ge(uq_rope, s)
                    pe_part = ACC[:, 2 * (s % 2) + 1, 0:256].rearrange("p (t h c) -> p t h c", t=T, c=ROPE)
                    qp = QPK.rearrange("p t (g h c) -> p t g h c", h=2, c=ROPE)[:, :, s]
                    rope((qp[:, :, :, 0:32], qp[:, :, :, 32:64]), pe_part[:, :, :, 0:32], pe_part[:, :, :, 32:64], COS,
                         SIN).then_inc(uq_rope, 1)
                if 5 <= s < HEADS + 5:
                    att_low(HEADS + s - 5)
                if 2 <= s < HEADS + 2:
                    att_inverse(HEADS + s - 2)
                if s < 2:
                    low_at(U_WO + s)
                if s in (8, 10, 11, 12):
                    low_at(U_WO + 2 + (8, 10, 11, 12).index(s))
            layer_norm(2, 7, U_FF2 - 1, 7)
            feed_forward(2, U_FF2)
            layer_norm(3, 8, N_UNITS - 1)

        @block.tensor
        def _(pe):
            def three(dst, s_h, s_l, m_h, m_l, first, last):
                pe.matmul(dst, s_h, m_h, start=first, stop=False, skip_group_check=True)
                pe.matmul(dst, s_h, m_l, start=False, stop=False, skip_group_check=True)
                return pe.matmul(dst, s_l, m_h, start=False, stop=last, skip_group_check=True)

            def tokens_out(n, src_h, src_l, k0, bank, first, last, nk=4, width=512, free=None):
                slot = n % SLOTS
                pe.wait_ge(lo_ready, n + 1)
                for t in range(T):
                    if free is not None:
                        pe.wait_ge(*free(t))
                    s = slice(128 * t, 128 * t + 128)
                    for k in range(nk):
                        w = slice(k * width, k * width + width)
                        m = three(bank(t), src_h[:, k0 + k, s], src_l[:, k0 + k, s], HI[:, slot, w], LO[:, slot, w],
                                  first and k == 0, last and k == nk - 1)
                m.then_inc(unit_used, 1)

            def tokens_pair(ns, src_h, src_l, k0s, banks, first, last, inputs=None, ends_stage=False, width=512, nk=4):
                for t in range(T):
                    s = slice(128 * t, 128 * t + 128)
                    if inputs is not None:
                        inputs(t)
                    for i, n in enumerate(ns):
                        if t == 0:
                            pe.wait_ge(lo_ready, n + 1)
                        for k in range(nk):
                            w = slice(k * width, k * width + width)
                            m = three(banks(t, i), src_h[:, k0s[i] + k, s], src_l[:, k0s[i] + k, s],
                                      HI[:, n % SLOTS, w], LO[:, n % SLOTS, w], first[i] and k == 0,
                                      last[i] and k == nk - 1)
                        if t == 1:
                            m.then_inc(unit_used, 1)
                    if t == 0 and ends_stage:
                        m.then_inc(tail, 1)

            def last_four(base, src_h, src_l, ready):
                for c in range(2):
                    pe.wait_ge(*ready(0))
                    tokens_out(base + c, src_h, src_l, 0, lambda t: ACC[:, 2 * t + c, :], True, False)
                pe.wait_ge(*ready(1))
                tokens_pair((base + 2, base + 3), src_h, src_l, (4, 4), lambda t, i: ACC[:, 2 * t + i, :], (False, False),
                            (True, True), ends_stage=True)

            def features_out(n, slot, dst, src_h, src_l, k0=0, nk=KD, width=256, tiles=(0, 1), inc=True, e=None):
                pe.wait_ge(lo_ready, n + 1)
                for i, j in enumerate(tiles):
                    for k in range(nk):
                        if e is not None and i == 0 and k in (0, 4):
                            pe.wait_ge(xt_lo, halves(e, 1, k // 4))
                        w = slice(k * width + 128 * j, k * width + 128 * j + 128)
                        m = three(dst(i), HI[:, slot, w], LO[:, slot, w], src_h[:, k0 + k, :], src_l[:, k0 + k, :],
                                  k == 0, k == nk - 1)
                if inc:
                    m.then_inc(unit_used, 1)
                return m

            def transpose_x(e, src, made, version, free=None, tiles=range(T)):
                for t in tiles:
                    if free is not None:
                        pe.wait_ge(*free(t))
                    for b in range(2):
                        pe.wait_ge(made, halves(version, t, b))
                        for k in range(4):
                            m = pe.transpose(C[:, 2 * t + b, 128 * k:128 * k + 128],
                                             src[:, t, 512 * b + 128 * k:512 * b + 128 * k + 128], IDENT)
                        m.then_inc(xt_psum, 1)

            def att_score(j, parts):
                if j:
                    pe.wait_ge(sc_read, j)
                for t in range(T):
                    dst = C[:, 1, 0:128] if t == 0 else C[:, 1, 128:384]
                    for i, (q, k) in enumerate(parts):
                        m = pe.matmul(dst, q[:, 128 * t:128 * t + 128], k[:, 0:128 * (t + 1)], start=(i == 0),
                                      stop=(i == len(parts) - 1), skip_group_check=True)
                m.then_inc(sc_psum, 1)

            def att_transpose(j):
                pe.wait_ge(diag_ready, j + 1)
                if j:
                    pe.wait_ge(pt_sb, j)
                for i in range(3):
                    m = pe.matmul(C[:, 2, 128 * i:128 * i + 128], prob(j)[:, 128 * i:128 * i + 128],
                                  diag(j)[:, min(i, 1), :], start=True, stop=True, skip_group_check=True)
                m.then_inc(pt_psum, 1)

            def att_values(j, v, h):
                pe.wait_ge(pt_sb, j + 1)
                if j:
                    pe.wait_ge(o_lo, j)
                p = PRTS[j // HEADS][:, j % 2, :]
                pe.matmul(C[:, 3, 0:256], v[:, 0, 128 * h:128 * h + 128], p[:, 0:256], start=True, stop=False,
                          skip_group_check=True)
                pe.matmul(C[:, 3, 128:256], v[:, 1, 128 * h:128 * h + 128], p[:, 256:384], start=False, stop=True,
                          skip_group_check=True).then_inc(o_psum, 1)

            def feed_forward(f, base, e):
                pe.wait_ge(const_set, 8)
                for bank in range(4):
                    pe.matmul(ACC[:, bank, :], ZERO[:, 0:128], ZERO[:, 128:640], start=True, stop=False,
                              skip_group_check=True)

                def up(c, slot0, n0):
                    for half in range(2):
                        pe.wait_ge(ff_relu, c * 2 + (16 * f + half - 1))
                        features_out(n0 + half, (slot0 + half) % SLOTS, lambda i: C[:, half, 256 * i:256 * i + 256], XT_h, XT_l)

                def down(c, par, slot0, n0):
                    for half in range(2):
                        pe.wait_ge(ff_lo, c * 2 + (16 * f + 2))
                        pe.wait_ge(lo_ready, n0 + half + 1)
                        slot = (slot0 + half) % SLOTS
                        for t in range(T):
                            s = slice(128 * t, 128 * t + 128)
                            for k in range(4):
                                w = slice(512 * k, 512 * k + 512)
                                m = three(ACC[:, 2 * t + half, :], HT_h[:, 4 * par + k, s], HT_l[:, 4 * par + k, s],
                                          HI[:, slot, w], LO[:, slot, w], False, False)
                        m.then_inc(unit_used, 1)

                for half in range(2):
                    features_out(base + half, (base + half) % SLOTS, lambda i: C[:, half, 256 * i:256 * i + 256], XT_h, XT_l,
                                 e=None if half else e)
                with pe.Fori(0, 3) as j:
                    for d in range(2):
                        up(j * 2 + (d + 1), (base + 2) % SLOTS, j * 8 + (base + 2 + 4 * d))
                        down(j * 2 + d, d, (base + 4) % SLOTS, j * 8 + (base + 4 + 4 * d))
                up(7, (base + 26) % SLOTS, base + 26)
                down(6, 0, (base + 28) % SLOTS, base + 28)
                pe.wait_ge(ff_lo, 16 * f + 16)
                tokens_pair((base + 30, base + 31), HT_h, HT_l, (4, 4), lambda t, i: ACC[:, 2 * t + i, :], (False, False),
                            (True, True), ends_stage=True)

            pe.wait_ge(ident_loaded, 16)
            transpose_x(0, XN0, xn_ready, 0)

            for u in range(N_MIX):
                b = u // 2
                if u < 36:
                    if u % 2 == 0:
                        if b >= 2:
                            pe.wait_ge(*block_read(b - 2))
                    src_h, src_l = (HT_h, HT_l) if b in (13, 15) else (XT_h, XT_l)
                    if b == 13 and u % 2 == 0:
                        pe.wait_ge(g3_lo, 2 * GLA_H)
                    if u < 2:
                        pe.wait_ge(xt_lo, halves(0, 1, u))
                    tokens_out(u, src_h, src_l, 4 * (u % 2), lambda t: ACC[:, 2 * (b % 2) + t, :], u % 2 == 0, u % 2 == 1)
                elif u < 40:
                    c, kh = (u - 36) // 2, (u - 36) % 2
                    pe.wait_ge(*block_read(16 + c))
                    pe.wait_ge(o_lo, HEADS)
                    tokens_out(u, OT_h, OT_l, 4 * kh, lambda t: ACC[:, 2 * c + t, :], kh == 0, kh == 1)
                elif u < 42:
                    pe.wait_ge(xt_lo, halves(1, 0))
                    tokens_out(u, XT_h, XT_l, 0, lambda t: ACC[:, 2 * t + u - 40, :], True, False,
                               free=lambda t: (y_ready, 3 + t))
                elif u == 42:
                    pe.wait_ge(xt_lo, halves(1, 1))
                    tokens_pair((42, 43), XT_h, XT_l, (4, 4), lambda t, i: ACC[:, 2 * t + i, :], (False, False),
                                (True, True), ends_stage=True)
                if u == 0:
                    pe.wait_ge(lr_split, 2)
                    for t in range(T):
                        s = slice(128 * t, 128 * t + 128)
                        for k in range(KD):
                            m = three(C[:, 0, GLA_RANK * t:GLA_RANK * t + GLA_RANK], XT_h[:, k, s], XT_l[:, k, s],
                                      LR_h[:, k, :], LR_l[:, k, :], k == 0, k == KD - 1)
                    m.then_inc(lr_psum, 1)
                    pe.wait_ge(rows_loaded, 16 * 6)
                    pe.transpose(C[:, 2, 0:N_VEC], ROWS, IDENT[0:N_VEC, 0:N_VEC]).then_inc(cols_psum, 1)
                    pe.wait_ge(p_loaded, 16)
                    for k in range(2):
                        for t in range(T):
                            m = pe.transpose(C[:, 3, 256 * k + 128 * t:256 * k + 128 * t + 128],
                                             P_RAW[:, t, 128 * k:128 * k + 128], IDENT)
                    m.then_inc(p_psum, 1)
                    pe.wait_ge(lr_sb, 1)
                    for t in range(T):
                        m = pe.transpose(C[0:GLA_RANK, 1, 128 * t:128 * t + 128], GLR[:, t, :], IDENT)
                    m.then_inc(lrt_psum, 1)
                if u == 1:
                    pe.wait_ge(lrt_sb, 1)
                    pe.wait_ge(w2_loaded, 32)
                    for t in range(T):
                        m = pe.matmul(C[:, t, :], GLRT[:, 128 * t:128 * t + 128], W2E, start=True, stop=True)
                    m.then_inc(z_psum, 1)
                if u == 3:
                    pe.wait_ge(la_ready, 1)
                    pe.wait_ge(cst_loaded, 16)
                    pe.wait_ge(cols_ready, 1)
                    pe.wait_ge(p_lo, 1)
                    for h in range(GLA_H):
                        for t in range(T):
                            pe.matmul(C[:, h // 2, 256 * (h % 2) + 128 * t:256 * (h % 2) + 128 * t + 128],
                                      LA[:, t, 128 * h:128 * h + 128], TRI, start=True, stop=True, skip_group_check=True)
                    for t in range(T):
                        m = pe.matmul(C[:, 2 + t, :], REM, LA[:, t, :], start=True, stop=True)
                    m.then_inc(cum_psum, 1)
                for at, src, bank, done, before in ((4, GQ, 2, qt_psum, 1), (5, GK, 0, kt_psum, 2)):
                    if u == at:
                        pe.wait_ge(blk_sb, before)
                        pe.wait_ge(cum_exp, 1)
                        for h in range(GLA_H):
                            for t in range(T):
                                m = pe.transpose(C[:, bank + h // 2, 256 * (h % 2) + 128 * t:256 * (h % 2) + 128 * t + 128],
                                                 src[:, t, 128 * h:128 * h + 128], IDENT)
                        m.then_inc(done, 1)
                for h in range(GLA_H):
                    if u == 10 + 2 * h:
                        pe.wait_ge(kd_ready, 2)
                        pe.wait_ge(qd_ready, 1)
                        pe.wait_ge(blk_sb, 3 + h // 2)
                        if h:
                            pe.wait_ge(g1_ready, h)
                        for n in range(4):
                            t, j = n // 2, n % 2
                            c = slice(GLA_CHUNK * n, GLA_CHUNK * n + GLA_CHUNK)
                            pe.matmul(C[64 * j:64 * j + 64, 1, 256 + 64 * t:256 + 64 * t + 64], KDT[:, h, c], QD[:, h, c],
                                      start=True, stop=True, skip_group_check=True)
                        for n in (0, 2, 1):
                            t, q = n // 2, slice(64 * (n % 2), 64 * (n % 2) + 64)
                            m = pe.matmul(KV_of(n), GK[q, t, 128 * h:128 * h + 128],
                                          GV_head(q, h, t), start=True, stop=True, skip_group_check=True)
                        m.then_inc(g1_psum, 1)
                    if u == 11 + 2 * h:
                        pe.wait_ge(g1_ready, h + 1)
                        if h:
                            pe.wait_ge(g2_ready, h)
                        for t in range(T):
                            dst = slice(256 * t, 256 * t + 256)
                            m = pe.matmul(C[:, 2, dst], AT[:, t, :], GV_head(slice(0, 128), h, t), start=True, stop=False,
                                          skip_group_check=True)
                            for n in range(max(1, 2 * t), 2 * t + 2):
                                j = n % 2
                                m = pe.matmul(C[64 * j:64 * j + 64, 2, dst], QD[:, h, 64 * n:64 * n + 64], S[:, n - 1, :],
                                              start=False, stop=(j == 1), skip_group_check=True)
                        m.then_inc(g2_psum, 1)
                    if u == 12 + 2 * h:
                        pe.wait_ge(g2_ready, h + 1)
                        if h:
                            pe.wait_ge(g3_lo, 2 * h)
                        for j in range(2):
                            for t in range(T):
                                m = pe.transpose(C[:, 3, 256 * j + 128 * t:256 * j + 128 * t + 128],
                                                 OTOK[:, t, 128 * j:128 * j + 128], IDENT)
                        m.then_inc(g3_psum, 1)
                h = u - 22
                if 0 <= h < HEADS:
                    if h == 0:
                        pe.wait_ge(m_norm, 4)
                        pe.wait_ge(g3_lo, 2 * GLA_H)
                    else:
                        pe.wait_ge(m2_k, h)
                        pe.wait_ge(m2_q, h)
                    for i, src in enumerate((MQ, MK)):
                        for t in range(T):
                            m = pe.transpose(C[:, 0, 256 * i + 128 * t:256 * i + 128 * t + 128],
                                             src[:, h // 4, t, 128 * (h % 4):128 * (h % 4) + 128], IDENT)
                    m.then_inc(m2_psum, 1)
                if 1 <= h < HEADS + 1:
                    j = h - 1
                    pe.wait_ge(m2_q, j + 1)
                    pe.wait_ge(m2_k, j + 1)
                    att_score(j, [(QKT[:, j % 2, 0:256], QKT[:, j % 2, 256:512])])
                if 2 <= h < HEADS + 2:
                    att_transpose(h - 2)
                if 3 <= h < HEADS + 3:
                    j = h - 3
                    pe.wait_ge(blk_sb, 9 + j // 4)
                    att_values(j, MVt, j)
                if u in (38, 40):
                    y, k0 = (Y0, 0) if u == 38 else (Y1, 4)
                    pe.wait_ge(y_ready, 3 if u == 38 else 4)
                    for k in range(4):
                        for t in range(T):
                            m = pe.transpose(C[:, (k0 + k) // 2, 256 * (k % 2) + 128 * t:256 * (k % 2) + 128 * t + 128],
                                             y[:, t, 128 * k:128 * k + 128], IDENT)
                    m.then_inc(xt_psum, 2)

            transpose_x(2, XN, xn_ready, 1)
            feed_forward(0, U_FF0, 2)
            pe.wait_ge(lo_ready, U_PLE + 1)
            for t in range(T):
                s = slice(128 * t, 128 * t + 128)
                for c in range(2):
                    for k in range(2):
                        w = slice(1024 * k + 512 * c, 1024 * k + 512 * c + 512)
                        m = three(C[:, 2 * t + c, :], PT_h[:, k, s], PT_l[:, k, s], HI[:, U_PLE % SLOTS, w],
                                  LO[:, U_PLE % SLOTS, w], k == 0, k == 1)
                m.then_inc(unit_used if t else tail, 1)

            def gate_input(t):
                transpose_x(3, XN, xn_ready, 2, lambda t: (ple_sb, t + 1), tiles=(t,))
                pe.wait_ge(xt_lo, halves(3, t, 0))

            tokens_pair((U_PLE + 1, U_PLE + 2), XT_h, XT_l, (0, 0), lambda t, i: ACC[:, 2 * t + i, :], (True, True),
                        (False, False), inputs=gate_input)
            pe.wait_ge(xt_lo, halves(3, 1))
            tokens_pair((U_PLE + 3, U_PLE + 4), XT_h, XT_l, (4, 4), lambda t, i: ACC[:, 2 * t + i, :], (False, False),
                        (True, True), ends_stage=True)
            transpose_x(4, X, x_ready, 2)
            for q in range(12):
                n, pair, part = U_CONV + q, q // 3, q % 3
                if q >= 4:
                    old, opart = (q - 4) // 3, (q - 4) % 3
                    pe.wait_ge((cv_c, cv_z, cv_v)[opart], old + 1)
                features_out(n, n % SLOTS, lambda i: C[:, q % 4, 256 * i:256 * i + 256], XT_h, XT_l, e=None if q else 4)
            last_four(U_CONVO, OT_h, OT_l, lambda kh: (cv_lo, 2 * kh + 2))
            transpose_x(5, X, x_ready, 3, lambda t: (cv_v, 4))
            feed_forward(1, U_FF1, 5)

            def latent_input(t):
                transpose_x(6, X, x_ready, 4, tiles=(t,))
                pe.wait_ge(xt_lo, halves(6, t))

            tokens_pair((U_MLA, U_MLA + 1), XT_h, XT_l, (0, 4), lambda t, i: ACC[:, t, 0:KVL + ROPE], (True, False),
                        (False, True), inputs=latent_input, width=KVL + ROPE)
            for k in range(2):
                tokens_out(U_MLA + 2 + k, XT_h, XT_l, 4 * k, lambda t: ACC[:, 2 + t, 0:QL], k == 0, k == 1, width=QL)
                if k == 0:
                    pe.wait_ge(l_norm, 2)
                    for i in range(2):
                        for t in range(T):
                            m = pe.transpose(C[:, 2, 256 * i + 128 * t:256 * i + 128 * t + 128],
                                             CKV[:, t, 128 * i:128 * i + 128], IDENT)
                    m.then_inc(l_psum, 1)
            pe.wait_ge(l_norm, 3)
            for t in range(T):
                m = pe.transpose(C[:, 3, 128 * t:128 * t + 128], KPK[:, t, :], IDENT)
            m.then_inc(kp_psum, 1)

            def latent_q():
                pe.wait_ge(l_norm, 5)
                for k in range(3):
                    for t in range(T):
                        m = pe.transpose(C[:, k // 2, 256 * (k % 2) + 128 * t:256 * (k % 2) + 128 * t + 128],
                                         CQ[:, t, 128 * k:128 * k + 128], IDENT)
                m.then_inc(l_psum, 1)

            def keys(groups):
                for g in groups:
                    features_out(U_MLA + 4, (U_MLA + 4) % SLOTS, lambda i: ACC[:, g, 256 * i:256 * i + 256], HT_h, HT_l,
                                 k0=3, nk=2, width=1024, tiles=(2 * g, 2 * g + 1), inc=(g == 3))

            def values(t):
                n = U_MLA + 5
                pe.wait_ge(lo_ready, n + 1)
                s = slice(128 * t, 128 * t + 128)
                for c in range(2):
                    for k in range(2):
                        w = slice(1024 * k + 512 * c, 1024 * k + 512 * c + 512)
                        m = three(C[:, 2 * t + c, :], HT_h[:, 3 + k, s], HT_l[:, 3 + k, s], HI[:, n % SLOTS, w],
                                  LO[:, n % SLOTS, w], k == 0, k == 1)
                return m

            pe.wait_ge(l_lo, 2)
            keys((0, 1))
            pe.wait_ge(kp_sb, 1)
            values(1)
            latent_q()
            keys((2, 3))
            pe.wait_ge(l_lo, 5)
            values(0).then_inc(unit_used, 1)

            def project_q(q):
                n = U_MLA + 6 + q
                slot = n % SLOTS
                if q < 2:
                    pe.wait_ge(kn_sb, 1)
                else:
                    pe.wait_ge(uq_nope, q - 1)
                    pe.wait_ge(uq_rope, q - 1)
                pe.wait_ge(lo_ready, n + 1)
                nope, rot = ACC[:, 2 * (q % 2), :], ACC[:, 2 * (q % 2) + 1, :]
                for i in range(2):
                    for k in range(3):
                        w = slice(384 * k + 192 * i, 384 * k + 192 * i + 128)
                        three(nope[:, 256 * i:256 * i + 256], HI[:, slot, w], LO[:, slot, w], HT_h[:, k, :], HT_l[:, k, :],
                              k == 0, k == 2)
                for t in range(T):
                    s = slice(128 * t, 128 * t + 128)
                    for k in range(3):
                        hi_w, lo_w = (W[:, slot, 384 * k:384 * k + 384].rearrange("p (h c) -> p h c", c=192)[:, :, 128:192]
                                      for W in (HI, LO))
                        m = three(rot[:, 128 * t:128 * t + 128], HT_h[:, k, s], HT_l[:, k, s], hi_w, lo_w, k == 0, k == 2)
                m.then_inc(unit_used, 1)

            def rope_transpose(q):
                pe.wait_ge(uq_rope, q + 1)
                pe.wait_ge(v_sb, 1)
                if q:
                    pe.wait_ge(qp_sb, q)
                for t in range(T):
                    m = pe.transpose(C[:, 0, 128 * t:128 * t + 128], QPK[:, t, 128 * q:128 * q + 128], IDENT)
                m.then_inc(qp_psum, 1)

            for s in range(4 + HEADS + 2):
                if s < 4:
                    project_q(s)
                h = s - 2
                if 0 <= h < HEADS:
                    pe.wait_ge(qp_sb, h // 2 + 1)
                    pe.wait_ge(uq_nope, h // 2 + 1)
                    r = slice(ROPE * (h % 2), ROPE * (h % 2) + ROPE)
                    att_score(HEADS + h, [(QNT[:, h, :], KNT[:, h, :]), (QPT[r, h // 2, :], KPT[r, :])])
                if 2 <= h < HEADS + 2:
                    att_transpose(HEADS + h - 2)
                if 1 <= s < 5:
                    rope_transpose(s - 1)
                if 3 <= h < HEADS + 3:
                    att_values(HEADS + h - 3, VT, h - 3)
                if s in (9, 12):
                    pe.wait_ge(o_lo, HEADS + 4)
                    pe.wait_ge(uq_rope, 4)
                    tokens_out(U_WO + s // 12, OT_h, OT_l, 0, lambda t: ACC[:, 2 * t + s // 12, :], True, False)
            pe.wait_ge(o_lo, 2 * HEADS)
            tokens_pair((U_WO + 2, U_WO + 3), OT_h, OT_l, (4, 4), lambda t, i: ACC[:, 2 * t + i, :], (False, False),
                        (True, True), ends_stage=True)
            transpose_x(7, X, x_ready, 5)
            feed_forward(2, U_FF2, 7)


_INS = ["x", "p", "norm_mix", "w_in", "gla_gate_w2", "gla_gate_b", "gla_out_norm", "moba_q_norm", "moba_k_norm",
        "w_branch_a", "w_branch_b", "w_out", "norm_mlp", "w_up", "w_down", "norm_ple", "w_ple_gate", "w_ple",
        "sc_w_in_2", "sc_conv_w_2", "sc_w_out_2", "mla_w_dq_2", "mla_g_q_2", "mla_w_uq_2", "mla_w_dkv_2",
        "mla_g_kv_2", "mla_w_uk_2", "mla_w_uv_2", "mla_w_o_2", "ff_w1_2", "ff_w2_2", "ln_mix_g_2", "ln_mix_b_2",
        "ln_ff_g_2", "ln_ff_b_2"]


def _constants(np):
    c = np.zeros((128, N_CONST), np.float32)
    i, j = np.arange(128)[:, None], np.arange(128)[None, :]
    same = i // GLA_CHUNK == j // GLA_CHUNK
    c[:, C_ID:C_ID + 128] = i == j
    c[:, C_TRI:C_TRI + 128] = (same & (i <= j)) / 16.0
    c[:, C_REM:C_REM + 128] = (same & (i > j)) / 16.0
    for o, tq, tk in ((0, 0, 0), (128, 1, 0), (256, 1, 1)):
        q, k = 128 * tq + i, 128 * tk + j
        c[:, C_DIST + o:C_DIST + o + 128] = np.where(q >= k, k - q, MASKED)
        c[:, C_CHM + o:C_CHM + o + 128] = np.where(k // 64 <= q // 64, 0.0, MASKED)
    freq = np.float32(10000.0) ** (-np.arange(0, ROPE, 2, dtype=np.float32) / np.float32(ROPE))
    ang = (np.arange(SEQ, dtype=np.float32)[:, None] * freq[None, :].astype(np.float32)).astype(np.float32)
    for o, f in ((C_COS, np.cos), (C_SIN, np.sin)):
        c[:, o:o + 64] = f(ang).astype(np.float32).reshape(T, 128, 32).transpose(1, 0, 2).reshape(128, 64)
    mask = (np.arange(128)[:, None] % 64 <= np.arange(64)[None, :]).astype(np.float32)
    c[:, C_GM:C_GM + 128] = np.concatenate([mask, mask], axis=1)
    return c


def kernel(**inputs):
    import numpy as _np
    import concourse.bacc as _bacc
    from concourse import mybir as _mybir
    from concourse.bass_utils import run_bass_kernel_spmd as _run

    nc = _bacc.Bacc("TRN2", target_bir_lowering=False, num_devices=1)
    arrays, args = {}, {}
    for name in _INS + ["consts"]:
        v = _constants(_np) if name == "consts" else _np.ascontiguousarray(inputs[name])
        arrays[f"in_{name}"] = v
        args[name] = nc.dram_tensor(f"in_{name}", v.shape, _mybir.dt.from_np(v.dtype), kind="ExternalInput").ap()
    out = nc.dram_tensor("out", (1, SEQ, D), _mybir.dt.float32, kind="ExternalOutput").ap()
    program(nc, args, out)
    r = _run(nc, [arrays], core_ids=[0])
    return r.results[0]["out"]
```
